# Optimizing a Trainium2 kernel written in Bass

```python
import math
import jax
import jax.numpy as jnp
from jax import lax
import numpy as np

D_MODEL = 1024
BATCH = 1
SEQ = 256
DEPTH = 2

GRID_W = 64
Q_BLOCK = 128
HEAD_DIM = 64
N_BRANCH = 4
BRANCH_W = 256

MLA_HEADS = 4
MLA_NOPE = 64
MLA_ROPE = 32
MLA_V = 64
MLA_Q_LORA = 192
MLA_KV_LORA = 128

DIL_GROUPS = ((128, 1), (512, 4), (2048, 16))
DIL_N_GROUPS = 3
DIL_HEADS = 4

GQA_Q_HEADS = 4
GQA_KV_HEADS = 2

DIFF_HEADS = 4
DIFF_D = 32
DIFF_V = 64

D_FF = 3584
N_EXPERTS = 8
TOP_K = 2
D_EXPERT = 3584

ROPE_THETA = 10000.0
LN_EPS = 1e-5
RMS_EPS = 1e-6
DIFF_NORM_EPS = 1e-5
DEEPNORM_ALPHA = (2 * DEPTH) ** 0.25
DEEPNORM_BETA = (8 * DEPTH) ** -0.25

IN_SPLITS = (
    MLA_Q_LORA,
    MLA_KV_LORA,
    MLA_ROPE,
    3 * DIL_N_GROUPS * DIL_HEADS * HEAD_DIM,
    GQA_Q_HEADS * HEAD_DIM,
    2 * GQA_KV_HEADS * HEAD_DIM,
    2 * DIFF_HEADS * 2 * DIFF_D,
    DIFF_HEADS * DIFF_V,
    N_BRANCH * D_MODEL,
)
N_IN = sum(IN_SPLITS)

kernel_name = 'hybrid_gated_mixer_encoder'

def _layernorm(x, g, b):
    xf = x.astype(jnp.float32)
    mu = jnp.mean(xf, axis=-1, keepdims=True)
    var = jnp.mean(jnp.square(xf - mu), axis=-1, keepdims=True)
    return ((xf - mu) * lax.rsqrt(var + LN_EPS) * g + b).astype(x.dtype)

def _rmsnorm(x, g, eps=RMS_EPS):
    xf = x.astype(jnp.float32)
    return (xf * lax.rsqrt(jnp.mean(xf * xf, axis=-1, keepdims=True) + eps) * g).astype(x.dtype)

def _rope_angles(pos, dim):
    inv = ROPE_THETA ** (-(jnp.arange(0, dim, 2, dtype=jnp.float32) / dim))
    return pos[:, None] * inv[None, :]

def _apply_rope(x, ang):
    cos = jnp.cos(ang)[None, :, None, :]
    sin = jnp.sin(ang)[None, :, None, :]
    x1, x2 = jnp.split(x.astype(jnp.float32), 2, axis=-1)
    return jnp.concatenate([x1 * cos - x2 * sin, x2 * cos + x1 * sin], axis=-1).astype(x.dtype)

def _axial_rope(x, ang_row, ang_col):
    half = x.shape[-1] // 2
    return jnp.concatenate([_apply_rope(x[..., :half], ang_row), _apply_rope(x[..., half:], ang_col)], axis=-1)

def _alibi_slopes(n):
    return 2.0 ** (-8.0 * jnp.arange(1, n + 1, dtype=jnp.float32) / n)

def _sweep_query_blocks(block_fn, seq):
    starts = jnp.arange(seq // Q_BLOCK, dtype=jnp.int32) * Q_BLOCK
    out = lax.map(block_fn, starts)
    out = jnp.moveaxis(out, 0, 1)
    return out.reshape((out.shape[0], seq) + out.shape[3:])

def _mla(c_q, c_kv, k_r, q_norm, kv_norm, w_uq, w_ukv, ang):
    B, S, _ = c_q.shape
    q = (_rmsnorm(c_q, q_norm) @ w_uq).reshape(B, S, MLA_HEADS, MLA_NOPE + MLA_ROPE)
    q_nope = q[..., :MLA_NOPE]
    q_rope = _apply_rope(q[..., MLA_NOPE:], ang)
    kv = (_rmsnorm(c_kv, kv_norm) @ w_ukv).reshape(B, S, MLA_HEADS, MLA_NOPE + MLA_V)
    k_nope = kv[..., :MLA_NOPE]
    v = kv[..., MLA_NOPE:]
    k_rope = _apply_rope(k_r[:, :, None, :], ang)[:, :, 0]
    scale = (MLA_NOPE + MLA_ROPE) ** -0.5

    def block(start):
        qn = lax.dynamic_slice_in_dim(q_nope, start, Q_BLOCK, axis=1)
        qr = lax.dynamic_slice_in_dim(q_rope, start, Q_BLOCK, axis=1)
        s = jnp.einsum('bqhd,bkhd->bhqk', qn, k_nope) + jnp.einsum('bqhd,bkd->bhqk', qr, k_rope)
        p = jax.nn.softmax(s.astype(jnp.float32) * scale, axis=-1)
        return jnp.einsum('bhqk,bkhd->bqhd', p.astype(v.dtype), v)

    return _sweep_query_blocks(block, S).reshape(B, S, MLA_HEADS * MLA_V)

def _dilated_attention(q, k, v):
    B, S = q.shape[:2]
    scale = HEAD_DIM ** -0.5
    slopes = _alibi_slopes(DIL_N_GROUPS * DIL_HEADS).reshape(DIL_N_GROUPS, DIL_HEADS)
    k_groups = [k[:, :, g] for g in range(DIL_N_GROUPS)]
    v_groups = [v[:, :, g] for g in range(DIL_N_GROUPS)]

    def block(start):
        t = start + jnp.arange(Q_BLOCK, dtype=jnp.int32)
        qb = lax.dynamic_slice_in_dim(q, start, Q_BLOCK, axis=1)
        outs, lses = [], []
        for g, (window, dil) in enumerate(DIL_GROUPS):
            off = np.arange(-(window // 2), window // 2 + 1, dil, dtype=np.int32)
            idx = t[:, None] + off[None, :]
            valid = (idx >= 0) & (idx < S)
            idx_c = jnp.clip(idx, 0, S - 1)
            kg = jnp.take(k_groups[g], idx_c, axis=1)
            vg = jnp.take(v_groups[g], idx_c, axis=1)
            s = jnp.einsum('bqhd,bqjhd->bhqj', qb[:, :, g], kg).astype(jnp.float32) * scale
            s = s - slopes[g][None, :, None, None] * jnp.abs(off).astype(jnp.float32)[None, None, None, :]
            s = jnp.where(valid[None, None], s, -jnp.inf)
            lse = jax.nn.logsumexp(s, axis=-1)
            p = jnp.exp(s - lse[..., None])
            outs.append(jnp.einsum('bhqj,bqjhd->bqhd', p.astype(vg.dtype), vg).astype(jnp.float32))
            lses.append(lse)
        wts = jax.nn.softmax(jnp.stack(lses, axis=0), axis=0)
        wts = jnp.transpose(wts, (0, 1, 3, 2))[..., None]
        return jnp.sum(wts * jnp.stack(outs, axis=0), axis=0).astype(q.dtype)

    return _sweep_query_blocks(block, S).reshape(B, S, DIL_HEADS * HEAD_DIM)

def _axial_gqa(q, k, v, q_norm, k_norm, ang_row, ang_col):
    B, S = q.shape[:2]
    group = GQA_Q_HEADS // GQA_KV_HEADS
    q = _axial_rope(_rmsnorm(q, q_norm), ang_row, ang_col).reshape(B, S, GQA_KV_HEADS, group, HEAD_DIM)
    k = _axial_rope(_rmsnorm(k, k_norm), ang_row, ang_col)
    scale = HEAD_DIM ** -0.5

    def block(start):
        qb = lax.dynamic_slice_in_dim(q, start, Q_BLOCK, axis=1)
        s = jnp.einsum('bqkgd,bskd->bkgqs', qb, k).astype(jnp.float32) * scale
        p = jax.nn.softmax(s, axis=-1)
        return jnp.einsum('bkgqs,bskd->bqkgd', p.astype(v.dtype), v)

    return _sweep_query_blocks(block, S).reshape(B, S, GQA_Q_HEADS * HEAD_DIM)

def _diff_attention(q, k, v, lam_params, subln, lam_init):
    B, S = q.shape[:2]
    lp = lam_params.astype(jnp.float32)
    lam = jnp.exp(jnp.sum(lp[0] * lp[1])) - jnp.exp(jnp.sum(lp[2] * lp[3])) + lam_init
    slopes = _alibi_slopes(DIFF_HEADS)
    scale = DIFF_D ** -0.5
    keys = jnp.arange(S, dtype=jnp.int32)

    def block(start):
        t = start + jnp.arange(Q_BLOCK, dtype=jnp.int32)
        qb = lax.dynamic_slice_in_dim(q, start, Q_BLOCK, axis=1)
        s = jnp.einsum('bqhmd,bkhmd->bhmqk', qb, k).astype(jnp.float32) * scale
        dist = jnp.abs(t[:, None] - keys[None, :]).astype(jnp.float32)
        s = s - slopes[None, :, None, None, None] * dist[None, None, None]
        p = jax.nn.softmax(s, axis=-1)
        a = p[:, :, 0] - lam * p[:, :, 1]
        return jnp.einsum('bhqk,bkhd->bqhd', a.astype(v.dtype), v)

    o = _sweep_query_blocks(block, S)
    o = _rmsnorm(o, subln, DIFF_NORM_EPS) * (1.0 - lam_init)
    return o.reshape(B, S, DIFF_HEADS * DIFF_V)

def _token_mixers(h, w_in, b_gate, mla_q_norm, mla_kv_norm, mla_w_uq, mla_w_ukv, gqa_q_norm, gqa_k_norm,
                  diff_lambda, diff_subln, w_branch, w_out, ang_1d, ang_row, ang_col, lam_init):
    B, S, _ = h.shape
    proj = h @ w_in
    c_q, c_kv, k_r, dil_qkv, g_q, g_kv, d_qk, d_v, gate_lin = jnp.split(
        proj, np.cumsum(IN_SPLITS)[:-1].tolist(), axis=-1)
    y_a = _mla(c_q, c_kv, k_r, mla_q_norm, mla_kv_norm, mla_w_uq, mla_w_ukv, ang_1d)
    dil = dil_qkv.reshape(B, S, 3, DIL_N_GROUPS, DIL_HEADS, HEAD_DIM)
    y_b = _dilated_attention(dil[:, :, 0], dil[:, :, 1], dil[:, :, 2])
    g_kv = g_kv.reshape(B, S, 2, GQA_KV_HEADS, HEAD_DIM)
    y_c = _axial_gqa(g_q.reshape(B, S, GQA_Q_HEADS, HEAD_DIM), g_kv[:, :, 0], g_kv[:, :, 1],
                     gqa_q_norm, gqa_k_norm, ang_row, ang_col)
    d_qk = d_qk.reshape(B, S, 2, DIFF_HEADS, 2, DIFF_D)
    y_d = _diff_attention(d_qk[:, :, 0], d_qk[:, :, 1], d_v.reshape(B, S, DIFF_HEADS, DIFF_V),
                          diff_lambda, diff_subln, lam_init)
    branches = jnp.stack([y_a, y_b, y_c, y_d], axis=2)
    branches = jnp.einsum('bsnc,ncd->bsnd', branches, w_branch)
    gates = jax.nn.sigmoid(gate_lin.reshape(B, S, N_BRANCH, D_MODEL) + b_gate)
    return jnp.sum(gates * branches, axis=2) @ w_out

def _swiglu(x, w13, w2):
    a, b = jnp.split(x @ w13, 2, axis=-1)
    return (jax.nn.silu(a) * b) @ w2

def _moe_swiglu(h, w_router, w13, w2):
    B, S, D = h.shape
    xt = h.reshape(B * S, D)
    logits = (xt @ w_router).astype(jnp.float32)
    top_val, top_idx = lax.top_k(logits, TOP_K)
    top_w = jax.nn.softmax(top_val, axis=-1)
    gate = jnp.sum(jax.nn.one_hot(top_idx, N_EXPERTS, dtype=jnp.float32) * top_w[..., None], axis=1)
    out = jnp.zeros((B * S, D), jnp.float32)
    for e in range(N_EXPERTS):
        out = out + gate[:, e:e + 1] * _swiglu(xt, w13[e], w2[e]).astype(jnp.float32)
    return out.astype(h.dtype).reshape(B, S, D)

def setup_inputs(seed: int = 0) -> dict:
    key = jax.random.key(seed)
    ks = iter(jax.random.split(key, 32))
    L = DEPTH
    n_even = (DEPTH + 1) // 2
    n_odd = DEPTH // 2

    def nrm(shape, scale):
        return jax.random.normal(next(ks), shape, jnp.float32) * scale

    def gain(shape):
        return 1.0 + nrm(shape, 0.02)

    return {
        'x': nrm((BATCH, SEQ, D_MODEL), 1.0),
        'ln_emb_g': gain((D_MODEL,)),
        'ln_emb_b': nrm((D_MODEL,), 0.02),
        'w_in': nrm((L, D_MODEL, N_IN), D_MODEL ** -0.5),
        'b_gate': nrm((L, N_BRANCH, D_MODEL), 0.02),
        'mla_q_norm': gain((L, MLA_Q_LORA)),
        'mla_kv_norm': gain((L, MLA_KV_LORA)),
        'mla_w_uq': nrm((L, MLA_Q_LORA, MLA_HEADS * (MLA_NOPE + MLA_ROPE)), MLA_Q_LORA ** -0.5),
        'mla_w_ukv': nrm((L, MLA_KV_LORA, MLA_HEADS * (MLA_NOPE + MLA_V)), MLA_KV_LORA ** -0.5),
        'gqa_q_norm': gain((L, HEAD_DIM)),
        'gqa_k_norm': gain((L, HEAD_DIM)),
        'diff_lambda': nrm((L, 4, DIFF_D), 0.1),
        'diff_subln': gain((L, DIFF_V)),
        'w_branch': nrm((L, N_BRANCH, BRANCH_W, D_MODEL), BRANCH_W ** -0.5),
        'w_out': nrm((L, D_MODEL, D_MODEL), D_MODEL ** -0.5 * DEEPNORM_BETA),
        'ln1_g': gain((L, D_MODEL)),
        'ln1_b': nrm((L, D_MODEL), 0.02),
        'ffn_w13': nrm((n_even, D_MODEL, 2 * D_FF), D_MODEL ** -0.5),
        'ffn_w2': nrm((n_even, D_FF, D_MODEL), D_FF ** -0.5 * DEEPNORM_BETA),
        'moe_router': nrm((n_odd, D_MODEL, N_EXPERTS), D_MODEL ** -0.5),
        'moe_w13': nrm((n_odd, N_EXPERTS, D_MODEL, 2 * D_EXPERT), D_MODEL ** -0.5),
        'moe_w2': nrm((n_odd, N_EXPERTS, D_EXPERT, D_MODEL), D_EXPERT ** -0.5 * DEEPNORM_BETA),
        'ln2_g': gain((L, D_MODEL)),
        'ln2_b': nrm((L, D_MODEL), 0.02),
    }

def reference(x, ln_emb_g, ln_emb_b, w_in, b_gate, mla_q_norm, mla_kv_norm, mla_w_uq, mla_w_ukv,
              gqa_q_norm, gqa_k_norm, diff_lambda, diff_subln, w_branch, w_out, ln1_g, ln1_b,
              ffn_w13, ffn_w2, moe_router, moe_w13, moe_w2, ln2_g, ln2_b):
    S = x.shape[1]
    rows = S // GRID_W
    row_idx = jnp.repeat(jnp.arange(rows, dtype=jnp.float32), GRID_W)
    col_idx = jnp.tile(jnp.arange(GRID_W, dtype=jnp.float32), rows)
    ang_1d = _rope_angles(jnp.arange(S, dtype=jnp.float32), MLA_ROPE)
    ang_row = _rope_angles(row_idx, HEAD_DIM // 2)
    ang_col = _rope_angles(col_idx, HEAD_DIM // 2)
    alpha = DEEPNORM_ALPHA

    h = _layernorm(x, ln_emb_g, ln_emb_b)
    for l in range(DEPTH):
        lam_init = 0.8 - 0.6 * math.exp(-0.3 * l)
        m = _token_mixers(h, w_in[l], b_gate[l], mla_q_norm[l], mla_kv_norm[l], mla_w_uq[l], mla_w_ukv[l],
                          gqa_q_norm[l], gqa_k_norm[l], diff_lambda[l], diff_subln[l], w_branch[l], w_out[l],
                          ang_1d, ang_row, ang_col, lam_init)
        h = _layernorm(alpha * h + m, ln1_g[l], ln1_b[l])
        if l % 2 == 0:
            f = _swiglu(h, ffn_w13[l // 2], ffn_w2[l // 2])
        else:
            f = _moe_swiglu(h, moe_router[l // 2], moe_w13[l // 2], moe_w2[l // 2])
        h = _layernorm(alpha * h + f, ln2_g[l], ln2_b[l])
    return h


_drawn_inputs = setup_inputs


def setup_inputs(seed=0):
    import zlib

    import numpy as np

    out = dict(_drawn_inputs(seed))
    spreads = {}
    factors = {'b_gate': 8.0,
     'mla_q_norm': 8.0,
     'mla_kv_norm': 8.0,
     'gqa_q_norm': 8.0,
     'gqa_k_norm': 8.0,
     'diff_subln': 8.0}
    for name, (base, spread) in spreads.items():
        noise = np.random.default_rng([zlib.crc32(name.encode()), seed]).standard_normal(out[name].shape)
        drawn = base * np.exp(spread * noise) if base else spread * noise
        out[name] = jnp.asarray(drawn.astype(out[name].dtype))
    for name, factor in factors.items():
        out[name] = (out[name] * factor).astype(out[name].dtype)
    return out
```

```python
import math
from contextlib import ExitStack

import numpy as np

import concourse.bass as bass
from concourse import mybir

F32 = mybir.dt.float32
F32R = mybir.dt.float32r
I32 = mybir.dt.int32
ALU = mybir.AluOpType
ACT = mybir.ActivationFunctionType
AX = mybir.AxisListType

P = 128
D = 1024
S = 256
NT = S // P
DK = D // P
DEPTH = 2
GRID_W = 64
FF = 3584
NE = 8
TOP_K = 2
MAX_ITEMS = 12
NBR = 4
BW = 256
QL, KVL, MR = 192, 128, 32
HD = 64
DIL_GROUPS = ((128, 1), (512, 4), (2048, 16))
ALPHA = (2 * DEPTH) ** 0.25
LN_EPS, RMS_EPS, DIFF_EPS = 1e-5, 1e-6, 1e-5
FAR = 1e30
NOWHERE = 1e6

C_TOK = (0, 352)
C_FEAT = 352
C_DV = 1888
C_DQK = 3168
C_DIFFV = 3680
C_GATE = 3936

CH = 2048
RAW = 6
SPL = 3
AHEAD = 2
FB = 512
NB = FF // FB

SLOTS = [(0, 352, False)] + [(C_FEAT + 512 * i, 512, True) for i in range(3)] + \
        [(C_DV, 512, False), (C_DV + 512, 256, False), (C_DV + 768, 512, False),
         (C_DQK, 512, True), (C_DIFFV, 256, False)]


def expert_order():
    order = []
    for j in range(NB):
        order += [("a", j, 0), ("a", j, 1), ("b", j, 0), ("b", j, 1)]
        if j:
            order += [("w", j - 1, 0), ("w", j - 1, 1)]
    return order + [("w", NB - 1, 0), ("w", NB - 1, 1)]


ORDER = expert_order()
NX = len(ORDER)
N_PROJ = 2 * len(SLOTS)
N_GATE = 5 * NBR
N_OUT = 4
N_MIX = N_PROJ + N_GATE + N_OUT
MIX_WIDTH = [4 * SLOTS[i // 2][1] for i in range(N_PROJ)] + [CH] * (N_GATE + N_OUT)
assert NX % RAW == 0 and N_MIX % RAW == 0 and NX % SPL == 0 and N_MIX % SPL == 0
DENSE_PASSES = NT


def mix_base(l):
    return l * (N_MIX + DENSE_PASSES * NX)


DENSE_BASE = N_MIX
MOE_BASE = mix_base(1) + N_MIX


def units(part):
    if part == 0:
        return [("dil", h, t, 0) for t in range(NT) for h in range(4)] + \
               [("diff", h, t, m) for h in range(4) for t in range(NT) for m in range(2)]
    return [("mla", h, t, 0) for h in range(4) for t in range(NT)] + \
           [("gqa", h, t, 0) for h in range(4) for t in range(NT)]


PARTS = [units(0), units(1)]
N_UNIT = len(PARTS[0]) + len(PARTS[1])
EVAC = {"dil": (1, 1), "diff": (1, 0), "mla": (0, 1), "gqa": (0, 1)}
EVACS = [(0, 0)]
for _l in range(DEPTH):
    for _u in PARTS[0] + PARTS[1]:
        EVACS.append((EVACS[-1][0] + EVAC[_u[0]][0], EVACS[-1][1] + EVAC[_u[0]][1]))


def scale_of(kind):
    return {"mla": 96 ** -0.5, "gqa": HD ** -0.5}.get(kind, 1.0)


K_ID = 0
K_DIST = 128
K_IOTA = K_DIST + 4 * 384
K_TRI = K_IOTA + 128
K_ONES = K_TRI + 128
K_MC = K_ONES + 128
K_MS = K_MC + 2 * 32
K_GC = K_MS + 2 * 32
K_GS = K_GC + 2 * 64
K_TIE = K_GS + 2 * 64
K_ITEM = K_TIE + 64
K_ALL = K_ITEM + MAX_ITEMS * 8


def constants():
    k = np.zeros((P, K_ALL), np.float32)
    p = np.arange(P)
    k[:, K_ID:K_ID + P] = np.eye(P)
    d = np.abs(np.arange(-128, 256)[None, :] - p[:, None])
    for g, (window, dil) in enumerate(DIL_GROUPS):
        k[:, K_DIST + 384 * g:K_DIST + 384 * (g + 1)] = np.where((d <= window // 2) & (d % dil == 0), d, FAR)
    k[:, K_DIST + 384 * 3:K_DIST + 384 * 4] = d
    k[:, K_IOTA:K_IOTA + P] = p[None, :]
    k[:, K_TRI:K_TRI + P] = p[:, None] < p[None, :]
    k[:, K_ONES:K_ONES + P] = 1.0
    inv = (10000.0 ** -(np.arange(0, 32, 2, dtype=np.float32) / np.float32(32))).astype(np.float32)
    for t in range(NT):
        pos = (t * P + p).astype(np.float32)
        for c0, s0, angs in ((K_MC, K_MS, [pos]), (K_GC, K_GS, [pos // GRID_W, pos % GRID_W])):
            n = 32 * len(angs)
            for i, a in enumerate(angs):
                ang = a[:, None] * inv[None, :]
                c, s = c0 + t * n + 32 * i, s0 + t * n + 32 * i
                k[:, c:c + 16] = k[:, c + 16:c + 32] = np.cos(ang)
                k[:, s:s + 16] = -np.sin(ang)
                k[:, s + 16:s + 32] = np.sin(ang)
    e = np.arange(64)
    k[:, K_TIE:K_TIE + 64] = (e % 8 < e // 8)[None, :]
    k[:, K_ITEM:K_ALL] = (np.arange(MAX_ITEMS * 8) // 8)[None, :]
    return k


def encoder(nc, a):
    with ExitStack() as ctx:
        def sb(name, shape, dt=F32):
            return ctx.enter_context(nc.sbuf_tensor(name, shape, dt))

        def sem(name):
            return ctx.enter_context(nc.semaphore(name))

        raw = sb("raw", [P, RAW, CH])
        w_hi = sb("w_hi", [P, SPL, CH], F32R)
        w_lo = sb("w_lo", [P, SPL, CH], F32R)
        h = sb("h", [P, NT, D])
        actT_hi = sb("actT_hi", [P, DK, S], F32R)
        actT_lo = sb("actT_lo", [P, DK, S], F32R)
        brT_hi = sb("brT_hi", [P, DK, S], F32R)
        brT_lo = sb("brT_lo", [P, DK, S], F32R)
        const = sb("const", [P, K_ALL])
        small = sb("small", [P, 2048])
        lamp = sb("lamp", [P, 4, 32])
        stat = sb("stat", [P, 96])
        n_items = sb("n_items", [1, 1], I32)
        item_expert = sb("item_expert", [1, MAX_ITEMS], I32)
        work = sb("work", [P, 12992])
        ps = ctx.enter_context(nc.psum_tensor("banks", [P, 8, 512], F32))

        def at(off, n):
            return work[:, off:off + n]

        ident = const[:, K_ID:K_ID + P]
        iota = const[:, K_IOTA:K_IOTA + P]
        tri = const[:, K_TRI:K_TRI + P]
        ones = const[:, K_ONES:K_ONES + P]

        featT = at(0, 4096).rearrange("p (b t) -> p b t", b=16)
        dilv = at(4096, 1536).rearrange("p (t n) -> p t n", t=NT)
        diffv = at(5632, 512).rearrange("p (t n) -> p t n", t=NT)
        gqa = at(6144, 1024).rearrange("p (t n) -> p t n", t=NT)
        cqkv = at(7168, 704).rearrange("p (t n) -> p t n", t=NT)
        y = at(7872, 2048).rearrange("p (t n) -> p t n", t=NT)
        prob = at(9920, 1536).rearrange("p (b n) -> p b n", b=2)
        probT = at(9920 + 1536, 1536).rearrange("p (b n) -> p b n", b=2)
        mqT = at(0, 1024).rearrange("p (h t) -> p h t", h=4)
        mkT = at(1024, 1024).rearrange("p (h t) -> p h t", h=4)
        gT = at(2048, 1536).rearrange("p (h t) -> p h t", h=6)
        rope_a = at(0, 768).rearrange("p (t n) -> p t n", t=NT)
        rope_m = at(768, 512).rearrange("p (t n) -> p t n", t=NT)
        mq = at(4096, 768).rearrange("p (t h d) -> p t h d", t=NT, h=4)
        mk = at(4864, 768).rearrange("p (t h d) -> p t h d", t=NT, h=4)
        mv = at(5632, 512).rearrange("p (t h d) -> p t h d", t=NT, h=4)
        cn = at(9920, 640).rearrange("p (t n) -> p t n", t=NT)
        gn = at(9920 + 640, 768).rearrange("p (t n) -> p t n", t=NT)
        gr = at(9920 + 1408, 768).rearrange("p (t n) -> p t n", t=NT)
        cT = at(9920 + 2176, 768).rearrange("p (c t) -> p c t", c=3)
        sq_c = at(9920 + 2176, 640).rearrange("p (t n) -> p t n", t=NT)
        gate_bias = at(0, 4096).rearrange("p (n d) -> p n d", n=NBR)
        gate_sb = at(9920, 2048).rearrange("p (b n) -> p b n", b=4)
        gate_pr = at(9920 + 2048, 1024).rearrange("p (b n) -> p b n", b=2)
        xT_hi, xT_lo = brT_hi[:, :, 0:P], brT_lo[:, :, 0:P]
        hidT_hi, hidT_lo = brT_hi[:, 0:4, P:S], brT_lo[:, 0:4, P:S]
        acc = y
        silu = at(9920, 512)
        hid = at(10432, 512)
        pick = at(0, 256).rearrange("p (t s) -> p t s", t=NT)
        pick_g = at(256, 256).rearrange("p (t s) -> p t s", t=NT)
        pick_gT = at(512, 256)
        y_exp = at(1024, 1024)
        logit = at(2048, 16).rearrange("p (t e) -> p t e", t=NT)
        cmp_a = at(2064, 128).rearrange("p (t n) -> p t n", t=NT)
        cmp_b = at(2192, 128).rearrange("p (t n) -> p t n", t=NT)
        rank = at(2320, 16).rearrange("p (t e) -> p t e", t=NT)
        sel = at(2336, 16).rearrange("p (t e) -> p t e", t=NT)
        expo = at(2352, 16).rearrange("p (t e) -> p t e", t=NT)
        gate = at(2368, 16).rearrange("p (t e) -> p t e", t=NT)
        slot = at(2384, 16).rearrange("p (t e) -> p t e", t=NT)
        item_slot = at(2496, 2 * MAX_ITEMS).rearrange("p (t i) -> p t i", t=NT)
        item_gate = at(2520, 2 * MAX_ITEMS).rearrange("p (t i) -> p t i", t=NT)
        item_hot = at(2544, MAX_ITEMS * NE).rearrange("p (i e) -> p i e", e=NE)
        item_tmp = at(2640, MAX_ITEMS * NE).rearrange("p (i e) -> p i e", e=NE)
        item_e = at(2736, MAX_ITEMS)
        item_round = at(2748, MAX_ITEMS)
        ends = at(2760, NE)
        tiles_of = at(2768, 2 * NE).rearrange("p (a e) -> p a e", a=2)
        r_raw = at(2432, 64).rearrange("p (k e) -> p k e", k=DK)
        r_hi = sb("r_hi", [P, DK, NE], F32R)
        r_lo = sb("r_lo", [P, DK, NE], F32R)
        w_uq0, w_uq1 = small[:, 0:384], small[0:64, 384:768]
        w_ukv = small[:, 768:1280]
        g_q, g_kv = small[:, 1280:1472], small[:, 1472:1600]
        g_gqa, g_sub = small[:, 1600:1984], small[:, 1984:2048]

        chunk_loaded = [sem(f"chunk_loaded{i}") for i in range(RAW)]
        hi_done, lo_done = sem("hi_done"), sem("lo_done")
        chunk_used = sem("chunk_used")
        phase_done = sem("phase_done")
        start_loaded, gains_loaded = sem("start_loaded"), sem("gains_loaded")
        params_loaded, bias_loaded = sem("params_loaded"), sem("bias_loaded")
        router_loaded, stored = sem("router_loaded"), sem("stored")
        dve_step, act_step = sem("dve_step"), sem("act_step")
        turned4, turn_hi = sem("turned4"), sem("turn_hi")
        proj_used = [sem("proj_used_act"), sem("proj_used_dve")]
        var_ready, std_ready = sem("var_ready"), sem("std_ready")
        lam_sum, lam_exp = sem("lam_sum"), sem("lam_exp")
        scores, negmax, exps = sem("scores"), sem("negmax"), sem("exps")
        prob_turned, pv_done, out_taken = sem("prob_turned"), sem("pv_done"), sem("out_taken")
        turned_taken = [sem("turned_taken_act"), sem("turned_taken_dve")]
        prep_dve, prep_act, prep_pe = sem("prep_dve"), sem("prep_act"), sem("prep_pe")
        gate_biased, gate_open, branch_used = sem("gate_biased"), sem("gate_open"), sem("branch_used")
        silu_done, hid_made, hid_turned = sem("silu_done"), sem("hid_made"), sem("hid_turned")
        hidT_hi_done, hidT_lo_done = sem("hidT_hi_done"), sem("hidT_lo_done")
        x_hi_done, x_lo_done = sem("x_hi_done"), sem("x_lo_done")
        y_free, acc_added = sem("y_free"), sem("acc_added")
        picked, gathered, pick_turned, pickT_ready = sem("picked"), sem("gathered"), sem("pick_turned"), sem("pickT_ready")
        scattered = sem("scattered")
        router_hi, router_lo, logits_done, logits_copied = sem("router_hi"), sem("router_lo"), sem("logits_done"), sem("logits_copied")
        expo_in, expo_out, sel_done, counted, items_known = sem("expo_in"), sem("expo_out"), sem("sel_done"), sem("counted"), sem("items_known")

        block = ctx.enter_context(nc.Block())

        def bank(i):
            return ps[:, i, :]

        def token_dst(c0, n, t):
            if c0 == 0:
                return cqkv[:, t, :]
            if c0 < C_DV + 768:
                return dilv[:, t, c0 - C_DV:c0 - C_DV + n]
            return gqa[:, t, :] if c0 == C_DV + 768 else diffv[:, t, :]

        class Steps:

            def __init__(self, eng, s, base=0):
                self.eng, self.s, self.base, self.n = eng, s, base, 0

            def __call__(self, ins):
                self.n += 1
                ins.then_inc(self.s, 1)
                self.eng.wait_ge(self.s, self.base + self.n)

        class Phases:

            def __init__(self, eng):
                self.eng, self.n = eng, 0

            def __call__(self):
                self.n += 1
                self.eng.drain().then_inc(phase_done, 1)
                self.eng.wait_ge(phase_done, 3 * self.n)

        @block.sync
        def _(sp):
            sp.dma_start(const[:, :], a["consts"]).then_inc(start_loaded, 16)
            sp.dma_start(h[:, :, :], a["x"][0].rearrange("(t p) d -> p t d", p=P)).then_inc(start_loaded, 16)
            sp.dma_start(small[:, 0:D], a["ln_emb_g"].partition_broadcast(P)).then_inc(start_loaded, 16)
            sp.dma_start(small[:, D:2 * D], a["ln_emb_b"].partition_broadcast(P)).then_inc(start_loaded, 16)

            def load(pos, i, src, width, k):
                s = i % RAW
                if not (isinstance(pos, int) and pos + i < RAW):
                    sp.wait_ge(lo_done, pos + (i - RAW + 1))
                dst = raw[:, s, 0:width].rearrange("p (k n) -> p k n", k=k)
                sp.dma_start(dst, src).then_inc(chunk_loaded[s], 16)

            def mixer(l):
                base = mix_base(l)
                w_in = a["w_in"][l].rearrange("(k p) n -> p k n", p=P)
                w_br = a["w_branch"][l].rearrange("n (k p) d -> n p k d", p=P)
                w_out = a["w_out"][l].rearrange("(k p) n -> p k n", p=P)
                i = 0
                for c0, n, _feat in SLOTS:
                    for half in range(2):
                        load(base, i, w_in[:, 4 * half:4 * half + 4, c0:c0 + n], 4 * n, 4)
                        i += 1
                for n in range(NBR):
                    for c in range(2):
                        for half in range(2):
                            c0 = C_GATE + n * D + c * 512
                            load(base, i, w_in[:, 4 * half:4 * half + 4, c0:c0 + 512], CH, 4)
                            i += 1
                    load(base, i, w_br[n], CH, 2)
                    i += 1
                for q in range(N_OUT):
                    load(base, i, w_out[:, 2 * q:2 * q + 2, :], CH, 2)
                    i += 1

            def expert(pos, w13, w2):
                for i, (m, j, half) in enumerate(ORDER):
                    if m == "w":
                        load(pos, i, w2[:, 4 * j + 2 * half:4 * j + 2 * half + 2, :], CH, 2)
                    else:
                        c0 = j * FB + (FF if m == "b" else 0)
                        load(pos, i, w13[:, 4 * half:4 * half + 4, c0:c0 + FB], CH, 4)

            mixer(0)
            with sp.Fori(0, DENSE_PASSES) as g:
                expert(g * NX + DENSE_BASE, a["ffn_w13"][0].rearrange("(k p) n -> p k n", p=P),
                       a["ffn_w2"][0].rearrange("(k p) n -> p k n", p=P))
            mixer(1)
            sp.wait_ge(items_known, 1)
            items = sp.value_load(n_items[0:1, 0:1], min_val=1, max_val=MAX_ITEMS)
            w13 = a["moe_w13"][0].rearrange("e (k p) n -> e p k n", p=P)
            w2 = a["moe_w2"][0].rearrange("e (k p) n -> e p k n", p=P)
            with sp.Fori(0, items) as g:
                e = sp.value_load(item_expert[0:1, bass.ds(g, 1)], min_val=0, max_val=NE - 1)
                expert(g * NX + MOE_BASE, w13[bass.ds(e, 1)].squeeze(0), w2[bass.ds(e, 1)].squeeze(0))
            sp.wait_ge(phase_done, 3 * N_PHASES)
            sp.dma_start(a["out"][0].rearrange("(t p) d -> p t d", p=P), h[:, :, :]).then_inc(stored, 16)
            sp.wait_ge(stored, 16)

        @block.tensor
        def _(pe):
            phase = Phases(pe)

            def three(out, l_hi, l_lo, r_hi_, r_lo_, start, stop):
                pe.matmul(out, l_hi, r_hi_, start=start, stop=False, skip_group_check=True)
                pe.matmul(out, l_hi, r_lo_, start=False, stop=False, skip_group_check=True)
                return pe.matmul(out, l_lo, r_hi_, start=False, stop=stop, skip_group_check=True)

            def chunk(pos, i):
                pe.wait_ge(lo_done, pos + (i + 1))
                return w_hi[:, i % SPL, :], w_lo[:, i % SPL, :]

            def turn(src):
                for b in range(4):
                    t, half = b // 2, b % 2
                    for i in range(4):
                        c = (4 * half + i) * P
                        mm = pe.transpose(bank(b)[:, i * P:(i + 1) * P], src[:, t, c:c + P], ident)
                    mm.then_inc(turned4, 1)

            def project(l):
                base = mix_base(l)
                for s, (c0, n, feat) in enumerate(SLOTS):
                    b0 = 2 * (s % 2)
                    if s >= 2:
                        for q in range(2):
                            pe.wait_ge(proj_used[q], l * len(SLOTS) + s - 1)
                    for half in range(2):
                        hi, lo = chunk(base, 2 * s + half)
                        for o in range(4 if feat else NT):
                            for kk in range(4):
                                k, first, last = 4 * half + kk, half == 0 and kk == 0, half == 1 and kk == 3
                                if feat:
                                    w = slice(kk * n + o * P, kk * n + (o + 1) * P)
                                    out = bank(b0 + o // 2)[:, (o % 2) * S:(o % 2 + 1) * S]
                                    mm = three(out, hi[:, w], lo[:, w], actT_hi[:, k, :], actT_lo[:, k, :],
                                               first and o % 2 == 0, last)
                                else:
                                    w = slice(kk * n, (kk + 1) * n)
                                    x = slice(o * P, (o + 1) * P)
                                    mm = three(bank(b0 + o)[:, 0:n], actT_hi[:, k, x], actT_lo[:, k, x],
                                               hi[:, w], lo[:, w], first, last)
                        mm.then_inc(chunk_used, 1)

            def operands(kind, hd, t, m):
                q = slice(t * P, (t + 1) * P)
                if kind == "dil":
                    out = []
                    for g in range(3):
                        n = g * 4 + hd
                        r = slice(64 * (n % 2), 64 * (n % 2) + 64)
                        out.append((featT[r, n // 2, q], featT[r, 6 + n // 2, :],
                                    [dilv[:, kt, n * HD:(n + 1) * HD] for kt in range(NT)]))
                    return out
                if kind == "diff":
                    r0 = (hd % 2) * 64 + m * 32
                    return [(featT[r0:r0 + 32, 12 + hd // 2, q], featT[r0:r0 + 32, 14 + hd // 2, :],
                             [diffv[:, kt, hd * HD:(hd + 1) * HD] for kt in range(NT)])]
                if kind == "mla":
                    return [(mqT[0:96, hd, q], mkT[0:96, hd, :], [mv[:, kt, hd, :] for kt in range(NT)])]
                kv = hd // 2
                return [(gT[0:64, hd, q], gT[0:64, 4 + kv, :],
                         [gqa[:, kt, 384 + kv * HD:384 + (kv + 1) * HD] for kt in range(NT)])]

            def attend(l, part):
                us = PARTS[part]
                base = l * N_UNIT + part * len(PARTS[0])
                for i in range(len(us) + 2):
                    if i < len(us):
                        u = base + i
                        if i >= 2:
                            pe.wait_ge(exps, u - 1)
                        for g, (q, k, _v) in enumerate(operands(*us[i])):
                            out = bank(2 * (i % 2) + g // 2)[:, (g % 2) * S:(g % 2 + 1) * S]
                            mm = pe.matmul(out, q, k, start=True, stop=True)
                        mm.then_inc(scores, 1)
                    if 1 <= i <= len(us):
                        u, kind = base + i - 1, us[i - 1][0]
                        pe.wait_ge(exps, u + 1)
                        for q in range(2):
                            if i >= 2 and EVACS[u][q]:
                                pe.wait_ge(turned_taken[q], EVACS[u][q])
                        for b in range(6 if kind == "dil" else 2):
                            out = bank(4 + b // 3)[:, (b % 3) * P:(b % 3 + 1) * P]
                            mm = pe.transpose(out, prob[:, (i - 1) % 2, b * P:(b + 1) * P], ident)
                        mm.then_inc(prob_turned, 1)
                    if i >= 2:
                        u, kind = base + i - 2, us[i - 2][0]
                        for q in range(2):
                            if EVAC[kind][q]:
                                pe.wait_ge(turned_taken[q], EVACS[u + 1][q])
                        if i >= 4:
                            pe.wait_ge(out_taken, u - 1)
                        vs = [v for (_q, _k, vv) in operands(*us[i - 2]) for v in vv]
                        for b, v in enumerate(vs):
                            mm = pe.matmul(bank(6 + (i - 2) % 2)[:, 0:HD],
                                           probT[:, (i - 2) % 2, b * P:(b + 1) * P], v,
                                           start=(b == 0), stop=(b == len(vs) - 1))
                        mm.then_inc(pv_done, 1)

            def prepare(l):
                pe.wait_ge(prep_dve, 5 * l + 1)
                for t in range(NT):
                    pe.transpose(bank(t)[:, 0:P], cn[:, t, 0:P], ident)
                    pe.transpose(bank(t)[0:64, P:2 * P], cn[:, t, P:QL], ident)
                    pe.transpose(bank(t)[:, 2 * P:3 * P], cn[:, t, QL:QL + KVL], ident).then_inc(prep_pe, 1)
                pe.wait_ge(params_loaded, 16 * N_PARAM * (l + 1))
                for t in range(NT):
                    x = slice(t * P, (t + 1) * P)
                    pe.wait_ge(prep_act, 6 * l + t + 1)
                    pe.matmul(bank(2 + t)[:, 0:384], cT[:, 0, x], w_uq0, start=True, stop=False)
                    pe.matmul(bank(2 + t)[:, 0:384], cT[0:64, 1, x], w_uq1, start=False, stop=True)
                    pe.matmul(bank(4 + t)[:, :], cT[:, 2, x], w_ukv, start=True, stop=True).then_inc(prep_pe, 1)
                pe.wait_ge(prep_dve, 5 * l + 2)
                for b in range(2):
                    for i in range(4):
                        hd, t = 2 * b + i // 2, i % 2
                        mm = pe.transpose(bank(6 + b)[0:64, i * P:(i + 1) * P], gr[:, t, hd * HD:(hd + 1) * HD], ident)
                    mm.then_inc(prep_pe, 1)
                for i in range(4):
                    hd, t = 4 + i // 2, i % 2
                    mm = pe.transpose(bank(0)[0:64, i * P:(i + 1) * P], gr[:, t, hd * HD:(hd + 1) * HD], ident)
                mm.then_inc(prep_pe, 1)
                pe.wait_ge(prep_dve, 5 * l + 3)
                pe.wait_ge(prep_act, 6 * l + 4)
                for src, b0 in ((mq, 2), (mk, 4)):
                    for b in range(2):
                        for i in range(4):
                            hd, t = 2 * b + i // 2, i % 2
                            mm = pe.transpose(bank(b0 + b)[0:96, i * P:(i + 1) * P], src[:, t, hd, :], ident)
                        mm.then_inc(prep_pe, 1)

            def gates(l):
                base = mix_base(l)
                for n in range(NBR):
                    i0 = N_PROJ + 5 * n
                    for c in range(2):
                        for half in range(2):
                            hi, lo = chunk(base, i0 + 2 * c + half)
                            for t in range(NT):
                                x = slice(t * P, (t + 1) * P)
                                if n and half == 0:
                                    pe.wait_ge(gate_biased, 16 * l + 4 * (n - 1) + 2 * c + t + 1)
                                for kk in range(4):
                                    k, w = 4 * half + kk, slice(kk * 512, (kk + 1) * 512)
                                    mm = three(bank(4 + 2 * c + t), actT_hi[:, k, x], actT_lo[:, k, x],
                                               hi[:, w], lo[:, w], k == 0, k == DK - 1)
                            mm.then_inc(chunk_used, 1)
                    hi, lo = chunk(base, i0 + 4)
                    if n:
                        pe.wait_ge(branch_used, 16 * l + 4 * n)
                    for c in range(2):
                        for t in range(NT):
                            x = slice(t * P, (t + 1) * P)
                            for kk in range(2):
                                w = slice(kk * D + c * 512, kk * D + (c + 1) * 512)
                                mm = three(bank(2 * c + t), brT_hi[:, 2 * n + kk, x], brT_lo[:, 2 * n + kk, x],
                                           hi[:, w], lo[:, w], kk == 0, kk == 1)
                    mm.then_inc(chunk_used, 1)

            def output(l):
                base = mix_base(l)
                for q in range(N_OUT):
                    hi, lo = chunk(base, N_PROJ + N_GATE + q)
                    for kk in range(2):
                        k = 2 * q + kk
                        for t in range(NT):
                            x = slice(t * P, (t + 1) * P)
                            for c in range(2):
                                w = slice(kk * D + c * 512, kk * D + (c + 1) * 512)
                                mm = three(bank(4 + 2 * t + c), actT_hi[:, k, x], actT_lo[:, k, x], hi[:, w], lo[:, w],
                                           k == 0, k == DK - 1)
                    mm.then_inc(chunk_used, 1)

            def expert(pos, g, moe):
                if moe:
                    pe.wait_ge(picked, g - 1)
                    for r in range(2):
                        for i in range(4):
                            d = (4 * r + i) * P
                            for t in range(NT):
                                mm = pe.matmul(bank(6 + r)[:, i * P:(i + 1) * P], h[:, t, d:d + P], pick[:, t, :],
                                               start=(t == 0), stop=(t == 1))
                        mm.then_inc(gathered, 1)
                for i, (m, j, half) in enumerate(ORDER):
                    if (m, half) == ("b", 0) and j or (m, j, half) == ("w", NB - 1, 0):
                        jt = NB - 1 if m == "w" else j - 1
                        pe.wait_ge(hid_made, g * NB + (jt + 1))
                        for q in range(4):
                            mm = pe.transpose(bank(7)[:, q * P:(q + 1) * P], hid[:, q * P:(q + 1) * P], ident)
                        mm.then_inc(hid_turned, 1)
                        if moe and jt == 1:
                            for t in range(NT):
                                mm = pe.transpose(bank(6)[:, t * P:(t + 1) * P], pick_g[:, t, :], ident)
                            mm.then_inc(pick_turned, 1)
                    hi, lo = chunk(pos, i)
                    if i == 0:
                        pe.wait_ge(x_lo_done, 2 * g + 2)
                        pe.wait_ge(acc_added, 4 * g + 1)
                    if m in "ab":
                        b = j % 2 + (2 if m == "b" else 0)
                        if j >= 2 and half == 0:
                            pe.wait_ge(hid_made, g * NB + (j - 1))
                        for kk in range(4):
                            k, w = 4 * half + kk, slice(kk * FB, (kk + 1) * FB)
                            mm = three(bank(b), xT_hi[:, k, :], xT_lo[:, k, :], hi[:, w], lo[:, w], k == 0, k == DK - 1)
                    else:
                        if half == 0:
                            pe.wait_ge(hidT_lo_done, g * NB + (j + 1))
                            if j == 0:
                                pe.wait_ge(y_free, 2 * g + 1)
                        for kk in range(2):
                            for c in range(2):
                                w = slice(kk * D + c * 512, kk * D + (c + 1) * 512)
                                mm = three(bank(4 + c), hidT_hi[:, 2 * half + kk, :], hidT_lo[:, 2 * half + kk, :],
                                           hi[:, w], lo[:, w], (j, half, kk) == (0, 0, 0), (j, half, kk) == (NB - 1, 1, 1))
                    mm.then_inc(chunk_used, 1)
                if moe:
                    pe.wait_ge(y_free, 2 * g + 3)
                    pe.wait_ge(pickT_ready, g - 1)
                    for t in range(NT):
                        for c in range(2):
                            mm = pe.matmul(bank(2 * t + c), pick_gT[:, t * P:(t + 1) * P], y_exp[:, c * 512:(c + 1) * 512],
                                           start=True, stop=True)
                            mm.then_inc(scattered, 1)

            def route():
                pe.wait_ge(router_lo, 1)
                for t in range(NT):
                    x = slice(t * P, (t + 1) * P)
                    for k in range(DK):
                        mm = three(bank(t)[:, 0:NE], actT_hi[:, k, x], actT_lo[:, k, x], r_hi[:, k, :], r_lo[:, k, :],
                                   k == 0, k == DK - 1)
                mm.then_inc(logits_done, 1)
                pe.wait_ge(sel_done, 1)
                pe.matmul(bank(2)[:, 0:NE], tri, sel[:, 0, :], start=True, stop=True)
                pe.matmul(bank(3)[:, 0:NE], ones, sel[:, 0, :], start=True, stop=False)
                pe.matmul(bank(3)[:, 0:NE], tri, sel[:, 1, :], start=False, stop=True)
                pe.matmul(bank(4)[:, 0:NE], ones, sel[:, 0, :], start=True, stop=False)
                pe.matmul(bank(4)[:, 0:NE], ones, sel[:, 1, :], start=False, stop=True).then_inc(counted, 1)

            def mixer(l):
                turn(h)
                phase()
                project(l)
                phase()
                attend(l, 0)
                phase()
                prepare(l)
                phase()
                attend(l, 1)
                phase()
                phase()
                turn(y)
                phase()
                gates(l)
                phase()
                turn(y)
                phase()
                output(l)
                phase()
                phase()
                turn(h)
                phase()

            pe.wait_ge(start_loaded, 64)
            phase()
            mixer(0)
            with pe.Fori(0, DENSE_PASSES) as g:
                expert(g * NX + DENSE_BASE, g, False)
            phase()
            phase()
            mixer(1)
            route()
            phase()
            pe.wait_ge(items_known, 1)
            items = pe.value_load(n_items[0:1, 0:1], min_val=1, max_val=MAX_ITEMS)
            with pe.Fori(0, items) as g:
                expert(g * NX + MOE_BASE, pe.snap(g + DENSE_PASSES), True)
            phase()
            phase()

        @block.scalar
        def _(act):
            phase = Phases(act)
            step = Steps(act, act_step)

            def split(pos, i, width=CH):
                s, q = i % RAW, i % SPL
                turns = pos // RAW if isinstance(pos, int) else None
                if turns is None:
                    act.wait_ge(chunk_loaded[s], loop_turns[0] + 16 * (i // RAW + 1))
                else:
                    act.wait_ge(chunk_loaded[s], 16 * (turns + i // RAW + 1))
                if not (isinstance(pos, int) and pos + i < SPL):
                    act.wait_ge(chunk_used, pos + (i - SPL + 1))
                act.activation(w_hi[:, q, 0:width], raw[:, s, 0:width], ACT.Copy).then_inc(hi_done, 1)

            loop_turns = [None]

            def take_turned(n, dst_hi):
                for b in range(4):
                    t, half = b // 2, b % 2
                    act.wait_ge(turned4, 4 * n + b + 1)
                    act.activation(dst_hi[:, 4 * half:4 * half + 4, t * P:(t + 1) * P],
                                   bank(b).rearrange("p (k t) -> p k t", k=4), ACT.Copy).then_inc(turn_hi, 1)

            def load_gains(g, b):
                act.dma_start(small[:, 0:D], g.partition_broadcast(P)).then_inc(gains_loaded, 16)
                act.dma_start(small[:, D:2 * D], b.partition_broadcast(P)).then_inc(gains_loaded, 16)

            def load_params(l):
                q = a["mla_w_uq"][l]
                for dst, src in ((w_uq0, q[0:P, :]), (w_uq1, q[P:QL, :]), (w_ukv, a["mla_w_ukv"][l]),
                                 (g_q, a["mla_q_norm"][l].partition_broadcast(P)),
                                 (g_kv, a["mla_kv_norm"][l].partition_broadcast(P)),
                                 (g_sub, a["diff_subln"][l].partition_broadcast(P)),
                                 (lamp[:, :, :], a["diff_lambda"][l].partition_broadcast(P))):
                    act.dma_start(dst, src).then_inc(params_loaded, 16)
                for hd in range(6):
                    g = a["gqa_q_norm" if hd < 4 else "gqa_k_norm"][l].partition_broadcast(P)
                    act.dma_start(g_gqa[:, hd * HD:(hd + 1) * HD], g).then_inc(params_loaded, 16)

            def norm_std(n):
                act.wait_ge(var_ready, n + 1)
                act.activation(stat[:, 16:32], stat[:, 0:16], ACT.Sqrt).then_inc(std_ready, 1)

            def project(l):
                base = mix_base(l)
                for s, (c0, n, feat) in enumerate(SLOTS):
                    for half in range(2):
                        i = 2 * s + half
                        if i == 0:
                            for q in range(AHEAD):
                                split(base, q, MIX_WIDTH[q])
                        if i + AHEAD < N_PROJ:
                            split(base, i + AHEAD, MIX_WIDTH[i + AHEAD])
                    b0 = 2 * (s % 2)
                    act.wait_ge(chunk_used, base + 2 * s + 2)
                    if feat:
                        f = (c0 - C_FEAT) // P if c0 < C_DV else 12
                        scale = HD ** -0.5 if f < 6 else 32 ** -0.5 if f == 12 else 1.0
                        act.activation(featT[:, f:f + 2, :], bank(b0).rearrange("p (b t) -> p b t", b=2), ACT.Copy,
                                       scale=scale).then_inc(proj_used[0], 1)
                    else:
                        act.activation(token_dst(c0, n, 0), bank(b0)[:, 0:n], ACT.Copy).then_inc(proj_used[0], 1)

            def attend(l, part):
                us = PARTS[part]
                base = l * N_UNIT + part * len(PARTS[0])
                for i in range(len(us) + 1):
                    if i < len(us):
                        u, kind = base + i, us[i][0]
                        n = 3 * S if kind == "dil" else S
                        act.wait_ge(negmax, u + 1)
                        if i >= 2:
                            act.wait_ge(prob_turned, u - 1)
                        src = prob[:, i % 2, 0:n] if part == 0 else bank(2 * (i % 2))[:, 0:n]
                        act.activation(prob[:, i % 2, 0:n], src, ACT.Exp, bias=stat[:, 32 + i % 2:33 + i % 2],
                                       scale=scale_of(kind), accum_out=stat[:, 36 + i % 4:37 + i % 4]).then_inc(exps, 1)
                    if i >= 1 and EVAC[us[i - 1][0]][0]:
                        u, kind = base + i - 1, us[i - 1][0]
                        act.wait_ge(prob_turned, u + 1)
                        if i >= 3:
                            act.wait_ge(pv_done, u - 1)
                        n = 384 if kind == "dil" else S
                        act.activation(probT[:, (i - 1) % 2, 0:n], bank(4)[:, 0:n], ACT.Copy).then_inc(turned_taken[0], 1)

            def prepare(l):
                norm_std(VAR_PREP[l])
                for t in range(NT):
                    act.wait_ge(prep_pe, 11 * l + t + 1)
                    x = slice(t * P, (t + 1) * P)
                    act.activation(cT[:, 0, x], bank(t)[:, 0:P], ACT.Copy)
                    act.activation(cT[0:64, 1, x], bank(t)[0:64, P:2 * P], ACT.Copy)
                    act.activation(cT[:, 2, x], bank(t)[:, 2 * P:3 * P], ACT.Copy).then_inc(prep_act, 1)
                for t in range(NT):
                    act.wait_ge(prep_pe, 11 * l + 2 + t + 1)
                    q = bank(2 + t)[:, 0:384].rearrange("p (h d) -> p h d", h=4)
                    kv = bank(4 + t).rearrange("p (h d) -> p h d", h=4)
                    act.activation(mq[:, t, :, 0:64], q[:, :, 0:64], ACT.Copy)
                    act.activation(mk[:, t, :, 0:64], kv[:, :, 0:64], ACT.Copy)
                    act.activation(mv[:, t, :, :], kv[:, :, 64:128], ACT.Copy).then_inc(prep_act, 1)
                for b in range(2):
                    act.wait_ge(prep_pe, 11 * l + 4 + b + 1)
                    if b == 0:
                        act.wait_ge(prep_dve, 5 * l + 3)
                    act.activation(gT[0:64, 2 * b:2 * b + 2, :], bank(6 + b)[0:64].rearrange("p (h t) -> p h t", h=2),
                                   ACT.Copy)
                for b in range(2):
                    act.wait_ge(prep_pe, 11 * l + 7 + b + 1)
                    act.activation(mqT[0:96, 2 * b:2 * b + 2, :], bank(2 + b)[0:96].rearrange("p (h t) -> p h t", h=2),
                                   ACT.Copy).then_inc(prep_act, 1)

            def gates(l):
                base = mix_base(l)
                load_gains(a["ln1_g"][l], a["ln1_b"][l])
                for n in range(NBR):
                    act.dma_start(gate_bias[:, n, :], a["b_gate"][l][n].partition_broadcast(P)).then_inc(bias_loaded, 16)
                for q in range(AHEAD):
                    split(base, N_PROJ + q)
                for i in range(N_GATE):
                    if i + AHEAD < N_GATE:
                        split(base, N_PROJ + i + AHEAD)
                    n, c = i // 5, (i % 5) // 2
                    if i % 5 in (1, 3):
                        for t in range(NT):
                            k = 16 * l + 4 * n + 2 * c + t
                            act.wait_ge(gate_biased, k + 1)
                            s = gate_sb[:, 2 * c + t, :]
                            act.activation(s, s, ACT.Sigmoid).then_inc(gate_open, 1)

            def output(l):
                base = mix_base(l) + N_PROJ + N_GATE
                for q in range(N_OUT):
                    split(mix_base(l), N_PROJ + N_GATE + q)

            def expert(pos, g, moe, tile=None):
                for q in range(AHEAD):
                    split(pos, q)
                if moe:
                    for r in range(2):
                        act.wait_ge(gathered, 2 * g + (r - 3))
                        act.activation(xT_hi[:, 4 * r:4 * r + 4, :], bank(6 + r).rearrange("p (k s) -> p k s", k=4),
                                       ACT.Copy).then_inc(x_hi_done, 1)
                else:
                    act.wait_ge(chunk_used, pos)
                    act.activation(xT_hi, actT_hi[:, :, bass.ds(tile, P)].bitcast(F32), ACT.Copy).then_inc(x_hi_done, 2)
                for i, (m, j, half) in enumerate(ORDER):
                    if i + AHEAD < NX:
                        split(pos, i + AHEAD)
                    if (m, half) == ("a", 1):
                        act.wait_ge(chunk_used, pos + (i + 1))
                        if j:
                            act.wait_ge(hid_made, g * NB + j)
                        act.activation(silu, bank(j % 2), ACT.Silu).then_inc(silu_done, 1)
                    if ((m, half) == ("a", 1) and j) or (m, j, half) == ("w", NB - 2, 1):
                        jt = NB - 1 if m == "w" else j - 1
                        act.wait_ge(hid_turned, g * NB + (jt + 1))
                        act.activation(hidT_hi, bank(7).rearrange("p (k s) -> p k s", k=4), ACT.Copy).then_inc(hidT_hi_done, 1)
                        if moe and jt == 1:
                            act.wait_ge(pick_turned, g - 1)
                            act.activation(pick_gT, bank(6)[:, 0:S], ACT.Copy).then_inc(pickT_ready, 1)
                act.wait_ge(chunk_used, pos + NX)
                if moe:
                    act.activation(y_exp[:, 0:512], bank(4), ACT.Copy).then_inc(y_free, 1)
                else:
                    act.activation(acc[:, bass.ds(g, 1), 0:512].squeeze(1), bank(4), ACT.Copy).then_inc(y_free, 1)

            def route():
                act.dma_start(r_raw, a["moe_router"][0].rearrange("(k p) e -> p k e", p=P)).then_inc(router_loaded, 16)
                act.wait_ge(router_loaded, 16)
                act.activation(r_hi[:, :, :], r_raw, ACT.Copy).then_inc(router_hi, 1)
                act.wait_ge(expo_in, 1)
                for t in range(NT):
                    act.activation(expo[:, t, :], logit[:, t, :], ACT.Exp, bias=stat[:, 40 + t:41 + t]).then_inc(expo_out, 1)

            def mixer(l):
                load_params(l)
                take_turned(4 * l, actT_hi)
                phase()
                project(l)
                phase()
                act.wait_ge(lam_sum, l + 1)
                act.activation(stat[:, 50:52], stat[:, 48:50], ACT.Exp).then_inc(lam_exp, 1)
                attend(l, 0)
                phase()
                prepare(l)
                phase()
                attend(l, 1)
                phase()
                norm_std(VAR_PREP[l] + 1)
                phase()
                take_turned(4 * l + 1, brT_hi)
                phase()
                gates(l)
                phase()
                take_turned(4 * l + 2, actT_hi)
                phase()
                output(l)
                phase()
                norm_std(VAR_PREP[l] + 2)
                phase()
                take_turned(4 * l + 3, actT_hi)
                phase()

            act.wait_ge(start_loaded, 64)
            norm_std(0)
            phase()
            mixer(0)
            load_gains(a["ln2_g"][0], a["ln2_b"][0])
            with act.Fori(0, DENSE_PASSES) as g:
                loop_turns[0] = act.snap(g * (16 * NX // RAW) + 16 * DENSE_BASE // RAW)
                expert(g * NX + DENSE_BASE, g, False, act.snap(g * P))
            phase()
            norm_std(VAR_PREP[0] + 3)
            phase()
            mixer(1)
            load_gains(a["ln2_g"][1], a["ln2_b"][1])
            route()
            phase()
            act.wait_ge(items_known, 1)
            items = act.value_load(n_items[0:1, 0:1], min_val=1, max_val=MAX_ITEMS)
            with act.Fori(0, items) as g:
                loop_turns[0] = act.snap(g * (16 * NX // RAW) + 16 * MOE_BASE // RAW)
                expert(g * NX + MOE_BASE, act.snap(g + DENSE_PASSES), True)
            phase()
            norm_std(VAR_PREP[1] + 3)
            phase()

        @block.vector
        def _(dve):
            phase = Phases(dve)
            step = Steps(dve, dve_step)

            def split(pos, i, width=CH):
                s, q = i % RAW, i % SPL
                dve.wait_ge(hi_done, pos + (i + 1))
                dve.tensor_tensor(w_lo[:, q, 0:width], raw[:, s, 0:width], w_hi[:, q, 0:width].bitcast(F32),
                                  ALU.subtract).then_inc(lo_done, 1)

            def take_turned(n, dst_hi, dst_lo):
                for b in range(4):
                    t, half = b // 2, b % 2
                    x = (slice(None), slice(4 * half, 4 * half + 4), slice(t * P, (t + 1) * P))
                    dve.wait_ge(turn_hi, 4 * n + b + 1)
                    dve.tensor_tensor(dst_lo[x], bank(b).rearrange("p (k t) -> p k t", k=4), dst_hi[x].bitcast(F32),
                                      ALU.subtract)

            def std(n):
                dve.wait_ge(std_ready, n + 1)
                r, v = stat[:, 16:32], stat[:, 0:16]
                step(dve.reciprocal(r, r))
                step(dve.tensor_tensor(v, v, r, ALU.mult))
                step(dve.tensor_tensor(v, v, r, ALU.mult))
                step(dve.tensor_scalar(v, v, -0.5, 1.5, ALU.mult, ALU.add))
                step(dve.tensor_tensor(r, r, v, ALU.mult))

            def layernorm(n, gains_at):
                for t in range(NT):
                    for c in range(2):
                        last = dve.bn_stats(stat[:, 56 + 12 * t + 6 * c:62 + 12 * t + 6 * c], h[:, t, c * 512:(c + 1) * 512])
                step(last)
                for t in range(NT):
                    step(dve.bn_aggr(stat[:, 80 + 2 * t:82 + 2 * t], stat[:, 56 + 12 * t:68 + 12 * t]))
                step(dve.memset(stat[:, 0:16], 1.0))
                dve.tensor_scalar(stat[:, 0:2], stat[:, 81:84:2], LN_EPS, None, ALU.add).then_inc(var_ready, 1)
                std(n)
                if gains_at:
                    dve.wait_ge(gains_loaded, 32 * gains_at)
                for t in range(NT):
                    step(dve.tensor_scalar(h[:, t, :], h[:, t, :], stat[:, 80 + 2 * t:81 + 2 * t], stat[:, 16 + t:17 + t],
                                           ALU.subtract, ALU.mult))
                    step(dve.tensor_tensor(h[:, t, :], h[:, t, :], small[:, 0:D], ALU.mult))
                    step(dve.tensor_tensor(h[:, t, :], h[:, t, :], small[:, D:2 * D], ALU.add))

            def project(l):
                base = mix_base(l)
                for s, (c0, n, feat) in enumerate(SLOTS):
                    for half in range(2):
                        i = 2 * s + half
                        if i == 0:
                            for q in range(AHEAD):
                                split(base, q, MIX_WIDTH[q])
                        if i + AHEAD < N_PROJ:
                            split(base, i + AHEAD, MIX_WIDTH[i + AHEAD])
                    b1 = 2 * (s % 2) + 1
                    dve.wait_ge(chunk_used, base + 2 * s + 2)
                    if feat:
                        f = ((c0 - C_FEAT) // P if c0 < C_DV else 12) + 2
                        dve.tensor_scalar(featT[:, f:f + 2, :], bank(b1).rearrange("p (b t) -> p b t", b=2),
                                          HD ** -0.5 if f < 6 else 1.0, None, ALU.mult).then_inc(proj_used[1], 1)
                    else:
                        dve.tensor_copy(token_dst(c0, n, 1), bank(b1)[:, 0:n]).then_inc(proj_used[1], 1)

            def diff_lambda(l):
                init = 0.8 - 0.6 * math.exp(-0.3 * l)
                dve.wait_ge(params_loaded, 16 * N_PARAM * (l + 1))
                lp = lamp[:, :, :].rearrange("p (m w) d -> p m w d", w=2)
                prod = prob[:, 0, 0:64].rearrange("p (m d) -> p m d", m=2)
                step(dve.tensor_tensor(prod, lp[:, :, 0, :], lp[:, :, 1, :], ALU.mult))
                dve.tensor_reduce(stat[:, 48:50], prod, AX.X, ALU.add).then_inc(lam_sum, 1)
                dve.wait_ge(lam_exp, l + 1)
                step(dve.tensor_tensor(stat[:, 52:53], stat[:, 51:52], stat[:, 50:51], ALU.subtract))
                step(dve.tensor_scalar(stat[:, 52:53], stat[:, 52:53], -init, None, ALU.add))

            def attend(l, part):
                us = PARTS[part]
                base = l * N_UNIT + part * len(PARTS[0])
                for i in range(len(us) + 2):
                    if i < len(us):
                        u = base + i
                        kind, hd, t, m = us[i]
                        nm = stat[:, 32 + i % 2:33 + i % 2]
                        dve.wait_ge(scores, u + 1)
                        if i >= 2:
                            dve.wait_ge(prob_turned, u - 1)
                            dve.wait_ge(exps, u - 1)
                        if part == 0:
                            for g in range(3 if kind == "dil" else 1):
                                slope = 2.0 ** (-8.0 * (4 * g + hd + 1) / 12) if kind == "dil" else 2.0 ** (-8.0 * (hd + 1) / 4)
                                k = K_DIST + 384 * (g if kind == "dil" else 3) + P * (1 - t)
                                last = dve.scalar_tensor_tensor(
                                    prob[:, i % 2, g * S:(g + 1) * S], const[:, k:k + S], -slope,
                                    bank(2 * (i % 2) + g // 2)[:, (g % 2) * S:(g % 2 + 1) * S], ALU.mult, ALU.add)
                            step(last)
                            n = 3 * S if kind == "dil" else S
                            dve.tensor_reduce(nm, prob[:, i % 2, 0:n], AX.X, ALU.max, negate=True).then_inc(negmax, 1)
                        else:
                            step(dve.tensor_reduce(nm, bank(2 * (i % 2))[:, 0:S], AX.X, ALU.max, negate=True))
                            dve.tensor_scalar(nm, nm, scale_of(kind), None, ALU.mult).then_inc(negmax, 1)
                    if 1 <= i <= len(us) and EVAC[us[i - 1][0]][1]:
                        u, kind = base + i - 1, us[i - 1][0]
                        dve.wait_ge(prob_turned, u + 1)
                        if i >= 3:
                            dve.wait_ge(pv_done, u - 1)
                        if kind == "dil":
                            dve.tensor_copy(probT[:, (i - 1) % 2, 384:768], bank(5)[:, 0:384]).then_inc(turned_taken[1], 1)
                        else:
                            dve.tensor_copy(probT[:, (i - 1) % 2, 0:S], bank(4)[:, 0:S]).then_inc(turned_taken[1], 1)
                    if i >= 2:
                        u = base + i - 2
                        kind, hd, t, m = us[i - 2]
                        r = stat[:, 44:45]
                        c0 = {"mla": 0, "dil": 1, "gqa": 2, "diff": 3}[kind] * BW + hd * HD
                        dst, o = y[:, t, c0:c0 + HD], bank(6 + (i - 2) % 2)[:, 0:HD]
                        step(dve.reciprocal(r, stat[:, 36 + (i - 2) % 4:37 + (i - 2) % 4]))
                        dve.wait_ge(pv_done, u + 1)
                        if m:
                            step(dve.tensor_tensor(r, r, stat[:, 52:53], ALU.mult))
                            step(dve.scalar_tensor_tensor(dst, o, r, dst, ALU.mult, ALU.add))
                        else:
                            step(dve.tensor_scalar(dst, o, r, None, ALU.mult))
                        dve.engine_nop().then_inc(out_taken, 1)

            def rope(dst, x, tmp, cos, sin, n):
                dve.tensor_tensor(tmp[:, :, :, 0, :], x[:, :, :, 1, :], sin[:, :, :, 0, :], ALU.mult)
                dve.tensor_tensor(tmp[:, :, :, 1, :], x[:, :, :, 0, :], sin[:, :, :, 1, :], ALU.mult)

            def prepare(l):
                cq, ck = cqkv[:, :, 0:QL], cqkv[:, :, QL:QL + KVL]
                step(dve.memset(stat[:, 0:16], 1.0))
                step(dve.tensor_tensor(sq_c, cqkv[:, :, 0:QL + KVL], cqkv[:, :, 0:QL + KVL], ALU.mult))
                dve.tensor_reduce(stat[:, 0:2], sq_c[:, :, 0:QL], AX.X, ALU.add)
                dve.tensor_reduce(stat[:, 2:4], sq_c[:, :, QL:QL + KVL], AX.X, ALU.add)
                step(dve.tensor_tensor(gn, gqa[:, :, 0:384], gqa[:, :, 0:384], ALU.mult))
                step(dve.tensor_reduce(stat[:, 4:16], gn.rearrange("p t (h d) -> p (t h) d", d=HD), AX.X, ALU.add))
                dve.tensor_scalar(stat[:, 0:2], stat[:, 0:2], 1.0 / QL, RMS_EPS, ALU.mult, ALU.add)
                dve.tensor_scalar(stat[:, 2:4], stat[:, 2:4], 1.0 / KVL, RMS_EPS, ALU.mult, ALU.add)
                dve.tensor_scalar(stat[:, 4:16], stat[:, 4:16], 1.0 / HD, RMS_EPS, ALU.mult, ALU.add).then_inc(var_ready, 1)
                std(VAR_PREP[l])
                for t in range(NT):
                    dve.scalar_tensor_tensor(cn[:, t, 0:QL], cqkv[:, t, 0:QL], stat[:, 16 + t:17 + t], g_q, ALU.mult, ALU.mult)
                    last = dve.scalar_tensor_tensor(cn[:, t, QL:QL + KVL], cqkv[:, t, QL:QL + KVL], stat[:, 18 + t:19 + t],
                                                    g_kv, ALU.mult, ALU.mult)
                last.then_inc(prep_dve, 1)
                for t in range(NT):
                    x3 = gn[:, t, :].rearrange("p (h d) -> p h d", d=HD)
                    rs = stat[:, 20 + 6 * t:26 + 6 * t].unsqueeze(2).to_broadcast([P, 6, HD])
                    step(dve.tensor_tensor(x3, gqa[:, t, 0:384].rearrange("p (h d) -> p h d", d=HD), rs, ALU.mult))
                    step(dve.tensor_tensor(gn[:, t, :], gn[:, t, :], g_gqa, ALU.mult))
                    x5 = gn[:, t, :].rearrange("p (h a w d) -> p h a w d", h=6, a=2, w=2)
                    r5 = rope_a[:, t, :].rearrange("p (h a w d) -> p h a w d", h=6, a=2, w=2)
                    sin = const[:, K_GS + 64 * t:K_GS + 64 * t + 64].rearrange("p (a w d) -> p a w d", a=2, w=2)
                    cos = const[:, K_GC + 64 * t:K_GC + 64 * t + 64]
                    for w in range(2):
                        dve.tensor_tensor(r5[:, :, :, w, :], x5[:, :, :, 1 - w, :],
                                          sin[:, :, w, :].unsqueeze(1).to_broadcast([P, 6, 2, 16]), ALU.mult)
                    step(dve.tensor_tensor(gr[:, t, :].rearrange("p (h d) -> p h d", d=HD), x3,
                                           cos.unsqueeze(1).to_broadcast([P, 6, HD]), ALU.mult))
                    last = dve.tensor_tensor(gr[:, t, :], gr[:, t, :], rope_a[:, t, :], ALU.add)
                last.then_inc(prep_dve, 1)
                for t in range(NT):
                    sin = const[:, K_MS + 32 * t:K_MS + 32 * t + 32].rearrange("p (w d) -> p w d", w=2)
                    cos = const[:, K_MC + 32 * t:K_MC + 32 * t + 32]
                    dve.wait_ge(prep_act, 6 * l + 2 + t + 1)
                    q = bank(2 + t)[:, 0:384].rearrange("p (h d) -> p h d", h=4)[:, :, 64:96]
                    q4 = q.rearrange("p h (w d) -> p h w d", w=2)
                    tq = rope_m[:, t, 0:P].rearrange("p (h w d) -> p h w d", h=4, w=2)
                    tc = rope_m[:, t, P:2 * P].rearrange("p (h d) -> p h d", h=4)
                    for w in range(2):
                        dve.tensor_tensor(tq[:, :, w, :], q4[:, :, 1 - w, :],
                                          sin[:, w, :].unsqueeze(1).to_broadcast([P, 4, 16]), ALU.mult)
                    step(dve.tensor_tensor(tc, q, cos.unsqueeze(1).to_broadcast([P, 4, 32]), ALU.mult))
                    step(dve.tensor_tensor(mq[:, t, :, 64:96], tc, rope_m[:, t, 0:P].rearrange("p (h d) -> p h d", h=4), ALU.add))
                    kr = cqkv[:, t, QL + KVL:QL + KVL + MR].rearrange("p (w d) -> p w d", w=2)
                    tk = rope_m[:, t, 0:32].rearrange("p (w d) -> p w d", w=2)
                    for w in range(2):
                        dve.tensor_tensor(tk[:, w, :], kr[:, 1 - w, :], sin[:, w, :], ALU.mult)
                    step(dve.tensor_tensor(rope_m[:, t, 32:64], cqkv[:, t, QL + KVL:QL + KVL + MR], cos, ALU.mult))
                    last = dve.tensor_tensor(mk[:, t, :, 64:96], rope_m[:, t, 0:32].unsqueeze(1).to_broadcast([P, 4, 32]),
                                             rope_m[:, t, 32:64].unsqueeze(1).to_broadcast([P, 4, 32]), ALU.add)
                last.then_inc(prep_dve, 1)
                dve.wait_ge(prep_pe, 11 * l + 7)
                dve.tensor_copy(gT[0:64, 4:6, :], bank(0)[0:64].rearrange("p (h t) -> p h t", h=2)).then_inc(prep_dve, 1)
                for b in range(2):
                    dve.wait_ge(prep_pe, 11 * l + 9 + b + 1)
                    last = dve.tensor_copy(mkT[0:96, 2 * b:2 * b + 2, :], bank(4 + b)[0:96].rearrange("p (h t) -> p h t", h=2))
                last.then_inc(prep_dve, 1)

            def diff_norm(l):
                init = 0.8 - 0.6 * math.exp(-0.3 * l)
                sq = prob[:, 0, 0:512].rearrange("p (t n) -> p t n", t=NT)
                yd = y[:, :, 3 * BW:4 * BW]
                step(dve.memset(stat[:, 0:16], 1.0))
                step(dve.tensor_tensor(sq, yd, yd, ALU.mult))
                step(dve.tensor_reduce(stat[:, 0:8], sq.rearrange("p t (h d) -> p (t h) d", d=HD), AX.X, ALU.add))
                dve.tensor_scalar(stat[:, 0:8], stat[:, 0:8], 1.0 / HD, DIFF_EPS, ALU.mult, ALU.add).then_inc(var_ready, 1)
                std(VAR_PREP[l] + 1)
                for t in range(NT):
                    yt = y[:, t, 3 * BW:4 * BW].rearrange("p (h d) -> p h d", d=HD)
                    rs = stat[:, 16 + 4 * t:20 + 4 * t].unsqueeze(2).to_broadcast([P, 4, HD])
                    step(dve.tensor_tensor(yt, yt, rs, ALU.mult))
                    step(dve.tensor_tensor(yt, yt, g_sub.unsqueeze(1).to_broadcast([P, 4, HD]), ALU.mult))
                    step(dve.tensor_scalar(yt, yt, 1.0 - init, None, ALU.mult))

            def gates(l):
                base = mix_base(l)
                for q in range(AHEAD):
                    split(base, N_PROJ + q)
                dve.wait_ge(bias_loaded, 16 * NBR * (l + 1))
                for i in range(N_GATE):
                    if i + AHEAD < N_GATE:
                        split(base, N_PROJ + i + AHEAD)
                    n, c = i // 5, (i % 5) // 2
                    if i % 5 in (1, 3):
                        dve.wait_ge(chunk_used, base + N_PROJ + i + 1)
                        for t in range(NT):
                            dve.tensor_tensor(gate_sb[:, 2 * c + t, :], bank(4 + 2 * c + t),
                                              gate_bias[:, n, c * 512:(c + 1) * 512], ALU.add).then_inc(gate_biased, 1)
                    if i % 5 == 4:
                        dve.wait_ge(chunk_used, base + N_PROJ + i + 1)
                        for c in range(2):
                            for t in range(NT):
                                k = 16 * l + 4 * n + 2 * c + t
                                dst = y[:, t, c * 512:(c + 1) * 512]
                                dve.wait_ge(gate_open, k + 1)
                                if n == 0:
                                    step(dve.tensor_tensor(dst, gate_sb[:, 2 * c + t, :], bank(2 * c + t), ALU.mult))
                                else:
                                    pr = gate_pr[:, t, :]
                                    step(dve.tensor_tensor(pr, gate_sb[:, 2 * c + t, :], bank(2 * c + t), ALU.mult))
                                    step(dve.tensor_tensor(dst, dst, pr, ALU.add))
                                dve.engine_nop().then_inc(branch_used, 1)

            def output(l):
                for q in range(N_OUT):
                    split(mix_base(l), N_PROJ + N_GATE + q)
                dve.wait_ge(chunk_used, mix_base(l) + N_MIX)
                for t in range(NT):
                    for c in range(2):
                        x = h[:, t, c * 512:(c + 1) * 512]
                        step(dve.scalar_tensor_tensor(x, x, ALPHA, bank(4 + 2 * t + c), ALU.mult, ALU.add))

            def expert(pos, g, moe, tile=None, item=None):
                if moe:
                    dve.wait_ge(pickT_ready, g - 1)
                    for t in range(NT):
                        s_i = item_slot[:, t, bass.ds(item, 1)]
                        dve.tensor_scalar(pick[:, t, :], iota, s_i, None, ALU.is_equal)
                        last = dve.tensor_scalar(pick_g[:, t, :], iota, s_i, item_gate[:, t, bass.ds(item, 1)],
                                                 ALU.is_equal, ALU.mult)
                    last.then_inc(picked, 1)
                for q in range(AHEAD):
                    split(pos, q)
                if moe:
                    for r in range(2):
                        dve.wait_ge(x_hi_done, 2 * g + (r + 1))
                        dve.tensor_tensor(xT_lo[:, 4 * r:4 * r + 4, :], bank(6 + r).rearrange("p (k s) -> p k s", k=4),
                                          xT_hi[:, 4 * r:4 * r + 4, :].bitcast(F32), ALU.subtract).then_inc(x_lo_done, 1)
                else:
                    dve.wait_ge(x_hi_done, 2 * g + 2)
                    dve.tensor_copy(xT_lo, actT_lo[:, :, bass.ds(tile, P)].bitcast(F32)).then_inc(x_lo_done, 2)
                for i, (m, j, half) in enumerate(ORDER):
                    if i + AHEAD < NX:
                        split(pos, i + AHEAD)
                    if (m, half) == ("b", 1):
                        dve.wait_ge(chunk_used, pos + (i + 1))
                        dve.wait_ge(silu_done, g * NB + (j + 1))
                        dve.tensor_tensor(hid, silu, bank(2 + j % 2), ALU.mult).then_inc(hid_made, 1)
                    if ((m, half) == ("a", 1) and j) or (m, j, half) == ("w", NB - 2, 1):
                        jt = NB - 1 if m == "w" else j - 1
                        dve.wait_ge(hidT_hi_done, g * NB + (jt + 1))
                        dve.tensor_tensor(hidT_lo, bank(7).rearrange("p (k s) -> p k s", k=4), hidT_hi.bitcast(F32),
                                          ALU.subtract).then_inc(hidT_lo_done, 1)
                dve.wait_ge(chunk_used, pos + NX)
                if moe:
                    dve.tensor_copy(y_exp[:, 512:1024], bank(5)).then_inc(y_free, 1)
                    for t in range(NT):
                        for c in range(2):
                            x = acc[:, t, c * 512:(c + 1) * 512]
                            dve.wait_ge(scattered, 4 * g + (2 * t + c - 7))
                            dve.tensor_tensor(x, x, bank(2 * t + c), ALU.add).then_inc(acc_added, 1)
                else:
                    dve.tensor_copy(acc[:, bass.ds(g, 1), 512:1024].squeeze(1), bank(5)).then_inc(y_free, 1)
                    dve.engine_nop().then_inc(acc_added, 4)

            def route():
                dve.wait_ge(router_hi, 1)
                dve.tensor_tensor(r_lo[:, :, :], r_raw, r_hi[:, :, :].bitcast(F32), ALU.subtract).then_inc(router_lo, 1)
                dve.wait_ge(logits_done, 1)
                for t in range(NT):
                    step(dve.tensor_copy(logit[:, t, :], bank(t)[:, 0:NE]))
                step(dve.tensor_reduce(stat[:, 40:42], logit, AX.X, ALU.max, negate=True))
                dve.engine_nop().then_inc(expo_in, 1)
                tie = const[:, K_TIE:K_TIE + 64]
                for t in range(NT):
                    this = logit[:, t, :].unsqueeze(2).to_broadcast([P, NE, NE])
                    other = logit[:, t, :].unsqueeze(1).to_broadcast([P, NE, NE])
                    ca = cmp_a[:, t, :].rearrange("p (e f) -> p e f", e=NE)
                    cb = cmp_b[:, t, :].rearrange("p (e f) -> p e f", e=NE)
                    step(dve.tensor_tensor(ca, other, this, ALU.is_gt))
                    step(dve.tensor_tensor(cb, other, this, ALU.is_equal))
                    step(dve.tensor_tensor(cmp_b[:, t, :], cmp_b[:, t, :], tie, ALU.mult))
                    step(dve.tensor_tensor(cmp_a[:, t, :], cmp_a[:, t, :], cmp_b[:, t, :], ALU.add))
                    step(dve.tensor_reduce(rank[:, t, :], ca, AX.X, ALU.add))
                dve.tensor_scalar(sel, rank, 2.0, None, ALU.is_lt).then_inc(sel_done, 1)
                dve.wait_ge(sel_done, 1)
                dve.wait_ge(expo_out, 2)
                step(dve.tensor_tensor(expo, expo, sel, ALU.mult))
                step(dve.tensor_reduce(stat[:, 42:44], expo, AX.X, ALU.add))
                step(dve.reciprocal(stat[:, 42:44], stat[:, 42:44]))
                for t in range(NT):
                    step(dve.tensor_scalar(gate[:, t, :], expo[:, t, :], stat[:, 42 + t:43 + t], None, ALU.mult))
                step(dve.tensor_scalar(slot, sel, -NOWHERE, NOWHERE, ALU.mult, ALU.add))
                dve.wait_ge(counted, 1)
                for t in range(NT):
                    step(dve.tensor_tensor(slot[:, t, :], slot[:, t, :], bank(2 + t)[:, 0:NE], ALU.add))
                step(dve.tensor_scalar(tiles_of[:, 0, :], bank(4)[:, 0:NE], 0.0, None, ALU.is_gt))
                step(dve.tensor_scalar(tiles_of[:, 1, :], bank(4)[:, 0:NE], float(P), None, ALU.is_gt))
                step(dve.tensor_tensor(ends, tiles_of[:, 0, :], tiles_of[:, 1, :], ALU.add))
                for e in range(1, NE):
                    step(dve.tensor_tensor(ends[:, e:e + 1], ends[:, e - 1:e], ends[:, e:e + 1], ALU.add))
                number = const[:, K_ITEM:K_ALL].rearrange("p (i e) -> p i e", e=NE)
                step(dve.tensor_tensor(item_tmp, ends.unsqueeze(1).to_broadcast([P, MAX_ITEMS, NE]), number, ALU.is_le))
                step(dve.tensor_reduce(item_e, item_tmp, AX.X, ALU.add))
                step(dve.memset(item_round, 0.0))
                step(dve.tensor_tensor(item_round[:, 1:], item_e[:, 1:], item_e[:, 0:MAX_ITEMS - 1], ALU.is_equal))
                step(dve.tensor_tensor(item_hot, item_e.unsqueeze(2).to_broadcast([P, MAX_ITEMS, NE]),
                                       const[:, K_ITEM:K_ITEM + NE * NE:NE].unsqueeze(1).to_broadcast([P, MAX_ITEMS, NE]),
                                       ALU.is_equal))
                for t in range(NT):
                    for src, dst in ((slot, item_slot), (gate, item_gate)):
                        step(dve.tensor_tensor(item_tmp, item_hot, src[:, t, :].unsqueeze(1).to_broadcast([P, MAX_ITEMS, NE]),
                                               ALU.mult))
                        step(dve.tensor_reduce(dst[:, t, :], item_tmp, AX.X, ALU.add))
                    step(dve.scalar_tensor_tensor(item_slot[:, t, :], item_round, -float(P), item_slot[:, t, :],
                                                  ALU.mult, ALU.add))
                step(dve.tensor_scalar(item_expert[0:1, :], item_e[0:1, :], float(NE - 1), None, ALU.min))
                dve.tensor_copy(n_items[0:1, 0:1], ends[0:1, NE - 1:NE]).then_inc(items_known, 1)
                step(dve.memset(acc, 0.0))

            def residual():
                for t in range(NT):
                    step(dve.scalar_tensor_tensor(h[:, t, :], h[:, t, :], ALPHA, acc[:, t, :], ALU.mult, ALU.add))

            def mixer(l):
                take_turned(4 * l, actT_hi, actT_lo)
                phase()
                project(l)
                phase()
                diff_lambda(l)
                attend(l, 0)
                phase()
                prepare(l)
                phase()
                attend(l, 1)
                phase()
                diff_norm(l)
                phase()
                take_turned(4 * l + 1, brT_hi, brT_lo)
                phase()
                gates(l)
                phase()
                take_turned(4 * l + 2, actT_hi, actT_lo)
                phase()
                output(l)
                phase()
                layernorm(VAR_PREP[l] + 2, 2 * l + 1)
                phase()
                take_turned(4 * l + 3, actT_hi, actT_lo)
                phase()

            dve.engine_nop().then_inc(y_free, 1)
            dve.engine_nop().then_inc(acc_added, 1)
            dve.wait_ge(start_loaded, 64)
            layernorm(0, 0)
            phase()
            mixer(0)
            with dve.Fori(0, DENSE_PASSES) as g:
                expert(g * NX + DENSE_BASE, g, False, dve.snap(g * P))
            phase()
            residual()
            layernorm(VAR_PREP[0] + 3, 2)
            phase()
            mixer(1)
            route()
            phase()
            items = dve.value_load(n_items[0:1, 0:1], min_val=1, max_val=MAX_ITEMS)
            dve.engine_nop().then_inc(pickT_ready, 1)
            with dve.Fori(0, items) as g:
                expert(g * NX + MOE_BASE, dve.snap(g + DENSE_PASSES), True, item=g)
            phase()
            residual()
            layernorm(VAR_PREP[1] + 3, 4)
            phase()


N_PARAM = 13
VAR_PREP = [1, 5]
N_PHASES = 1 + 12 * DEPTH + 2 + 1 + 2

INS = ["x", "ln_emb_g", "ln_emb_b", "w_in", "b_gate", "mla_q_norm", "mla_kv_norm", "mla_w_uq", "mla_w_ukv",
       "gqa_q_norm", "gqa_k_norm", "diff_lambda", "diff_subln", "w_branch", "w_out", "ln1_g", "ln1_b",
       "ffn_w13", "ffn_w2", "moe_router", "moe_w13", "moe_w2", "ln2_g", "ln2_b"]


def kernel(**inputs):
    import numpy as _np
    import concourse.bacc as _bacc
    from concourse import mybir as _mybir
    from concourse.bass_utils import run_bass_kernel_spmd as _run

    nc = _bacc.Bacc("TRN2", target_bir_lowering=False, num_devices=1)
    arrays, args = {}, {}
    for name in INS + ["consts"]:
        v = constants() if name == "consts" else _np.ascontiguousarray(inputs[name])
        arrays[f"in_{name}"] = v
        args[name] = nc.dram_tensor(f"in_{name}", v.shape, _mybir.dt.from_np(v.dtype), kind="ExternalInput").ap()
    args["out"] = nc.dram_tensor("out_h", (1, S, D), _mybir.dt.from_np(_np.dtype("float32")), kind="ExternalOutput").ap()
    encoder(nc, args)
    r = _run(nc, [arrays], core_ids=[0])
    return r.results[0]["out_h"]
```

```python
import math
from contextlib import ExitStack

import numpy as np

import concourse.bass as bass
from concourse import mybir

F32 = mybir.dt.float32
F32R = mybir.dt.float32r
I32 = mybir.dt.int32
ALU = mybir.AluOpType
ACT = mybir.ActivationFunctionType
AX = mybir.AxisListType

P = 128
D = 1024
S = 256
NT = S // P
DK = D // P
DEPTH = 2
GRID_W = 64
FF = 3584
NE = 8
TOP_K = 2
MAX_ITEMS = NE + 1
NBR = 4
BW = 256
QL, KVL, MR = 192, 128, 32
HD = 64
DIL_GROUPS = ((128, 1), (512, 4), (2048, 16))
ALPHA = (2 * DEPTH) ** 0.25
LN_EPS, RMS_EPS, DIFF_EPS = 1e-5, 1e-6, 1e-5
FAR = 1e30
NOWHERE = 1e6

C_TOK = (0, 352)
C_FEAT = 352
C_DV = 1888
C_DQK = 3168
C_DIFFV = 3680
C_GATE = 3936

CH = 2048
RAW = 6
RAW_MIX = 3
SPL = 3
AHEAD = 2
FB = 512
NB = FF // FB

SLOTS = [(C_DQK, 512, True), (C_DIFFV, 256, False)] + \
        [(C_FEAT + 512 * i, 512, True) for i in range(3)] + \
        [(C_DV, 512, False), (C_DV + 512, 256, False), (C_DV + 768, 512, False), (0, 352, False)]
SLOTS_DIFF, SLOTS_DIL = 2, 7


def expert_order():
    order = []
    for j in range(NB):
        order += [("a", j, 0), ("a", j, 1), ("b", j, 0), ("b", j, 1)]
        if j:
            order += [("w", j - 1, 0), ("w", j - 1, 1)]
    return order + [("w", NB - 1, 0), ("w", NB - 1, 1)]


ORDER = expert_order()


def turned_before(i, one):
    m, j, half = ORDER[i]
    if one:
        return j - 1 if (m, half) == ("b", 0) and j else NB - 1 if (m, j, half) == ("w", NB - 2, 1) else None
    if (m, j, half) == ("a", 1, 1):
        return 0
    if i and ORDER[i - 1][0] == "w" and ORDER[i - 1][2] == 1:
        return ORDER[i - 1][1] + 1
    return None


def take_after(i, one):
    return turned_before(i + 1, one) if i + 1 < len(ORDER) else None
NX = len(ORDER)
N_PROJ = 2 * len(SLOTS)
N_GATE = 5 * NBR
N_OUT = 4
N_MIX = N_PROJ + N_GATE + N_OUT
MIX_WIDTH = [4 * SLOTS[i // 2][1] for i in range(N_PROJ)] + [CH] * (N_GATE + N_OUT)
assert NX % RAW == 0 and N_MIX % RAW == 0 and NX % SPL == 0 and N_MIX % SPL == 0


def mix_base(l):
    return l * (N_MIX + NX)


DENSE_BASE = N_MIX
MOE_BASE = mix_base(1) + N_MIX


def slot_at(i):
    return i % RAW if DENSE_BASE <= i < DENSE_BASE + NX else i % RAW_MIX


def loads_at(i):
    return sum(slot_at(q) == slot_at(i) for q in range(i + 1))


LOADS = [sum(slot_at(q) == r for q in range(MOE_BASE)) for r in range(RAW)]


def width_at(i):
    for l in range(DEPTH):
        if mix_base(l) <= i < mix_base(l) + N_MIX:
            return MIX_WIDTH[i - mix_base(l)]
    return CH


BRANCHES = (3, 1, 0, 2)
DIFF, DIL, LATE = range(3)
PARTS = [[("diff", h, t, m) for h in range(4) for t in range(NT) for m in range(2)],
         [("dil", h, t, 0) for t in range(NT) for h in range(4)],
         [("mla", h, t, 0) for h in range(4) for t in range(NT)] +
         [("gqa", h, t, 0) for h in range(4) for t in range(NT)]]
N_UNIT = sum(len(u) for u in PARTS)


def unit_base(l, part):
    return l * N_UNIT + sum(len(PARTS[q]) for q in range(part))


N_PREP = 6


def side_plan():
    plan = {}

    def put(at, pieces):
        for piece in pieces:
            while at >= 2 * N_PROJ and (at - 2 * N_PROJ) % 10 == 9:
                at += 1
            plan.setdefault(divmod(at, 2), []).append(piece)
            at += 1
        return at

    late = [("unit", LATE, i) for i in range(len(PARTS[LATE]) + 3)]
    put(3, [("lambda",)])
    at = put(4 * SLOTS_DIFF, [("unit", DIFF, i) for i in range(len(PARTS[DIFF]) + 3)] + [("diff_norm",)])
    put(at + 1, [("turn", 0)])
    at = put(4 * SLOTS_DIL, [("unit", DIL, i) for i in range(len(PARTS[DIL]) + 3)])
    at = put(at, [("prep", 0), ("turn", 1), ("prep", 1)])
    at = put(at + 1, [("prep", 2), ("prep", 3)])
    at = put(at, [("prep", 4), ("prep", 5)])
    at = put(at + 1, late[:11] + [("turn", 2)] + late[11:])
    at = put(at + 1, [("turn", 3)])
    assert at <= 2 * (N_PROJ + N_GATE) - 2
    return plan


SIDE = side_plan()
EVAC = {"dil": (1, 1), "diff": (1, 0), "mla": (0, 1), "gqa": (0, 1)}
EVACS = [(0, 0)]
for _l in range(DEPTH):
    for _u in PARTS[DIFF] + PARTS[DIL] + PARTS[LATE]:
        EVACS.append((EVACS[-1][0] + EVAC[_u[0]][0], EVACS[-1][1] + EVAC[_u[0]][1]))


def scale_of(kind):
    return {"mla": 96 ** -0.5, "gqa": HD ** -0.5}.get(kind, 1.0)


K_ID = 0
K_DIST = 128
K_MC = K_DIST + 4 * 384
K_MS = K_MC + 2 * 32
K_GC = K_MS + 2 * 32
K_GS = K_GC + 2 * 64
K_ALL = K_GS + 2 * 64
R_IOTA = 0
R_TRI = R_IOTA + S
R_ONES = R_TRI + P
R_TIE = R_ONES + P
R_ITEM = R_TIE + 64
R_ALL = R_ITEM + MAX_ITEMS * NE


def constants():
    k = np.zeros((P, K_ALL), np.float32)
    p = np.arange(P)
    k[:, K_ID:K_ID + P] = np.eye(P)
    d = np.abs(np.arange(-128, 256)[None, :] - p[:, None])
    for g, (window, dil) in enumerate(DIL_GROUPS):
        k[:, K_DIST + 384 * g:K_DIST + 384 * (g + 1)] = np.where((d <= window // 2) & (d % dil == 0), d, FAR)
    k[:, K_DIST + 384 * 3:K_DIST + 384 * 4] = d
    inv = (10000.0 ** -(np.arange(0, 32, 2, dtype=np.float32) / np.float32(32))).astype(np.float32)
    for t in range(NT):
        pos = (t * P + p).astype(np.float32)
        for c0, s0, angs in ((K_MC, K_MS, [pos]), (K_GC, K_GS, [pos // GRID_W, pos % GRID_W])):
            n = 32 * len(angs)
            for i, a in enumerate(angs):
                ang = a[:, None] * inv[None, :]
                c, s = c0 + t * n + 32 * i, s0 + t * n + 32 * i
                k[:, c:c + 16] = k[:, c + 16:c + 32] = np.cos(ang)
                k[:, s:s + 16] = -np.sin(ang)
                k[:, s + 16:s + 32] = np.sin(ang)
    return k


def router_constants():
    k = np.zeros((P, R_ALL), np.float32)
    p, e = np.arange(P), np.arange(64)
    k[:, R_IOTA:R_IOTA + S] = np.arange(S)[None, :]
    k[:, R_TRI:R_TRI + P] = p[:, None] < p[None, :]
    k[:, R_ONES:R_ONES + P] = 1.0
    k[:, R_TIE:R_TIE + 64] = (e % 8 < e // 8)[None, :]
    k[:, R_ITEM:R_ALL] = (np.arange(MAX_ITEMS * NE) // NE)[None, :]
    return k


def encoder(nc, a):
    with ExitStack() as ctx:
        def sb(name, shape, dt=F32):
            return ctx.enter_context(nc.sbuf_tensor(name, shape, dt))

        def sem(name):
            return ctx.enter_context(nc.semaphore(name))

        raw = sb("raw", [P, RAW, CH])
        w_hi = sb("w_hi", [P, SPL, CH], F32R)
        w_lo = sb("w_lo", [P, SPL, CH], F32R)
        h = sb("h", [P, NT, D])
        actT_hi = sb("actT_hi", [P, DK, S], F32R)
        actT_lo = sb("actT_lo", [P, DK, S], F32R)
        brT_hi = sb("brT_hi", [P, DK, S], F32R)
        brT_lo = sb("brT_lo", [P, DK, S], F32R)
        const = sb("const", [P, K_ALL])
        small = sb("small", [P, 2048])
        lamp = sb("lamp", [P, 4, 32])
        stat = sb("stat", [P, 96])
        n_items = sb("n_items", [1, 1], I32)
        item_expert = sb("item_expert", [1, MAX_ITEMS], I32)
        item_tiles = sb("item_tiles", [1, MAX_ITEMS], I32)
        work = sb("work", [P, 13760])
        ps = ctx.enter_context(nc.psum_tensor("banks", [P, 8, 512], F32))

        def at(off, n):
            return work[:, off:off + n]

        ident = const[:, K_ID:K_ID + P]

        featT = at(0, 4096).rearrange("p (b t) -> p b t", b=16)
        dilv = at(4096, 1536).rearrange("p (t n) -> p t n", t=NT)
        diffv = at(5632, 512).rearrange("p (t n) -> p t n", t=NT)
        gqa = at(6144, 1024).rearrange("p (t n) -> p t n", t=NT)
        cqkv = at(7168, 704).rearrange("p (t n) -> p t n", t=NT)
        y = at(7872, 2048).rearrange("p (t n) -> p t n", t=NT)
        prob = at(9920, 2304).rearrange("p (b n) -> p b n", b=3)
        probT = at(9920 + 2304, 1536).rearrange("p (b n) -> p b n", b=2)
        mqT = at(0, 1024).rearrange("p (h t) -> p h t", h=4)
        mkT = at(1024, 1024).rearrange("p (h t) -> p h t", h=4)
        gT = at(2048, 1536).rearrange("p (h t) -> p h t", h=6)
        rope_a = at(0, 768).rearrange("p (t n) -> p t n", t=NT)
        rope_m = at(768, 512).rearrange("p (t n) -> p t n", t=NT)
        mq = at(4096, 768).rearrange("p (t h d) -> p t h d", t=NT, h=4)
        mk = at(4864, 768).rearrange("p (t h d) -> p t h d", t=NT, h=4)
        mv = at(5632, 512).rearrange("p (t h d) -> p t h d", t=NT, h=4)
        cn = at(9920, 640).rearrange("p (t n) -> p t n", t=NT)
        gn = at(9920 + 640, 768).rearrange("p (t n) -> p t n", t=NT)
        gr = at(9920 + 1408, 768).rearrange("p (t n) -> p t n", t=NT)
        cT = at(9920 + 2176, 768).rearrange("p (c t) -> p c t", c=3)
        sq_c = at(9920 + 2176, 640).rearrange("p (t n) -> p t n", t=NT)
        over = raw[:, RAW_MIX:RAW, :].rearrange("p s n -> p (s n)")
        mixed = over[:, 0:2048].rearrange("p (t n) -> p t n", t=NT)
        gate_sb = over[:, 2048:4096].rearrange("p (b n) -> p b n", b=4)
        gate_pr = over[:, 4096:5120].rearrange("p (b n) -> p b n", b=2)
        gate_bias = over[:, 5120:6144]
        xT_hi, xT_lo = actT_hi, actT_lo
        hidT_hi = [brT_hi[:, 4 * t:4 * t + 4, P:S] for t in range(NT)]
        hidT_lo = [brT_lo[:, 4 * t:4 * t + 4, P:S] for t in range(NT)]
        acc = y
        silu = at(9920, 1024).rearrange("p (t n) -> p t n", t=NT)
        hid = at(10944, 1024).rearrange("p (t n) -> p t n", t=NT)
        pick = at(0, 512).rearrange("p (t s) -> p t s", t=NT)
        pick_g = at(512, 512).rearrange("p (t s) -> p t s", t=NT)
        pick_gT = at(1024, 512).rearrange("p (i t) -> p i t", i=NT)
        y_exp = at(1536, 2048).rearrange("p (t n) -> p t n", t=NT)
        route_k = at(12000, R_ALL)
        iota = at(12000 + R_IOTA, S)
        tri = at(12000 + R_TRI, P)
        ones = at(12000 + R_ONES, P)
        places = iter(range(3600, 13760))

        def table(rows, n, name="i"):
            off = next(places)
            for _ in range(rows * n - 1):
                next(places)
            return at(off, rows * n).rearrange(f"p (r {name}) -> p r {name}", r=rows)

        logit, rank, sel, expo, gate, slot = (table(NT, NE) for _ in range(6))
        cmp_a, cmp_b = table(NT, NE * NE), table(NT, NE * NE)
        item_slot, item_gate = table(NT, MAX_ITEMS), table(NT, MAX_ITEMS)
        item_hot, item_tmp = table(MAX_ITEMS, NE), table(MAX_ITEMS, NE)
        item_e, item_two, ends = table(1, MAX_ITEMS)[:, 0, :], table(1, MAX_ITEMS)[:, 0, :], table(1, NE)[:, 0, :]
        tiles_of = table(2, NE)
        r_raw = table(DK, NE)
        r_hi = sb("r_hi", [P, DK, NE], F32R)
        r_lo = sb("r_lo", [P, DK, NE], F32R)
        w_uq0, w_uq1 = small[:, 0:384], small[0:64, 384:768]
        w_ukv = small[:, 768:1280]
        g_q, g_kv = small[:, 1280:1472], small[:, 1472:1600]
        g_gqa, g_sub = small[:, 1600:1984], small[:, 1984:2048]

        chunk_loaded = [sem(f"chunk_loaded{i}") for i in range(RAW)]
        hi_done, lo_done = sem("hi_done"), sem("lo_done")
        chunk_used = sem("chunk_used")
        phase_done = sem("phase_done")
        x_loaded, start_loaded, gains_loaded = sem("x_loaded"), sem("start_loaded"), sem("gains_loaded")
        ident_loaded, const_loaded = sem("ident_loaded"), sem("const_loaded")
        params_loaded, bias_loaded = sem("params_loaded"), sem("bias_loaded")
        router_loaded, stored = sem("router_loaded"), sem("stored")
        dve_step = sem("dve_step")
        turned4, turn_hi = sem("turned4"), sem("turn_hi")
        proj_used = [sem("proj_used_act"), sem("proj_used_dve")]
        var_ready, std_ready = sem("var_ready"), sem("std_ready")
        lam_sum, lam_exp = sem("lam_sum"), sem("lam_exp")
        scores, negmax, exps = sem("scores"), sem("negmax"), sem("exps")
        prob_turned, pv_done, out_taken = sem("prob_turned"), sem("pv_done"), sem("out_taken")
        branch_turned, branch_hi, branch_lo = sem("branch_turned"), sem("branch_hi"), sem("branch_lo")
        diff_normed = sem("diff_normed")
        turned_taken = [sem("turned_taken_act"), sem("turned_taken_dve")]
        prep_dve, prep_act, prep_pe = sem("prep_dve"), sem("prep_act"), sem("prep_pe")
        gate_biased, gate_open, branch_used = sem("gate_biased"), sem("gate_open"), sem("branch_used")
        branch_made = sem("branch_made")
        turn_lo, tile_made = sem("turn_lo"), sem("tile_made")
        silu_done, hid_made, hid_turned = sem("silu_done"), sem("hid_made"), sem("hid_turned")
        hidT_hi_done, hidT_lo_done = sem("hidT_hi_done"), sem("hidT_lo_done")
        x_hi_done, x_lo_done = sem("x_hi_done"), sem("x_lo_done")
        y_free, acc_added = sem("y_free"), sem("acc_added")
        picked, gathered, pick_turned, pickT_ready = sem("picked"), sem("gathered"), sem("pick_turned"), sem("pickT_ready")
        scattered = sem("scattered")
        gathered2, x2_hi_done, x2_lo_done = sem("gathered2"), sem("x2_hi_done"), sem("x2_lo_done")
        ln_tile = sem("ln_tile")
        router_hi, router_lo, logits_done, logits_copied = sem("router_hi"), sem("router_lo"), sem("logits_done"), sem("logits_copied")
        expo_in, expo_out, sel_done, counted, items_known = sem("expo_in"), sem("expo_out"), sem("sel_done"), sem("counted"), sem("items_known")

        block = ctx.enter_context(nc.Block())

        def bank(i):
            return ps[:, i, :]

        def token_dst(c0, n, t):
            if c0 == 0:
                return cqkv[:, t, :]
            if c0 < C_DV + 768:
                return dilv[:, t, c0 - C_DV:c0 - C_DV + n]
            return gqa[:, t, :] if c0 == C_DV + 768 else diffv[:, t, :]

        def turns_before(l, part, i):
            if part == DIL and i < 2:
                return 4 * l
            return 4 * l + (0, 1, 3 if i >= 11 else 2)[part]

        class Steps:

            def __init__(self, eng, s, base=0):
                self.eng, self.s, self.base, self.n = eng, s, base, 0

            def __call__(self, ins):
                self.n += 1
                ins.then_inc(self.s, 1)
                self.eng.wait_ge(self.s, self.base + self.n)

        class Phases:

            def __init__(self, eng):
                self.eng, self.n = eng, 0

            def __call__(self):
                self.n += 1
                self.eng.drain().then_inc(phase_done, 1)
                self.eng.wait_ge(phase_done, 3 * self.n)

        @block.sync
        def _(sp):
            x = a["x"][0].rearrange("(t p) d -> t p d", p=P)
            for t in range(NT):
                sp.dma_start(h[:, t, :], x[t]).then_inc(x_loaded, 16)
            sp.dma_start(ident, a["consts"][:, K_ID:K_ID + P]).then_inc(ident_loaded, 16)
            sp.dma_start(small[:, 0:D], a["ln_emb_g"].partition_broadcast(P)).then_inc(start_loaded, 16)
            sp.dma_start(small[:, D:2 * D], a["ln_emb_b"].partition_broadcast(P)).then_inc(start_loaded, 16)

            def load(pos, i, src, width, k):
                static = isinstance(pos, int)
                s = slot_at(pos + i) if static and pos + i < MOE_BASE else i % RAW
                if not static or pos + i >= MOE_BASE:
                    sp.wait_ge(lo_done, pos + (i - RAW + 1))
                elif pos + i >= RAW_MIX:
                    last = [q for q in range(pos + i) if slot_at(q) == s]
                    if last:
                        sp.wait_ge(lo_done, last[-1] + 1)
                    if DENSE_BASE <= pos + i < DENSE_BASE + RAW and s >= RAW_MIX:
                        sp.wait_ge(turned4, 4 * 2)
                dst = raw[:, s, 0:width].rearrange("p (k n) -> p k n", k=k)
                sp.dma_start(dst, src).then_inc(chunk_loaded[s], 16)

            def mixer(l):
                base = mix_base(l)
                w_in = a["w_in"][l].rearrange("(k p) n -> p k n", p=P)
                w_br = a["w_branch"][l].rearrange("n (k p) d -> n p k d", p=P)
                w_out = a["w_out"][l].rearrange("(k p) n -> p k n", p=P)
                i = 0
                for c0, n, _feat in SLOTS:
                    for half in range(2):
                        load(base, i, w_in[:, 4 * half:4 * half + 4, c0:c0 + n], 4 * n, 4)
                        i += 1
                        if i == 3:
                            load_params(l)
                for n in BRANCHES:
                    for c in range(2):
                        for half in range(2):
                            c0 = C_GATE + n * D + c * 512
                            load(base, i, w_in[:, 4 * half:4 * half + 4, c0:c0 + 512], CH, 4)
                            i += 1
                    load(base, i, w_br[n], CH, 2)
                    i += 1
                for q in range(N_OUT):
                    load(base, i, w_out[:, 2 * q:2 * q + 2, :], CH, 2)
                    i += 1

            def load_params(l):
                if l == 0:
                    rest = slice(K_ID + P, K_ALL)
                    sp.dma_start(const[:, rest], a["consts"][:, rest]).then_inc(const_loaded, 16)
                sp.wait_ge(ln_tile, NT * (2 * l + 1))
                q = a["mla_w_uq"][l]
                for dst, src in ((lamp[:, :, :], a["diff_lambda"][l].partition_broadcast(P)),
                                 (g_sub, a["diff_subln"][l].partition_broadcast(P)),
                                 (w_uq0, q[0:P, :]), (w_uq1, q[P:QL, :]), (w_ukv, a["mla_w_ukv"][l]),
                                 (g_q, a["mla_q_norm"][l].partition_broadcast(P)),
                                 (g_kv, a["mla_kv_norm"][l].partition_broadcast(P))):
                    sp.dma_start(dst, src).then_inc(params_loaded, 16)
                for hd in range(6):
                    g = a["gqa_q_norm" if hd < 4 else "gqa_k_norm"][l].partition_broadcast(P)
                    sp.dma_start(g_gqa[:, hd * HD:(hd + 1) * HD], g).then_inc(params_loaded, 16)
                if l:
                    sp.wait_ge(lo_done, mix_base(l))
                sp.dma_start(gate_bias, a["b_gate"][l][BRANCHES[0]].partition_broadcast(P)).then_inc(bias_loaded, 16)

            def expert(pos, w13, w2):
                for i, (m, j, half) in enumerate(ORDER):
                    if m == "w":
                        load(pos, i, w2[:, 4 * j + 2 * half:4 * j + 2 * half + 2, :], CH, 2)
                    else:
                        c0 = j * FB + (FF if m == "b" else 0)
                        load(pos, i, w13[:, 4 * half:4 * half + 4, c0:c0 + FB], CH, 4)

            mixer(0)
            expert(DENSE_BASE, a["ffn_w13"][0].rearrange("(k p) n -> p k n", p=P),
                   a["ffn_w2"][0].rearrange("(k p) n -> p k n", p=P))
            mixer(1)
            sp.wait_ge(items_known, 1)
            items = sp.value_load(n_items[0:1, 0:1], min_val=1, max_val=NE)
            w13 = a["moe_w13"][0].rearrange("e (k p) n -> e p k n", p=P)
            w2 = a["moe_w2"][0].rearrange("e (k p) n -> e p k n", p=P)
            with sp.Fori(0, items) as g:
                e = sp.value_load(item_expert[0:1, bass.ds(g, 1)], min_val=0, max_val=NE - 1)
                expert(g * NX + MOE_BASE, w13[bass.ds(e, 1)].squeeze(0), w2[bass.ds(e, 1)].squeeze(0))
            past = sp.snap(items * NX + MOE_BASE)
            for i in range(AHEAD):
                load(past, i, w13[0][:, 4 * i:4 * i + 4, 0:FB], CH, 4)
            out = a["out"][0].rearrange("(t p) d -> t p d", p=P)
            for t in range(NT):
                sp.wait_ge(ln_tile, NT * 2 * DEPTH + t + 1)
                sp.dma_start(out[t], h[:, t, :]).then_inc(stored, 16)
            sp.wait_ge(stored, 16 * NT)

        @block.tensor
        def _(pe):
            phase = Phases(pe)

            def three(out, l_hi, l_lo, r_hi_, r_lo_, start, stop):
                pe.matmul(out, l_hi, r_hi_, start=start, stop=False, skip_group_check=True)
                pe.matmul(out, l_hi, r_lo_, start=False, stop=False, skip_group_check=True)
                return pe.matmul(out, l_lo, r_hi_, start=False, stop=stop, skip_group_check=True)

            def chunk(pos, i):
                pe.wait_ge(lo_done, pos + (i + 1))
                return w_hi[:, i % SPL, :], w_lo[:, i % SPL, :]

            def turn(src, after):
                for b in range(4):
                    t, half = b // 2, b % 2
                    pe.wait_ge(ln_tile, NT * after + t + 1)
                    for i in range(4):
                        c = (4 * half + i) * P
                        mm = pe.transpose(bank(b)[:, i * P:(i + 1) * P], src[:, t, c:c + P], ident)
                    mm.then_inc(turned4, 1)

            def turn_mixed(l):
                pe.wait_ge(exps, (l + 1) * N_UNIT)
                for b in range(4):
                    c, t = b // 2, b % 2
                    pe.wait_ge(branch_used, 16 * l + 12 + b + 1)
                    for i in range(4):
                        x = c * 512 + i * P
                        mm = pe.transpose(bank(4 + b)[:, i * P:(i + 1) * P], mixed[:, t, x:x + P], ident)
                    mm.then_inc(turned4, 1)

            def side(l, i, half):
                for piece in SIDE.get((i, half), []):
                    if piece[0] == "unit":
                        unit(l, piece[1], piece[2])
                    elif piece[0] == "prep":
                        prepare(l, piece[1])
                    elif piece[0] == "turn":
                        turn_branch(l, piece[1])

            def project(l):
                base = mix_base(l)
                for s, (c0, n, feat) in enumerate(SLOTS):
                    b0 = 2 * (s % 2)
                    if s >= 2:
                        for q in range(2):
                            pe.wait_ge(proj_used[q], l * len(SLOTS) + s - 1)
                    for half in range(2):
                        hi, lo = chunk(base, 2 * s + half)
                        for o in range(4 if feat else NT):
                            for kk in range(4):
                                k, first, last = 4 * half + kk, half == 0 and kk == 0, half == 1 and kk == 3
                                if feat:
                                    w = slice(kk * n + o * P, kk * n + (o + 1) * P)
                                    out = bank(b0 + o // 2)[:, (o % 2) * S:(o % 2 + 1) * S]
                                    mm = three(out, hi[:, w], lo[:, w], actT_hi[:, k, :], actT_lo[:, k, :],
                                               first and o % 2 == 0, last)
                                else:
                                    w = slice(kk * n, (kk + 1) * n)
                                    x = slice(o * P, (o + 1) * P)
                                    mm = three(bank(b0 + o)[:, 0:n], actT_hi[:, k, x], actT_lo[:, k, x],
                                               hi[:, w], lo[:, w], first, last)
                            if o == (1 if feat else 0):
                                side(l, 2 * s + half, 0)
                        mm.then_inc(chunk_used, 1)
                        side(l, 2 * s + half, 1)

            def turn_branch(l, q):
                n = BRANCHES[q]
                units_done = unit_base(l, (DIFF, DIL, LATE, LATE)[q]) + (16, 8, 8, 16)[q]
                pe.wait_ge(out_taken, units_done)
                if q == 0:
                    pe.wait_ge(diff_normed, l + 1)
                for e in range(2):
                    if EVACS[units_done][e]:
                        pe.wait_ge(turned_taken[e], EVACS[units_done][e])
                for k in range(2):
                    for t in range(NT):
                        mm = pe.transpose(bank(6)[:, (2 * k + t) * P:(2 * k + t + 1) * P],
                                          y[:, t, n * BW + k * P:n * BW + (k + 1) * P], ident)
                mm.then_inc(branch_turned, 1)

            def operands(kind, hd, t, m):
                q = slice(t * P, (t + 1) * P)
                if kind == "dil":
                    out = []
                    for g in range(3):
                        n = g * 4 + hd
                        r = slice(64 * (n % 2), 64 * (n % 2) + 64)
                        out.append((featT[r, n // 2, q], featT[r, 6 + n // 2, :],
                                    [dilv[:, kt, n * HD:(n + 1) * HD] for kt in range(NT)]))
                    return out
                if kind == "diff":
                    r0 = (hd % 2) * 64 + m * 32
                    return [(featT[r0:r0 + 32, 12 + hd // 2, q], featT[r0:r0 + 32, 14 + hd // 2, :],
                             [diffv[:, kt, hd * HD:(hd + 1) * HD] for kt in range(NT)])]
                if kind == "mla":
                    return [(mqT[0:96, hd, q], mkT[0:96, hd, :], [mv[:, kt, hd, :] for kt in range(NT)])]
                kv = hd // 2
                return [(gT[0:64, hd, q], gT[0:64, 4 + kv, :],
                         [gqa[:, kt, 384 + kv * HD:384 + (kv + 1) * HD] for kt in range(NT)])]

            def unit(l, part, i):
                us, base = PARTS[part], unit_base(l, part)
                turned = i - 2 if 2 <= i < len(us) + 2 else None

                if turned is not None:
                    u, kind = base + turned, us[turned][0]
                    pe.wait_ge(exps, u + 1)
                    for e in range(2):
                        if EVACS[u][e]:
                            pe.wait_ge(turned_taken[e], EVACS[u][e])
                    if turns_before(l, part, i):
                        pe.wait_ge(branch_lo, turns_before(l, part, i))
                    if kind == "dil" and i >= 4:
                        pe.wait_ge(out_taken, base + i - 3)
                    for b in range(6 if kind == "dil" else 2):
                        dst = bank(6)[:, b * P:(b + 1) * P] if b < 4 else bank(7)[:, (b - 2) * P:(b - 1) * P]
                        mm = pe.transpose(dst, prob[:, turned % 3, b * P:(b + 1) * P], ident)
                    mm.then_inc(prob_turned, 1)
                if i < len(us):
                    u, kind = base + i, us[i][0]
                    if i == 0:
                        if part == LATE:
                            pe.wait_ge(prep_act, 8 * (l + 1))
                            pe.wait_ge(prep_dve, 5 * (l + 1))
                        else:
                            for e in range(2):
                                pe.wait_ge(proj_used[e], l * len(SLOTS) + (SLOTS_DIFF if part == DIFF else SLOTS_DIL))
                    if part == LATE and i >= 2:
                        pe.wait_ge(exps, u - 1)
                    elif part == DIFF and i >= 2:
                        pe.wait_ge(negmax, u - 1)
                    elif part != LATE and u:
                        pe.wait_ge(negmax, u)
                    for g, (q, k, _v) in enumerate(operands(*us[i])):
                        b = 4 + g // 2 if kind == "dil" else 4 + i % 2
                        mm = pe.matmul(bank(b)[:, (g % 2) * S:(g % 2 + 1) * S], q, k, start=True, stop=True)
                    mm.then_inc(scores, 1)
                if i >= 3:
                    j = i - 3
                    u, kind = base + j, us[j][0]
                    for e in range(2):
                        if EVAC[kind][e]:
                            pe.wait_ge(turned_taken[e], EVACS[u + 1][e])
                    if u:
                        pe.wait_ge(out_taken, u)
                    vs = [v for (_q, _k, vv) in operands(*us[j]) for v in vv]
                    for b, v in enumerate(vs):
                        mm = pe.matmul(bank(7)[:, 0:HD], probT[:, j % 2, b * P:(b + 1) * P], v,
                                       start=(b == 0), stop=(b == len(vs) - 1))
                    mm.then_inc(pv_done, 1)

            def prepare(l, stage):
                if stage == 1:
                    pe.wait_ge(prep_dve, 5 * l + 1)
                    pe.wait_ge(exps, unit_base(l, LATE))
                    for t in range(NT):
                        pe.transpose(bank(4 + t)[:, 0:P], cn[:, t, 0:P], ident)
                        pe.transpose(bank(4 + t)[0:64, P:2 * P], cn[:, t, P:QL], ident)
                        pe.transpose(bank(4 + t)[:, 2 * P:3 * P], cn[:, t, QL:QL + KVL], ident).then_inc(prep_pe, 1)
                if stage == 2:
                    pe.wait_ge(params_loaded, 16 * N_PARAM * (l + 1))
                    pe.wait_ge(branch_lo, 4 * l + 2)
                    for t in range(NT):
                        x = slice(t * P, (t + 1) * P)
                        pe.wait_ge(prep_act, 8 * l + t + 1)
                        pe.matmul(bank(4 + t)[:, 0:384], cT[:, 0, x], w_uq0, start=True, stop=False)
                        pe.matmul(bank(4 + t)[:, 0:384], cT[0:64, 1, x], w_uq1, start=False, stop=True)
                        pe.matmul(bank(6 + t)[:, :], cT[:, 2, x], w_ukv, start=True, stop=True).then_inc(prep_pe, 1)
                if stage == 4:
                    pe.wait_ge(prep_dve, 5 * l + 3)
                    pe.wait_ge(prep_act, 8 * l + 4)
                    for b in range(2):
                        for i in range(4):
                            hd, t = 2 * b + i // 2, i % 2
                            mm = pe.transpose(bank(6 + b)[0:64, i * P:(i + 1) * P], gr[:, t, hd * HD:(hd + 1) * HD], ident)
                        mm.then_inc(prep_pe, 1)
                    for i in range(4):
                        hd, t = 4 + i // 2, i % 2
                        mm = pe.transpose(bank(4)[0:64, i * P:(i + 1) * P], gr[:, t, hd * HD:(hd + 1) * HD], ident)
                    mm.then_inc(prep_pe, 1)
                if stage == 5:
                    for n, (src, hds, b) in enumerate(((mq, 0, 5), (mq, 2, 6), (mk, 0, 7), (mk, 2, 4))):
                        if n in (1, 2):
                            pe.wait_ge(prep_act, 8 * l + 4 + n)
                        if n == 3:
                            pe.wait_ge(prep_dve, 5 * l + 4)
                        for i in range(4):
                            hd, t = hds + i // 2, i % 2
                            mm = pe.transpose(bank(b)[0:96, i * P:(i + 1) * P], src[:, t, hd, :], ident)
                        mm.then_inc(prep_pe, 1)

            def gates(l):
                base = mix_base(l)
                for q, n in enumerate(BRANCHES):
                    i0 = N_PROJ + 5 * q
                    for c in range(2):
                        for half in range(2):
                            hi, lo = chunk(base, i0 + 2 * c + half)
                            if half == 0 and q:
                                pe.wait_ge(branch_used, 16 * l + 4 * (q - 1) + 2 * c + 2)
                            if half == 0 and q == 0:
                                for e in range(2):
                                    pe.wait_ge(proj_used[e], (l + 1) * len(SLOTS))
                            for t in range(NT):
                                x = slice(t * P, (t + 1) * P)
                                for kk in range(4):
                                    k, w = 4 * half + kk, slice(kk * 512, (kk + 1) * 512)
                                    mm = three(bank(2 * c + t), actT_hi[:, k, x], actT_lo[:, k, x],
                                               hi[:, w], lo[:, w], k == 0, k == DK - 1)
                                if t == 0:
                                    side(l, i0 + 2 * c + half, 0)
                            mm.then_inc(chunk_used, 1)
                            side(l, i0 + 2 * c + half, 1)
                    hi, lo = chunk(base, i0 + 4)
                    pe.wait_ge(branch_lo, 4 * l + q + 1)
                    for c in range(2):
                        for t in range(NT):
                            pe.wait_ge(gate_biased, 16 * l + 4 * q + 2 * c + t + 1)
                            x = slice(t * P, (t + 1) * P)
                            for kk in range(2):
                                w = slice(kk * D + c * 512, kk * D + (c + 1) * 512)
                                mm = three(bank(2 * c + t), brT_hi[:, 2 * n + kk, x], brT_lo[:, 2 * n + kk, x],
                                           hi[:, w], lo[:, w], kk == 0, kk == 1)
                            if (c, t) != (1, 1):
                                mm.then_inc(branch_made, 1)
                        if c == 0:
                            side(l, i0 + 4, 0)
                    mm.then_inc(chunk_used, 1)
                    side(l, i0 + 4, 1)

            def output(l):
                base = mix_base(l)
                for q in range(N_OUT):
                    if q % 2 == 0:
                        pe.wait_ge(turn_lo, 4 * (3 * l + 1) + q + 2)
                    hi, lo = chunk(base, N_PROJ + N_GATE + q)
                    for t in range(NT):
                        x = slice(t * P, (t + 1) * P)
                        for kk in range(2):
                            k = 2 * q + kk
                            for c in range(2):
                                w = slice(kk * D + c * 512, kk * D + (c + 1) * 512)
                                mm = three(bank(2 * t + c), actT_hi[:, k, x], actT_lo[:, k, x], hi[:, w], lo[:, w],
                                           k == 0, k == DK - 1)
                        if q == N_OUT - 1 and t == 0:
                            mm.then_inc(tile_made, 1)
                    mm.then_inc(chunk_used, 1)

            def gather(item, tile, banks, done):
                for r in range(2):
                    for i in range(4):
                        d = (4 * r + i) * P
                        for t in range(NT):
                            mm = pe.matmul(bank(banks + r)[:, i * P:(i + 1) * P], h[:, t, d:d + P],
                                           pick[:, t, tile * P:(tile + 1) * P], start=(t == 0), stop=(t == 1))
                    mm.then_inc(done, 1)

            def turn_picks(tiles, b):
                for i in range(tiles):
                    for t in range(NT):
                        mm = pe.transpose(bank(b)[:, (2 * i + t) * P:(2 * i + t + 1) * P],
                                          pick_g[:, t, i * P:(i + 1) * P], ident)
                mm.then_inc(pick_turned, 1)

            def expert(pos, g, tiles, item=None):
                one, moe = tiles == 1, item is not None
                if moe and one:
                    pe.nop().then_inc(gathered2, 2)
                if moe and not one:
                    gather(item, 1, 6, gathered2)
                    pe.wait_ge(acc_added, 4 * item + 1)
                    turn_picks(2, 3)
                for i, (m, j, half) in enumerate(ORDER):
                    jt = turned_before(i, one)
                    if jt is not None:
                        pe.wait_ge(hid_made, g * NB + (jt + 1))
                        for t in range(tiles):
                            for q in range(4):
                                mm = pe.transpose(bank(7 if one else 2 + t)[:, q * P:(q + 1) * P],
                                                  hid[:, t, q * P:(q + 1) * P], ident)
                        mm.then_inc(hid_turned, 1)
                        if moe and one and jt == 1:
                            turn_picks(1, 6)
                    hi, lo = chunk(pos, i)
                    if moe and i == 0:
                        pe.wait_ge(x_lo_done, 2 * item + 2)
                        if not one:
                            pe.wait_ge(x2_lo_done, 2 * item + 2)
                    if moe and (m, j, half) == ("b", 0, 0):
                        pe.wait_ge(acc_added, 4 * item + 1)
                    if m in "ab":
                        if one and j >= 2 and half == 0:
                            pe.wait_ge(hid_made, g * NB + (j - 1))
                        if not one and j and half == 0:
                            if m == "a":
                                pe.wait_ge(silu_done, g * NB + j)
                            else:
                                pe.wait_ge(hidT_lo_done, g * NB + j)
                        for t in range(tiles):
                            b = (j % 2 if one else t) + (2 if m == "b" else 0)
                            x = slice(t * P, (t + 1) * P)
                            for kk in range(4):
                                k, w = 4 * half + kk, slice(kk * FB, (kk + 1) * FB)
                                mm = three(bank(b), xT_hi[:, k, x], xT_lo[:, k, x], hi[:, w], lo[:, w],
                                           k == 0, k == DK - 1)
                    else:
                        if half == 0:
                            pe.wait_ge(hidT_lo_done, g * NB + (j + 1))
                        for t in range(tiles):
                            for kk in range(2):
                                for c in range(2):
                                    w = slice(kk * D + c * 512, kk * D + (c + 1) * 512)
                                    o = j % 2 if one else t
                                    mm = three(bank(4 + 2 * t + c), hidT_hi[o][:, 2 * half + kk, :],
                                               hidT_lo[o][:, 2 * half + kk, :], hi[:, w], lo[:, w],
                                               (j, half, kk) == (0, 0, 0), (j, half, kk) == (NB - 1, 1, 1))
                    mm.then_inc(chunk_used, 1)
                if moe:
                    pe.wait_ge(picked, item + 2)
                    gather(item, 0, 0, gathered)
                    pe.wait_ge(y_free, 2 * item + 2)
                    pe.wait_ge(pickT_ready, item + 1)
                    for t in range(NT):
                        for c in range(2):
                            for i in range(tiles):
                                mm = pe.matmul(bank(2 + 2 * t + c), pick_gT[:, i, t * P:(t + 1) * P],
                                               y_exp[:, i, c * 512:(c + 1) * 512], start=(i == 0), stop=(i == tiles - 1))
                            mm.then_inc(scattered, 1)

            def route():
                pe.wait_ge(router_lo, 1)
                for t in range(NT):
                    x = slice(t * P, (t + 1) * P)
                    for k in range(DK):
                        mm = three(bank(t)[:, 0:NE], actT_hi[:, k, x], actT_lo[:, k, x], r_hi[:, k, :], r_lo[:, k, :],
                                   k == 0, k == DK - 1)
                mm.then_inc(logits_done, 1)
                pe.wait_ge(sel_done, 1)
                pe.matmul(bank(2)[:, 0:NE], tri, sel[:, 0, :], start=True, stop=True)
                pe.matmul(bank(3)[:, 0:NE], ones, sel[:, 0, :], start=True, stop=False)
                pe.matmul(bank(3)[:, 0:NE], tri, sel[:, 1, :], start=False, stop=True)
                pe.matmul(bank(4)[:, 0:NE], ones, sel[:, 0, :], start=True, stop=False)
                pe.matmul(bank(4)[:, 0:NE], ones, sel[:, 1, :], start=False, stop=True).then_inc(counted, 1)

            def mixer(l):
                turn(h, 2 * l)
                phase()
                project(l)
                gates(l)
                turn_mixed(l)
                output(l)
                phase()
                turn(h, 2 * l + 1)
                phase()

            pe.wait_ge(ident_loaded, 16)
            mixer(0)
            expert(DENSE_BASE, 0, 2)
            phase()
            mixer(1)
            route()
            phase()
            pe.wait_ge(items_known, 1)
            items = pe.value_load(n_items[0:1, 0:1], min_val=1, max_val=NE)
            pe.wait_ge(picked, 1)
            gather(0, 0, 0, gathered)
            with pe.Fori(0, items) as item:
                two = pe.value_load(item_tiles[0:1, bass.ds(item, 1)], min_val=0, max_val=1)
                pos, g = pe.snap(item * NX + MOE_BASE), pe.snap(item + 1)
                with pe.If(two == 1):
                    expert(pos, g, 2, item)
                with pe.Else():
                    expert(pos, g, 1, item)
            phase()

        @block.scalar
        def _(act):
            phase = Phases(act)

            def split(pos, i, width=CH):
                q = i % SPL
                if isinstance(pos, int) and pos + i < MOE_BASE:
                    s = slot_at(pos + i)
                    act.wait_ge(chunk_loaded[s], 16 * loads_at(pos + i))
                else:
                    s = i % RAW
                    act.wait_ge(chunk_loaded[s], item_loads[0] + 16 * (LOADS[s] + i // RAW + 1))
                if not (isinstance(pos, int) and pos + i < SPL):
                    act.wait_ge(chunk_used, pos + (i - SPL + 1))
                act.activation(w_hi[:, q, 0:width], raw[:, s, 0:width], ACT.Copy).then_inc(hi_done, 1)

            item_loads = [0]

            def take_turned(n, dst_hi, first=0):
                for b in range(4):
                    t, half = (b % 2, b // 2) if first else (b // 2, b % 2)
                    act.wait_ge(turned4, 4 * n + b + 1)
                    act.activation(dst_hi[:, 4 * half:4 * half + 4, t * P:(t + 1) * P],
                                   bank(first + b).rearrange("p (k t) -> p k t", k=4), ACT.Copy).then_inc(turn_hi, 1)

            def load_gains(g, b):
                act.dma_start(small[:, 0:D], g.partition_broadcast(P)).then_inc(gains_loaded, 16)
                act.dma_start(small[:, D:2 * D], b.partition_broadcast(P)).then_inc(gains_loaded, 16)

            def norm_std(n):
                act.activation(stat[:, 94:95], ident[:, 0:1], ACT.Sqrt)
                act.wait_ge(var_ready, n + 1)
                act.activation(stat[:, 16:32], stat[:, 0:16], ACT.Sqrt).then_inc(std_ready, 1)

            def ahead(i):
                if i + AHEAD < MOE_BASE:
                    split(0, i + AHEAD, width_at(i + AHEAD))

            def side(l, i, half):
                for piece in SIDE.get((i, half), []):
                    if piece[0] == "unit":
                        unit(l, piece[1], piece[2])
                    elif piece[0] == "prep":
                        prepare(l, piece[1])
                    elif piece[0] == "turn":
                        n = BRANCHES[piece[1]]
                        act.wait_ge(branch_turned, 4 * l + piece[1] + 1)
                        act.activation(brT_hi[:, 2 * n:2 * n + 2, :], bank(6).rearrange("p (k t) -> p k t", k=2),
                                       ACT.Copy).then_inc(branch_hi, 1)
                    elif piece[0] == "diff_norm":
                        norm_std(VAR_PREP[l])
                    elif piece[0] == "lambda":
                        act.wait_ge(lam_sum, l + 1)
                        act.activation(stat[:, 50:52], stat[:, 48:50], ACT.Exp).then_inc(lam_exp, 1)

            def project(l):
                base = mix_base(l)
                for s, (c0, n, feat) in enumerate(SLOTS):
                    for half in range(2):
                        ahead(base + 2 * s + half)
                        side(l, 2 * s + half, 0)
                        if half:
                            b0 = 2 * (s % 2)
                            act.wait_ge(chunk_used, base + 2 * s + 2)
                            if feat:
                                f = (c0 - C_FEAT) // P if c0 < C_DV else 12
                                scale = HD ** -0.5 if f < 6 else 32 ** -0.5 if f == 12 else 1.0
                                act.activation(featT[:, f:f + 2, :], bank(b0).rearrange("p (b t) -> p b t", b=2),
                                               ACT.Copy, scale=scale).then_inc(proj_used[0], 1)
                            else:
                                act.activation(token_dst(c0, n, 0), bank(b0)[:, 0:n], ACT.Copy).then_inc(proj_used[0], 1)
                        side(l, 2 * s + half, 1)

            def unit(l, part, i):
                us, base = PARTS[part], unit_base(l, part)
                if i < len(us):
                    u, kind = base + i, us[i][0]
                    n = 3 * S if kind == "dil" else S
                    act.wait_ge(negmax, u + 1)
                    if part == LATE and i >= 3:
                        act.wait_ge(prob_turned, u - 2)
                    src = bank(4 + i % 2)[:, 0:n] if part == LATE else prob[:, i % 3, 0:n]
                    act.activation(prob[:, i % 3, 0:n], src, ACT.Exp, bias=stat[:, 32 + i % 2:33 + i % 2],
                                   scale=scale_of(kind), accum_out=stat[:, 36 + i % 4:37 + i % 4]).then_inc(exps, 1)
                if 2 <= i < len(us) + 2 and EVAC[us[i - 2][0]][0]:
                    j = i - 2
                    u, kind = base + j, us[j][0]
                    act.wait_ge(prob_turned, u + 1)
                    if j >= 2:
                        act.wait_ge(pv_done, u - 1)
                    n = 512 if kind == "dil" else S
                    act.activation(probT[:, j % 2, 0:n], bank(6)[:, 0:n], ACT.Copy).then_inc(turned_taken[0], 1)

            def prepare(l, stage):
                if stage == 0:
                    norm_std(VAR_PREP[l] + 1)
                if stage == 1:
                    for t in range(NT):
                        act.wait_ge(prep_pe, 11 * l + t + 1)
                        x = slice(t * P, (t + 1) * P)
                        act.activation(cT[:, 0, x], bank(4 + t)[:, 0:P], ACT.Copy)
                        act.activation(cT[0:64, 1, x], bank(4 + t)[0:64, P:2 * P], ACT.Copy)
                        act.activation(cT[:, 2, x], bank(4 + t)[:, 2 * P:3 * P], ACT.Copy).then_inc(prep_act, 1)
                if stage == 2:
                    for t in range(NT):
                        act.wait_ge(prep_pe, 11 * l + 2 + t + 1)
                        q = bank(4 + t)[:, 0:384].rearrange("p (h d) -> p h d", h=4)
                        kv = bank(6 + t).rearrange("p (h d) -> p h d", h=4)
                        act.activation(mq[:, t, :, 0:64], q[:, :, 0:64], ACT.Copy)
                        act.activation(mk[:, t, :, 0:64], kv[:, :, 0:64], ACT.Copy)
                        act.activation(mv[:, t, :, :], kv[:, :, 64:128], ACT.Copy).then_inc(prep_act, 1)
                if stage == 4:
                    for b in range(2):
                        act.wait_ge(prep_pe, 11 * l + 4 + b + 1)
                        act.activation(gT[0:64, 2 * b:2 * b + 2, :], bank(6 + b)[0:64].rearrange("p (h t) -> p h t", h=2),
                                       ACT.Copy).then_inc(prep_act, 1)
                if stage == 5:
                    for b in range(2):
                        act.wait_ge(prep_pe, 11 * l + 7 + b + 1)
                        act.activation(mqT[0:96, 2 * b:2 * b + 2, :], bank(5 + b)[0:96].rearrange("p (h t) -> p h t", h=2),
                                       ACT.Copy).then_inc(prep_act, 1)

            def gates(l):
                base = mix_base(l)
                for i in range(N_GATE):
                    ahead(base + N_PROJ + i)
                    side(l, N_PROJ + i, 0)
                    q, c = i // 5, (i % 5) // 2
                    if i % 5 in (1, 3):
                        for t in range(NT):
                            act.wait_ge(gate_biased, 16 * l + 4 * q + 2 * c + t + 1)
                            s = gate_sb[:, 2 * c + t, :]
                            act.activation(s, s, ACT.Sigmoid).then_inc(gate_open, 1)
                        if c == 1 and q + 1 < NBR:
                            load_bias(l, q + 1)
                    side(l, N_PROJ + i, 1)

            def load_bias(l, q):
                act.dma_start(gate_bias, a["b_gate"][l][BRANCHES[q]].partition_broadcast(P)).then_inc(bias_loaded, 16)

            def output(l):
                for q in range(N_OUT):
                    ahead(mix_base(l) + N_PROJ + N_GATE + q)

            def take_x(item, tile, banks, at_, ready):
                for r in range(2):
                    act.wait_ge(at_, 2 * item + (r + 1))
                    act.activation(xT_hi[:, 4 * r:4 * r + 4, tile * P:(tile + 1) * P],
                                   bank(banks + r).rearrange("p (k s) -> p k s", k=4), ACT.Copy).then_inc(ready, 1)

            def expert(pos, g, tiles, item=None):
                one, moe = tiles == 1, item is not None
                if moe and one:
                    act.nop().then_inc(x2_hi_done, 2)
                if moe and not one:
                    take_x(item, 1, 6, gathered2, x2_hi_done)
                    act.wait_ge(pick_turned, item + 1)
                    act.activation(pick_gT, bank(3).rearrange("p (i t) -> p i t", i=2), ACT.Copy).then_inc(pickT_ready, 1)
                for i, (m, j, half) in enumerate(ORDER):
                    if moe:
                        split(pos, i + AHEAD)
                    else:
                        ahead(pos + i)
                    if (m, half) == ("a", 1):
                        act.wait_ge(chunk_used, pos + (i + 1))
                        if j:
                            act.wait_ge(hid_made, g * NB + j)
                        for t in range(tiles):
                            last = act.activation(silu[:, t, :], bank(j % 2 if one else t), ACT.Silu)
                        last.then_inc(silu_done, 1)
                    jt = take_after(i, one)
                    if jt is not None:
                        act.wait_ge(hid_turned, g * NB + (jt + 1))
                        for t in range(tiles):
                            last = act.activation(hidT_hi[jt % 2 if one else t], bank(7 if one else 2 + t).rearrange("p (k s) -> p k s", k=4),
                                                  ACT.Copy)
                        last.then_inc(hidT_hi_done, 1)
                        if moe and one and jt == 1:
                            act.wait_ge(pick_turned, item + 1)
                            act.activation(pick_gT[:, 0, :], bank(6)[:, 0:S], ACT.Copy).then_inc(pickT_ready, 1)
                if moe:
                    act.wait_ge(chunk_used, pos + NX)
                    for t in range(tiles):
                        last = act.activation(y_exp[:, t, 0:512], bank(4 + 2 * t), ACT.Copy)
                    last.then_inc(y_free, 1)
                    take_x(item + 1, 0, 0, gathered, x_hi_done)

            def route():
                act.dma_start(r_raw, a["moe_router"][0].rearrange("(k p) e -> p k e", p=P)).then_inc(router_loaded, 16)
                act.dma_start(route_k, a["router_consts"]).then_inc(router_loaded, 16)
                act.wait_ge(router_loaded, 32)
                act.activation(r_hi[:, :, :], r_raw, ACT.Copy).then_inc(router_hi, 1)
                act.wait_ge(expo_in, 1)
                for t in range(NT):
                    act.activation(expo[:, t, :], logit[:, t, :], ACT.Exp, bias=stat[:, 40 + t:41 + t]).then_inc(expo_out, 1)

            def mixer(l):
                take_turned(3 * l, actT_hi)
                phase()
                project(l)
                gates(l)
                take_turned(3 * l + 1, actT_hi, 4)
                load_gains(a["ln1_g"][l], a["ln1_b"][l])
                output(l)
                phase()
                norm_std(VAR_PREP[l] + 2)
                take_turned(3 * l + 2, actT_hi)
                phase()

            act.wait_ge(ident_loaded, 16)
            norm_std(0)
            for q in range(AHEAD):
                split(0, q)
            mixer(0)
            load_gains(a["ln2_g"][0], a["ln2_b"][0])
            expert(DENSE_BASE, 0, 2)
            phase()
            norm_std(VAR_PREP[0] + 3)
            mixer(1)
            load_gains(a["ln2_g"][1], a["ln2_b"][1])
            route()
            phase()
            act.wait_ge(items_known, 1)
            items = act.value_load(n_items[0:1, 0:1], min_val=1, max_val=NE)
            for q in range(AHEAD):
                split(MOE_BASE, q)
            take_x(0, 0, 0, gathered, x_hi_done)
            with act.Fori(0, items) as item:
                two = act.value_load(item_tiles[0:1, bass.ds(item, 1)], min_val=0, max_val=1)
                item_loads[0] = act.snap(item * (16 * NX // RAW))
                pos, g = act.snap(item * NX + MOE_BASE), act.snap(item + 1)
                with act.If(two == 1):
                    expert(pos, g, 2, item)
                with act.Else():
                    expert(pos, g, 1, item)
            phase()
            norm_std(VAR_PREP[1] + 3)

        @block.vector
        def _(dve):
            phase = Phases(dve)
            step = Steps(dve, dve_step)

            def split(pos, i, width=CH):
                s, q = slot_at(pos + i) if isinstance(pos, int) and pos + i < MOE_BASE else i % RAW, i % SPL
                dve.wait_ge(hi_done, pos + (i + 1))
                dve.tensor_tensor(w_lo[:, q, 0:width], raw[:, s, 0:width], w_hi[:, q, 0:width].bitcast(F32),
                                  ALU.subtract).then_inc(lo_done, 1)

            def ahead(i):
                if i + AHEAD < MOE_BASE:
                    split(0, i + AHEAD, width_at(i + AHEAD))

            def take_turned(n, dst_hi, dst_lo, first=0):
                for b in range(4):
                    t, half = (b % 2, b // 2) if first else (b // 2, b % 2)
                    x = (slice(None), slice(4 * half, 4 * half + 4), slice(t * P, (t + 1) * P))
                    dve.wait_ge(turn_hi, 4 * n + b + 1)
                    dve.tensor_tensor(dst_lo[x], bank(first + b).rearrange("p (k t) -> p k t", k=4),
                                      dst_hi[x].bitcast(F32), ALU.subtract).then_inc(turn_lo, 1)

            def std(n):
                dve.wait_ge(std_ready, n + 1)
                r, v = stat[:, 16:32], stat[:, 0:16]
                step(dve.reciprocal(r, r))
                step(dve.tensor_tensor(v, v, r, ALU.mult))
                step(dve.tensor_tensor(v, v, r, ALU.mult))
                step(dve.tensor_scalar(v, v, -0.5, 1.5, ALU.mult, ALU.add))
                step(dve.tensor_tensor(r, r, v, ALU.mult))

            def layernorm(n, gains_at):
                for t in range(NT):
                    for c in range(2):
                        last = dve.bn_stats(stat[:, 56 + 12 * t + 6 * c:62 + 12 * t + 6 * c], h[:, t, c * 512:(c + 1) * 512])
                step(last)
                for t in range(NT):
                    step(dve.bn_aggr(stat[:, 80 + 2 * t:82 + 2 * t], stat[:, 56 + 12 * t:68 + 12 * t]))
                step(dve.memset(stat[:, 0:16], 1.0))
                dve.tensor_scalar(stat[:, 0:2], stat[:, 81:84:2], LN_EPS, None, ALU.add).then_inc(var_ready, 1)
                std(n)
                if gains_at:
                    dve.wait_ge(gains_loaded, 32 * gains_at)
                else:
                    dve.wait_ge(start_loaded, 32)
                for t in range(NT):
                    step(dve.scalar_tensor_tensor(h[:, t, :], h[:, t, :], stat[:, 80 + 2 * t:81 + 2 * t], small[:, 0:D],
                                                  ALU.subtract, ALU.mult))
                    dve.scalar_tensor_tensor(h[:, t, :], h[:, t, :], stat[:, 16 + t:17 + t], small[:, D:2 * D],
                                             ALU.mult, ALU.add).then_inc(ln_tile, 1)

            def side(l, i, half):
                for piece in SIDE.get((i, half), []):
                    if piece[0] == "unit":
                        unit(l, piece[1], piece[2])
                    elif piece[0] == "prep":
                        prepare(l, piece[1])
                    elif piece[0] == "turn":
                        n = BRANCHES[piece[1]]
                        dve.wait_ge(branch_hi, 4 * l + piece[1] + 1)
                        dve.tensor_tensor(brT_lo[:, 2 * n:2 * n + 2, :], bank(6).rearrange("p (k t) -> p k t", k=2),
                                          brT_hi[:, 2 * n:2 * n + 2, :].bitcast(F32), ALU.subtract).then_inc(branch_lo, 1)
                    elif piece[0] == "diff_norm":
                        diff_norm(l)
                    elif piece[0] == "lambda":
                        diff_lambda(l)

            def project(l):
                base = mix_base(l)
                for s, (c0, n, feat) in enumerate(SLOTS):
                    for half in range(2):
                        ahead(base + 2 * s + half)
                        side(l, 2 * s + half, 0)
                        if half:
                            b1 = 2 * (s % 2) + 1
                            dve.wait_ge(chunk_used, base + 2 * s + 2)
                            if feat:
                                f = ((c0 - C_FEAT) // P if c0 < C_DV else 12) + 2
                                dve.tensor_scalar(featT[:, f:f + 2, :], bank(b1).rearrange("p (b t) -> p b t", b=2),
                                                  HD ** -0.5 if f < 6 else 1.0, None, ALU.mult).then_inc(proj_used[1], 1)
                            else:
                                dve.tensor_copy(token_dst(c0, n, 1), bank(b1)[:, 0:n]).then_inc(proj_used[1], 1)
                        side(l, 2 * s + half, 1)

            def diff_lambda(l):
                init = 0.8 - 0.6 * math.exp(-0.3 * l)
                dve.wait_ge(params_loaded, 16 * N_PARAM * (l + 1))
                lp = lamp[:, :, :].rearrange("p (m w) d -> p m w d", w=2)
                prod = gate_pr[:, 0, 0:64].rearrange("p (m d) -> p m d", m=2)
                step(dve.tensor_tensor(prod, lp[:, :, 0, :], lp[:, :, 1, :], ALU.mult))
                dve.tensor_reduce(stat[:, 48:50], prod, AX.X, ALU.add).then_inc(lam_sum, 1)
                dve.wait_ge(lam_exp, l + 1)
                step(dve.tensor_tensor(stat[:, 52:53], stat[:, 51:52], stat[:, 50:51], ALU.subtract))
                step(dve.tensor_scalar(stat[:, 52:53], stat[:, 52:53], -init, None, ALU.add))

            def unit(l, part, i):
                us, base = PARTS[part], unit_base(l, part)
                if i < len(us):
                    u = base + i
                    kind, hd, t, m = us[i]
                    nm = stat[:, 32 + i % 2:33 + i % 2]
                    dve.wait_ge(scores, u + 1)
                    if i >= 2:
                        dve.wait_ge(exps, u - 1)
                    if i >= 3:
                        dve.wait_ge(prob_turned, u - 2)
                    if part != LATE:
                        for g in range(3 if kind == "dil" else 1):
                            slope = 2.0 ** (-8.0 * (4 * g + hd + 1) / 12) if kind == "dil" else 2.0 ** (-8.0 * (hd + 1) / 4)
                            k = K_DIST + 384 * (g if kind == "dil" else 3) + P * (1 - t)
                            b = 4 + g // 2 if kind == "dil" else 4 + i % 2
                            last = dve.scalar_tensor_tensor(
                                prob[:, i % 3, g * S:(g + 1) * S], const[:, k:k + S], -slope,
                                bank(b)[:, (g % 2) * S:(g % 2 + 1) * S], ALU.mult, ALU.add)
                        step(last)
                        n = 3 * S if kind == "dil" else S
                        dve.tensor_reduce(nm, prob[:, i % 3, 0:n], AX.X, ALU.max, negate=True).then_inc(negmax, 1)
                    else:
                        step(dve.tensor_reduce(nm, bank(4 + i % 2)[:, 0:S], AX.X, ALU.max, negate=True))
                        dve.tensor_scalar(nm, nm, scale_of(kind), None, ALU.mult).then_inc(negmax, 1)
                if 2 <= i < len(us) + 2 and EVAC[us[i - 2][0]][1]:
                    j = i - 2
                    u, kind = base + j, us[j][0]
                    if j >= 2:
                        dve.wait_ge(pv_done, u - 1)
                    if kind == "dil":
                        dve.wait_ge(prob_turned, u + 1)
                        if j:
                            dve.wait_ge(pv_done, u)
                        dve.tensor_copy(probT[:, j % 2, 512:768], bank(7)[:, S:2 * S]).then_inc(turned_taken[1], 1)
                    else:
                        dve.wait_ge(prob_turned, u + 1)
                        dve.tensor_copy(probT[:, j % 2, 0:S], bank(6)[:, 0:S]).then_inc(turned_taken[1], 1)
                if i >= 3:
                    j = i - 3
                    u = base + j
                    kind, hd, t, m = us[j]
                    r = stat[:, 44:45]
                    c0 = {"mla": 0, "dil": 1, "gqa": 2, "diff": 3}[kind] * BW + hd * HD
                    dst, o = y[:, t, c0:c0 + HD], bank(7)[:, 0:HD]
                    step(dve.reciprocal(r, stat[:, 36 + j % 4:37 + j % 4]))
                    if m:
                        step(dve.tensor_tensor(r, r, stat[:, 52:53], ALU.mult))
                    dve.wait_ge(pv_done, u + 1)
                    if m:
                        step(dve.scalar_tensor_tensor(dst, o, r, dst, ALU.mult, ALU.add))
                    else:
                        step(dve.tensor_scalar(dst, o, r, None, ALU.mult))
                    dve.engine_nop().then_inc(out_taken, 1)

            def prepare(l, stage):
                if stage == 0:
                    for e in range(2):
                        dve.wait_ge(proj_used[e], (l + 1) * len(SLOTS))
                    step(dve.memset(stat[:, 0:16], 1.0))
                    step(dve.tensor_tensor(sq_c, cqkv[:, :, 0:QL + KVL], cqkv[:, :, 0:QL + KVL], ALU.mult))
                    dve.tensor_reduce(stat[:, 0:2], sq_c[:, :, 0:QL], AX.X, ALU.add)
                    dve.tensor_reduce(stat[:, 2:4], sq_c[:, :, QL:QL + KVL], AX.X, ALU.add)
                    step(dve.tensor_tensor(gn, gqa[:, :, 0:384], gqa[:, :, 0:384], ALU.mult))
                    step(dve.tensor_reduce(stat[:, 4:16], gn.rearrange("p t (h d) -> p (t h) d", d=HD), AX.X, ALU.add))
                    dve.tensor_scalar(stat[:, 0:2], stat[:, 0:2], 1.0 / QL, RMS_EPS, ALU.mult, ALU.add)
                    dve.tensor_scalar(stat[:, 2:4], stat[:, 2:4], 1.0 / KVL, RMS_EPS, ALU.mult, ALU.add)
                    dve.tensor_scalar(stat[:, 4:16], stat[:, 4:16], 1.0 / HD, RMS_EPS, ALU.mult, ALU.add).then_inc(var_ready, 1)
                    std(VAR_PREP[l] + 1)
                    for t in range(NT):
                        dve.scalar_tensor_tensor(cn[:, t, 0:QL], cqkv[:, t, 0:QL], stat[:, 16 + t:17 + t], g_q, ALU.mult, ALU.mult)
                        last = dve.scalar_tensor_tensor(cn[:, t, QL:QL + KVL], cqkv[:, t, QL:QL + KVL], stat[:, 18 + t:19 + t],
                                                        g_kv, ALU.mult, ALU.mult)
                    last.then_inc(prep_dve, 1)
                if stage in (1, 2):
                    for t in (stage - 1,):
                        x3 = gn[:, t, :].rearrange("p (h d) -> p h d", d=HD)
                        rs = stat[:, 20 + 6 * t:26 + 6 * t].unsqueeze(2).to_broadcast([P, 6, HD])
                        step(dve.tensor_tensor(x3, gqa[:, t, 0:384].rearrange("p (h d) -> p h d", d=HD), rs, ALU.mult))
                        step(dve.tensor_tensor(gn[:, t, :], gn[:, t, :], g_gqa, ALU.mult))
                        x5 = gn[:, t, :].rearrange("p (h a w d) -> p h a w d", h=6, a=2, w=2)
                        r5 = rope_a[:, t, :].rearrange("p (h a w d) -> p h a w d", h=6, a=2, w=2)
                        sin = const[:, K_GS + 64 * t:K_GS + 64 * t + 64].rearrange("p (a w d) -> p a w d", a=2, w=2)
                        cos = const[:, K_GC + 64 * t:K_GC + 64 * t + 64]
                        for w in range(2):
                            dve.tensor_tensor(r5[:, :, :, w, :], x5[:, :, :, 1 - w, :],
                                              sin[:, :, w, :].unsqueeze(1).to_broadcast([P, 6, 2, 16]), ALU.mult)
                        step(dve.tensor_tensor(gr[:, t, :].rearrange("p (h d) -> p h d", d=HD), x3,
                                               cos.unsqueeze(1).to_broadcast([P, 6, HD]), ALU.mult))
                        last = dve.tensor_tensor(gr[:, t, :], gr[:, t, :], rope_a[:, t, :], ALU.add)
                    if stage == 2:
                        last.then_inc(prep_dve, 1)
                if stage == 3:
                    for t in range(NT):
                        sin = const[:, K_MS + 32 * t:K_MS + 32 * t + 32].rearrange("p (w d) -> p w d", w=2)
                        cos = const[:, K_MC + 32 * t:K_MC + 32 * t + 32]
                        dve.wait_ge(prep_act, 8 * l + 2 + t + 1)
                        q = bank(4 + t)[:, 0:384].rearrange("p (h d) -> p h d", h=4)[:, :, 64:96]
                        q4 = q.rearrange("p h (w d) -> p h w d", w=2)
                        tq = rope_m[:, t, 0:P].rearrange("p (h w d) -> p h w d", h=4, w=2)
                        tc = rope_m[:, t, P:2 * P].rearrange("p (h d) -> p h d", h=4)
                        for w in range(2):
                            dve.tensor_tensor(tq[:, :, w, :], q4[:, :, 1 - w, :],
                                              sin[:, w, :].unsqueeze(1).to_broadcast([P, 4, 16]), ALU.mult)
                        step(dve.tensor_tensor(tc, q, cos.unsqueeze(1).to_broadcast([P, 4, 32]), ALU.mult))
                        step(dve.tensor_tensor(mq[:, t, :, 64:96], tc, rope_m[:, t, 0:P].rearrange("p (h d) -> p h d", h=4), ALU.add))
                        kr = cqkv[:, t, QL + KVL:QL + KVL + MR].rearrange("p (w d) -> p w d", w=2)
                        tk = rope_m[:, t, 0:32].rearrange("p (w d) -> p w d", w=2)
                        for w in range(2):
                            dve.tensor_tensor(tk[:, w, :], kr[:, 1 - w, :], sin[:, w, :], ALU.mult)
                        step(dve.tensor_tensor(rope_m[:, t, 32:64], cqkv[:, t, QL + KVL:QL + KVL + MR], cos, ALU.mult))
                        last = dve.tensor_tensor(mk[:, t, :, 64:96], rope_m[:, t, 0:32].unsqueeze(1).to_broadcast([P, 4, 32]),
                                                 rope_m[:, t, 32:64].unsqueeze(1).to_broadcast([P, 4, 32]), ALU.add)
                    last.then_inc(prep_dve, 1)
                if stage == 4:
                    dve.wait_ge(prep_pe, 11 * l + 7)
                    dve.tensor_copy(gT[0:64, 4:6, :], bank(4)[0:64].rearrange("p (h t) -> p h t", h=2)).then_inc(prep_dve, 1)
                if stage == 5:
                    for b in range(2):
                        dve.wait_ge(prep_pe, 11 * l + 9 + b + 1)
                        last = dve.tensor_copy(mkT[0:96, 2 * b:2 * b + 2, :], bank((7, 4)[b])[0:96].rearrange("p (h t) -> p h t", h=2))
                    last.then_inc(prep_dve, 1)

            def diff_norm(l):
                init = 0.8 - 0.6 * math.exp(-0.3 * l)
                sq = prob[:, 0, 0:512].rearrange("p (t n) -> p t n", t=NT)
                yd = y[:, :, 3 * BW:4 * BW]
                step(dve.memset(stat[:, 0:16], 1.0))
                step(dve.tensor_tensor(sq, yd, yd, ALU.mult))
                step(dve.tensor_reduce(stat[:, 0:8], sq.rearrange("p t (h d) -> p (t h) d", d=HD), AX.X, ALU.add))
                dve.tensor_scalar(stat[:, 0:8], stat[:, 0:8], 1.0 / HD, DIFF_EPS, ALU.mult, ALU.add).then_inc(var_ready, 1)
                std(VAR_PREP[l])
                for t in range(NT):
                    yt = y[:, t, 3 * BW:4 * BW].rearrange("p (h d) -> p h d", d=HD)
                    rs = stat[:, 16 + 4 * t:20 + 4 * t].unsqueeze(2).to_broadcast([P, 4, HD])
                    step(dve.tensor_tensor(yt, yt, rs, ALU.mult))
                    step(dve.tensor_tensor(yt, yt, g_sub.unsqueeze(1).to_broadcast([P, 4, HD]), ALU.mult))
                    last = dve.tensor_scalar(yt, yt, 1.0 - init, None, ALU.mult)
                last.then_inc(diff_normed, 1)

            def take_branch(l, q, c):
                for t in range(NT):
                    dst = mixed[:, t, c * 512:(c + 1) * 512]
                    if (c, t) == (1, 1):
                        dve.wait_ge(chunk_used, mix_base(l) + N_PROJ + 5 * q + 5)
                    else:
                        dve.wait_ge(branch_made, 3 * (NBR * l + q) + 2 * c + t + 1)
                    dve.wait_ge(gate_open, 16 * l + 4 * q + 2 * c + t + 1)
                    if q == 0:
                        dve.tensor_tensor(dst, gate_sb[:, 2 * c + t, :], bank(2 * c + t), ALU.mult).then_inc(branch_used, 1)
                    else:
                        pr = gate_pr[:, t, :]
                        step(dve.tensor_tensor(pr, gate_sb[:, 2 * c + t, :], bank(2 * c + t), ALU.mult))
                        dve.tensor_tensor(dst, dst, pr, ALU.add).then_inc(branch_used, 1)

            def gates(l):
                base = mix_base(l)
                for i in range(N_GATE):
                    ahead(base + N_PROJ + i)
                    if i % 5 == 4:
                        take_branch(l, i // 5, 0)
                    side(l, N_PROJ + i, 0)
                    q, c = i // 5, (i % 5) // 2
                    if i % 5 in (1, 3):
                        dve.wait_ge(chunk_used, base + N_PROJ + i + 1)
                        dve.wait_ge(bias_loaded, 16 * (NBR * l + q + 1))
                        for t in range(NT):
                            dve.tensor_tensor(gate_sb[:, 2 * c + t, :], bank(2 * c + t),
                                              gate_bias[:, c * 512:(c + 1) * 512], ALU.add).then_inc(gate_biased, 1)
                    if i % 5 == 4:
                        take_branch(l, q, 1)
                    side(l, N_PROJ + i, 1)

            def output(l):
                for q in range(N_OUT):
                    ahead(mix_base(l) + N_PROJ + N_GATE + q)
                for t in range(NT):
                    if t == 0:
                        dve.wait_ge(tile_made, l + 1)
                    else:
                        dve.wait_ge(chunk_used, mix_base(l) + N_MIX)
                    for c in range(2):
                        x = h[:, t, c * 512:(c + 1) * 512]
                        step(dve.scalar_tensor_tensor(x, x, ALPHA, bank(2 * t + c), ALU.mult, ALU.add))

            def make_picks(item):
                for t in range(NT):
                    s_i = item_slot[:, t, bass.ds(item, 1)]
                    dve.tensor_scalar(pick[:, t, :], iota, s_i, None, ALU.is_equal)
                    last = dve.tensor_scalar(pick_g[:, t, :], iota, s_i, item_gate[:, t, bass.ds(item, 1)],
                                             ALU.is_equal, ALU.mult)
                last.then_inc(picked, 1)

            def take_x(item, tile, banks, at_, ready):
                for r in range(2):
                    x = (slice(None), slice(4 * r, 4 * r + 4), slice(tile * P, (tile + 1) * P))
                    dve.wait_ge(at_, 2 * item + (r + 1))
                    dve.tensor_tensor(xT_lo[x], bank(banks + r).rearrange("p (k s) -> p k s", k=4),
                                      xT_hi[x].bitcast(F32), ALU.subtract).then_inc(ready, 1)

            def expert(pos, g, tiles, item=None):
                one, moe = tiles == 1, item is not None
                if moe and one:
                    dve.engine_nop().then_inc(x2_lo_done, 2)
                if moe and not one:
                    take_x(item, 1, 6, x2_hi_done, x2_lo_done)
                for i, (m, j, half) in enumerate(ORDER):
                    if moe:
                        split(pos, i + AHEAD)
                    else:
                        ahead(pos + i)
                    if (m, half) == ("b", 1):
                        dve.wait_ge(chunk_used, pos + (i + 1))
                        dve.wait_ge(silu_done, g * NB + (j + 1))
                        for t in range(tiles):
                            last = dve.tensor_tensor(hid[:, t, :], silu[:, t, :], bank(2 + (j % 2 if one else t)), ALU.mult)
                        last.then_inc(hid_made, 1)
                    jt = take_after(i, one)
                    if jt is not None:
                        dve.wait_ge(hidT_hi_done, g * NB + (jt + 1))
                        for t in range(tiles):
                            o = jt % 2 if one else t
                            last = dve.tensor_tensor(hidT_lo[o], bank(7 if one else 2 + t).rearrange("p (k s) -> p k s", k=4),
                                                     hidT_hi[o].bitcast(F32), ALU.subtract)
                        last.then_inc(hidT_lo_done, 1)
                    if moe and (m, j, half) == ("w", 2, 1):
                        dve.wait_ge(pick_turned, item + 1)
                        make_picks(item + 1)
                if moe:
                    dve.wait_ge(chunk_used, pos + NX)
                    for t in range(tiles):
                        last = dve.tensor_copy(y_exp[:, t, 512:1024], bank(5 + 2 * t))
                    last.then_inc(y_free, 1)
                    take_x(item + 1, 0, 0, x_hi_done, x_lo_done)
                    for t in range(NT):
                        for c in range(2):
                            x = acc[:, t, c * 512:(c + 1) * 512]
                            dve.wait_ge(scattered, 4 * item + (2 * t + c + 1))
                            dve.tensor_tensor(x, x, bank(2 + 2 * t + c), ALU.add).then_inc(acc_added, 1)

            def route():
                dve.wait_ge(router_hi, 1)
                dve.tensor_tensor(r_lo[:, :, :], r_raw, r_hi[:, :, :].bitcast(F32), ALU.subtract).then_inc(router_lo, 1)
                dve.wait_ge(logits_done, 1)
                for t in range(NT):
                    step(dve.tensor_copy(logit[:, t, :], bank(t)[:, 0:NE]))
                step(dve.tensor_reduce(stat[:, 40:42], logit, AX.X, ALU.max, negate=True))
                dve.engine_nop().then_inc(expo_in, 1)
                dve.wait_ge(router_loaded, 32)
                tie = route_k[:, R_TIE:R_TIE + 64]
                for t in range(NT):
                    this = logit[:, t, :].unsqueeze(2).to_broadcast([P, NE, NE])
                    other = logit[:, t, :].unsqueeze(1).to_broadcast([P, NE, NE])
                    ca = cmp_a[:, t, :].rearrange("p (e f) -> p e f", e=NE)
                    cb = cmp_b[:, t, :].rearrange("p (e f) -> p e f", e=NE)
                    step(dve.tensor_tensor(ca, other, this, ALU.is_gt))
                    step(dve.tensor_tensor(cb, other, this, ALU.is_equal))
                    step(dve.tensor_tensor(cmp_b[:, t, :], cmp_b[:, t, :], tie, ALU.mult))
                    step(dve.tensor_tensor(cmp_a[:, t, :], cmp_a[:, t, :], cmp_b[:, t, :], ALU.add))
                    step(dve.tensor_reduce(rank[:, t, :], ca, AX.X, ALU.add))
                dve.tensor_scalar(sel, rank, 2.0, None, ALU.is_lt).then_inc(sel_done, 1)
                dve.wait_ge(sel_done, 1)
                dve.wait_ge(expo_out, 2)
                step(dve.tensor_tensor(expo, expo, sel, ALU.mult))
                step(dve.tensor_reduce(stat[:, 42:44], expo, AX.X, ALU.add))
                step(dve.reciprocal(stat[:, 42:44], stat[:, 42:44]))
                for t in range(NT):
                    step(dve.tensor_scalar(gate[:, t, :], expo[:, t, :], stat[:, 42 + t:43 + t], None, ALU.mult))
                step(dve.tensor_scalar(slot, sel, -NOWHERE, NOWHERE, ALU.mult, ALU.add))
                dve.wait_ge(counted, 1)
                for t in range(NT):
                    step(dve.tensor_tensor(slot[:, t, :], slot[:, t, :], bank(2 + t)[:, 0:NE], ALU.add))
                step(dve.tensor_scalar(tiles_of[:, 0, :], bank(4)[:, 0:NE], 0.0, None, ALU.is_gt))
                step(dve.tensor_scalar(tiles_of[:, 1, :], bank(4)[:, 0:NE], float(P), None, ALU.is_gt))
                step(dve.tensor_copy(ends, tiles_of[:, 0, :]))
                for e in range(1, NE):
                    step(dve.tensor_tensor(ends[:, e:e + 1], ends[:, e - 1:e], ends[:, e:e + 1], ALU.add))
                number = route_k[:, R_ITEM:R_ALL].rearrange("p (i e) -> p i e", e=NE)
                step(dve.tensor_tensor(item_tmp, ends.unsqueeze(1).to_broadcast([P, MAX_ITEMS, NE]), number, ALU.is_le))
                step(dve.tensor_reduce(item_e, item_tmp, AX.X, ALU.add))
                step(dve.tensor_tensor(item_hot, item_e.unsqueeze(2).to_broadcast([P, MAX_ITEMS, NE]),
                                       route_k[:, R_ITEM:R_ITEM + NE * NE:NE].unsqueeze(1).to_broadcast([P, MAX_ITEMS, NE]),
                                       ALU.is_equal))
                for t in range(NT):
                    for src, dst in ((slot, item_slot), (gate, item_gate)):
                        step(dve.tensor_tensor(item_tmp, item_hot, src[:, t, :].unsqueeze(1).to_broadcast([P, MAX_ITEMS, NE]),
                                               ALU.mult))
                        step(dve.tensor_reduce(dst[:, t, :], item_tmp, AX.X, ALU.add))
                step(dve.tensor_tensor(item_tmp, item_hot, tiles_of[:, 1, :].unsqueeze(1).to_broadcast([P, MAX_ITEMS, NE]),
                                       ALU.mult))
                step(dve.tensor_reduce(item_two, item_tmp, AX.X, ALU.add))
                step(dve.tensor_copy(item_tiles[0:1, :], item_two[0:1, :]))
                step(dve.tensor_scalar(item_expert[0:1, :], item_e[0:1, :], float(NE - 1), None, ALU.min))
                dve.tensor_copy(n_items[0:1, 0:1], ends[0:1, NE - 1:NE]).then_inc(items_known, 1)
                step(dve.memset(acc, 0.0))

            def residual(dense):
                for t in range(NT):
                    for c in range(2):
                        w = slice(c * 512, (c + 1) * 512)
                        last = dve.scalar_tensor_tensor(h[:, t, w], h[:, t, w], ALPHA,
                                                        bank(4 + 2 * t + c) if dense else acc[:, t, w], ALU.mult, ALU.add)
                step(last)

            def mixer(l):
                take_turned(3 * l, actT_hi, actT_lo)
                phase()
                if l == 0:
                    split(0, 1)
                    dve.wait_ge(const_loaded, 16)
                project(l)
                gates(l)
                take_turned(3 * l + 1, actT_hi, actT_lo, 4)
                output(l)
                phase()
                layernorm(VAR_PREP[l] + 2, 2 * l + 1)
                take_turned(3 * l + 2, actT_hi, actT_lo)
                phase()

            dve.engine_nop().then_inc(acc_added, 1)
            dve.wait_ge(x_loaded, 16 * NT)
            layernorm(0, 0)
            split(0, 0)
            mixer(0)
            expert(DENSE_BASE, 0, 2)
            phase()
            residual(True)
            layernorm(VAR_PREP[0] + 3, 2)
            mixer(1)
            route()
            phase()
            items = dve.value_load(n_items[0:1, 0:1], min_val=1, max_val=NE)
            make_picks(0)
            for q in range(AHEAD):
                split(MOE_BASE, q)
            take_x(0, 0, 0, x_hi_done, x_lo_done)
            with dve.Fori(0, items) as item:
                two = dve.value_load(item_tiles[0:1, bass.ds(item, 1)], min_val=0, max_val=1)
                pos, g = dve.snap(item * NX + MOE_BASE), dve.snap(item + 1)
                with dve.If(two == 1):
                    expert(pos, g, 2, item)
                with dve.Else():
                    expert(pos, g, 1, item)
            phase()
            residual(False)
            layernorm(VAR_PREP[1] + 3, 4)


N_PARAM = 13
VAR_PREP = [1, 5]

INS = ["x", "ln_emb_g", "ln_emb_b", "w_in", "b_gate", "mla_q_norm", "mla_kv_norm", "mla_w_uq", "mla_w_ukv",
       "gqa_q_norm", "gqa_k_norm", "diff_lambda", "diff_subln", "w_branch", "w_out", "ln1_g", "ln1_b",
       "ffn_w13", "ffn_w2", "moe_router", "moe_w13", "moe_w2", "ln2_g", "ln2_b"]


def kernel(**inputs):
    import numpy as _np
    import concourse.bacc as _bacc
    from concourse import mybir as _mybir
    from concourse.bass_utils import run_bass_kernel_spmd as _run

    nc = _bacc.Bacc("TRN2", target_bir_lowering=False, num_devices=1)
    arrays, args = {}, {}
    tables = {"consts": constants(), "router_consts": router_constants()}
    for name in INS + list(tables):
        v = tables[name] if name in tables else _np.ascontiguousarray(inputs[name])
        arrays[f"in_{name}"] = v
        args[name] = nc.dram_tensor(f"in_{name}", v.shape, _mybir.dt.from_np(v.dtype), kind="ExternalInput").ap()
    args["out"] = nc.dram_tensor("out_h", (1, S, D), _mybir.dt.from_np(_np.dtype("float32")), kind="ExternalOutput").ap()
    encoder(nc, args)
    r = _run(nc, [arrays], core_ids=[0])
    return r.results[0]["out_h"]
```

```python
import math
from contextlib import ExitStack

import numpy as np

import concourse.bass as bass
from concourse import mybir

F32 = mybir.dt.float32
F32R = mybir.dt.float32r
I32 = mybir.dt.int32
ALU = mybir.AluOpType
ACT = mybir.ActivationFunctionType
AX = mybir.AxisListType

P = 128
D = 1024
S = 256
NT = S // P
DK = D // P
DEPTH = 2
GRID_W = 64
FF = 3584
NE = 8
TOP_K = 2
MAX_ITEMS = NE + 1
NBR = 4
BW = 256
QL, KVL, MR = 192, 128, 32
HD = 64
DIL_GROUPS = ((128, 1), (512, 4), (2048, 16))
ALPHA = (2 * DEPTH) ** 0.25
LN_EPS, RMS_EPS, DIFF_EPS = 1e-5, 1e-6, 1e-5
FAR = 1e30
HALF = P // 2
NOWHERE = 1e6

C_FEAT = 352
C_DV = 1888
C_DQK = 3168
C_DIFFV = 3680
C_GATE = 3936

CH = 2048
RAW = 6
RAW_MIX = 3
SPL = 3
AHEAD = 2
EARLY = RAW + AHEAD
FB = 512
NB = FF // FB

SLOTS = [(C_DQK, 512, True), (C_DIFFV, 256, False)] + \
        [(C_FEAT + 512 * i, 512, True) for i in range(3)] + \
        [(C_DV, 512, False), (C_DV + 512, 256, False), (C_DV + 768, 512, False), (0, 352, False)]
SLOTS_DIFF, SLOTS_DIL = 2, 7


def expert_order():
    order = []
    for j in range(NB):
        order += [("a", j, 0), ("a", j, 1), ("b", j, 0), ("b", j, 1)]
        if j:
            order += [("w", j - 1, 0), ("w", j - 1, 1)]
    return order + [("w", NB - 1, 0), ("w", NB - 1, 1)]


ORDER = expert_order()


def turned_before(i, one):
    m, j, half = ORDER[i]
    if one:
        return j - 1 if (m, half) == ("b", 0) and j else NB - 1 if (m, j, half) == ("w", NB - 2, 1) else None
    if (m, j, half) == ("a", 1, 1):
        return 0
    if i and ORDER[i - 1][0] == "w" and ORDER[i - 1][2] == 1:
        return ORDER[i - 1][1] + 1
    return None


def take_after(i, one):
    return turned_before(i + 1, one) if i + 1 < len(ORDER) else None


NX = len(ORDER)
N_PROJ = 2 * len(SLOTS)
N_GATE = 5 * NBR
N_OUT = 4
N_MIX = N_PROJ + N_GATE + N_OUT
MIX_WIDTH = [4 * SLOTS[i // 2][1] for i in range(N_PROJ)] + [CH] * (N_GATE + N_OUT)
assert NX % RAW == 0 and N_MIX % RAW == 0 and NX % SPL == 0 and N_MIX % SPL == 0


def mix_base(l):
    return l * (N_MIX + NX)


DENSE_BASE = N_MIX
MOE_BASE = mix_base(1) + N_MIX


def slot_at(i):
    return i % RAW if DENSE_BASE <= i < DENSE_BASE + NX or i >= MOE_BASE else i % RAW_MIX


def loads_at(i):
    return sum(slot_at(q) == slot_at(i) for q in range(i + 1))


LOADS = [sum(slot_at(q) == r for q in range(MOE_BASE)) for r in range(RAW)]


def width_at(i):
    for l in range(DEPTH):
        if mix_base(l) <= i < mix_base(l) + N_MIX:
            return MIX_WIDTH[i - mix_base(l)]
    return CH


BRANCHES = (3, 1, 0, 2)
DIFF, DIL, LATE = range(3)
PARTS = [[("diff", h, t, m) for h in range(4) for t in range(NT) for m in range(2)],
         [("dil", h, t, 0) for t in range(NT) for h in range(4)],
         [("mla", h, t, 0) for h in range(4) for t in range(NT)] +
         [("gqa", h, t, 0) for h in range(4) for t in range(NT)]]
N_UNIT = sum(len(u) for u in PARTS)


def unit_base(l, part):
    return l * N_UNIT + sum(len(PARTS[q]) for q in range(part))




def side_plan():
    plan = {}

    def put(at, pieces):
        for piece in pieces:
            while at >= 2 * N_PROJ and (at - 2 * N_PROJ) % 10 == 9:
                at += 1
            plan.setdefault(divmod(at, 2), []).append(piece)
            at += 1
        return at

    late = [("unit", LATE, i) for i in range(len(PARTS[LATE]) + 3)]
    dil = [("unit", DIL, i) for i in range(len(PARTS[DIL]) + 3)]
    put(3, [("lambda",)])
    at = put(4 * SLOTS_DIFF, [("unit", DIFF, i) for i in range(len(PARTS[DIFF]) + 3)] + [("diff_var",), ("diff_norm",)])
    at = put(max(at, 4 * SLOTS_DIL), dil[:1])
    at = put(at, dil[1:])
    at = put(at, [("prep_var",), ("prep", 0)])
    at = put(at, [("turn", 0), ("turn", 1)])
    put(at - 1, [("prep", 1)])
    at = put(at, [("prep", 2), ("prep", 3)])
    at = put(at, [("prep", 4), ("prep", 5)])
    at = put(at + 1, late[:11] + [("turn", 2)] + late[11:])
    at = put(at, [("turn", 3)])
    assert at <= 2 * (N_PROJ + N_GATE) - 2
    return plan


SIDE = side_plan()
EVAC = {"dil": (1, 1), "diff": (1, 0), "mla": (0, 1), "gqa": (0, 1)}
EVACS = [(0, 0)]
for _l in range(DEPTH):
    for _u in PARTS[DIFF] + PARTS[DIL] + PARTS[LATE]:
        EVACS.append((EVACS[-1][0] + EVAC[_u[0]][0], EVACS[-1][1] + EVAC[_u[0]][1]))


def scale_of(kind):
    return {"mla": 96 ** -0.5, "gqa": HD ** -0.5}.get(kind, 1.0)


K_ID = 0
K_DIST = 128
K_MC = K_DIST + 4 * 384
K_MS = K_MC + 2 * 32
K_GC = K_MS + 2 * 32
K_GS = K_GC + 2 * 64
K_ALL = K_GS + 2 * 64
R_IOTA = 0
R_TRI = R_IOTA + S
R_ONES = R_TRI + P
R_TIE = R_ONES + P
R_ITEM = R_TIE + 64
R_ALL = R_ITEM + MAX_ITEMS * NE


def constants():
    k = np.zeros((P, K_ALL), np.float32)
    p = np.arange(P)
    k[:, K_ID:K_ID + P] = np.eye(P)
    d = np.abs(np.arange(-128, 256)[None, :] - p[:, None])
    for g, (window, dil) in enumerate(DIL_GROUPS):
        k[:, K_DIST + 384 * g:K_DIST + 384 * (g + 1)] = np.where((d <= window // 2) & (d % dil == 0), d, FAR)
    k[:, K_DIST + 384 * 3:K_DIST + 384 * 4] = d
    inv = (10000.0 ** -(np.arange(0, 32, 2, dtype=np.float32) / np.float32(32))).astype(np.float32)
    for t in range(NT):
        pos = (t * P + p).astype(np.float32)
        for c0, s0, angs in ((K_MC, K_MS, [pos]), (K_GC, K_GS, [pos // GRID_W, pos % GRID_W])):
            n = 32 * len(angs)
            for i, a in enumerate(angs):
                ang = a[:, None] * inv[None, :]
                c, s = c0 + t * n + 32 * i, s0 + t * n + 32 * i
                k[:, c:c + 16] = k[:, c + 16:c + 32] = np.cos(ang)
                k[:, s:s + 16] = -np.sin(ang)
                k[:, s + 16:s + 32] = np.sin(ang)
    return k


def router_constants():
    k = np.zeros((P, R_ALL), np.float32)
    p, e = np.arange(P), np.arange(64)
    k[:, R_IOTA:R_IOTA + S] = np.arange(S)[None, :]
    k[:, R_TRI:R_TRI + P] = p[:, None] < p[None, :]
    k[:, R_ONES:R_ONES + P] = 1.0
    k[:, R_TIE:R_TIE + 64] = (e % 8 < e // 8)[None, :]
    k[:, R_ITEM:R_ALL] = (np.arange(MAX_ITEMS * NE) // NE)[None, :]
    return k


def encoder(nc, a):
    with ExitStack() as ctx:
        def sb(name, shape, dt=F32):
            return ctx.enter_context(nc.sbuf_tensor(name, shape, dt))

        def sem(name):
            return ctx.enter_context(nc.semaphore(name))

        raw = sb("raw", [P, RAW, CH])
        w_hi = sb("w_hi", [P, SPL, CH], F32R)
        w_lo = sb("w_lo", [P, SPL, CH], F32R)
        h = sb("h", [P, NT, D])
        actT_hi = sb("actT_hi", [P, DK, S], F32R)
        actT_lo = sb("actT_lo", [P, DK, S], F32R)
        brT_hi = sb("brT_hi", [P, DK, S], F32R)
        brT_lo = sb("brT_lo", [P, DK, S], F32R)
        const = sb("const", [P, K_ALL])
        small = sb("small", [P, 2048])
        lamp = sb("lamp", [P, 4, 32])
        stat = sb("stat", [P, 96])
        landed = sb("landed", [P, RAW])
        n_items = sb("n_items", [1, 1], I32)
        item_expert = sb("item_expert", [1, MAX_ITEMS], I32)
        item_kind = sb("item_kind", [1, MAX_ITEMS], I32)
        work = sb("work", [P, 13760])
        ps = ctx.enter_context(nc.psum_tensor("banks", [P, 8, 512], F32))

        def at(off, n):
            return work[:, off:off + n]

        ident = const[:, K_ID:K_ID + P]

        featT = at(0, 4096).rearrange("p (b t) -> p b t", b=16)
        dilv = at(4096, 1536).rearrange("p (t n) -> p t n", t=NT)
        diffv = at(5632, 512).rearrange("p (t n) -> p t n", t=NT)
        gqa = at(6144, 1024).rearrange("p (t n) -> p t n", t=NT)
        cqkv = at(7168, 704).rearrange("p (t n) -> p t n", t=NT)
        y = at(7872, 2048).rearrange("p (t n) -> p t n", t=NT)
        prob = at(9920, 2304).rearrange("p (b n) -> p b n", b=3)
        probT = at(9920 + 2304, 1536).rearrange("p (b n) -> p b n", b=2)
        mqT = at(0, 1024).rearrange("p (h t) -> p h t", h=4)
        mkT = at(1024, 1024).rearrange("p (h t) -> p h t", h=4)
        gT = at(2048, 1536).rearrange("p (h t) -> p h t", h=6)
        rope_a = at(0, 768).rearrange("p (t n) -> p t n", t=NT)
        rope_m = at(768, 512).rearrange("p (t n) -> p t n", t=NT)
        mq = at(4096, 768).rearrange("p (t h d) -> p t h d", t=NT, h=4)
        mk = at(4864, 768).rearrange("p (t h d) -> p t h d", t=NT, h=4)
        mv = at(5632, 512).rearrange("p (t h d) -> p t h d", t=NT, h=4)
        cn = at(9920, 640).rearrange("p (t n) -> p t n", t=NT)
        gn = at(9920 + 640, 768).rearrange("p (t n) -> p t n", t=NT)
        gr = at(9920 + 1408, 768).rearrange("p (t n) -> p t n", t=NT)
        cT = at(9920 + 2176, 768).rearrange("p (c t) -> p c t", c=3)
        sq_c = at(9920 + 2176, 640).rearrange("p (t n) -> p t n", t=NT)
        over = raw[:, RAW_MIX:RAW, :].rearrange("p s n -> p (s n)")
        mixed = over[:, 0:2048].rearrange("p (t n) -> p t n", t=NT)
        gate_sb = over[:, 2048:4096].rearrange("p (b n) -> p b n", b=4)
        gate_pr = over[:, 4096:5120].rearrange("p (b n) -> p b n", b=2)
        gate_bias = over[:, 5120:6144]
        xT_hi, xT_lo = actT_hi, actT_lo
        hidT_hi = [brT_hi[:, 4 * t:4 * t + 4, P:S] for t in range(NT)]
        hidT_lo = [brT_lo[:, 4 * t:4 * t + 4, P:S] for t in range(NT)]
        acc = y
        silu = at(9920, 1024).rearrange("p (t n) -> p t n", t=NT)
        hid = at(10944, 1024).rearrange("p (t n) -> p t n", t=NT)
        pick = at(0, 512).rearrange("p (t s) -> p t s", t=NT)
        pick_g = at(512, 512).rearrange("p (t s) -> p t s", t=NT)
        pick_gT = at(1024, 512).rearrange("p (i t) -> p i t", i=NT)
        y_exp = at(1536, 2048).rearrange("p (t n) -> p t n", t=NT)
        route_k = at(12000, R_ALL)
        iota = at(12000 + R_IOTA, S)
        tri = at(12000 + R_TRI, P)
        ones = at(12000 + R_ONES, P)
        places = iter(range(3600, 13760))

        def table(rows, n, name="i"):
            off = next(places)
            for _ in range(rows * n - 1):
                next(places)
            return at(off, rows * n).rearrange(f"p (r {name}) -> p r {name}", r=rows)

        logit, rank, sel, expo = (table(NT, NE) for _ in range(4))
        slot_gate = table(2 * NT, NE)
        slot, gate = slot_gate[:, 0:NT, :], slot_gate[:, NT:2 * NT, :]
        cmp_a, cmp_b = table(NT, NE * NE), table(NT, NE * NE)
        item_sg = table(2 * NT, MAX_ITEMS)
        item_slot, item_gate = item_sg[:, 0:NT, :], item_sg[:, NT:2 * NT, :]
        item_four = table(2 * NT, MAX_ITEMS * NE).rearrange("p r (m e) -> p r m e", e=NE)
        item_hot, item_tmp = table(MAX_ITEMS, NE), table(MAX_ITEMS, NE)
        item_e, item_k, ends = table(1, MAX_ITEMS)[:, 0, :], table(1, MAX_ITEMS)[:, 0, :], table(1, NE)[:, 0, :]
        tiles_of = table(3, NE)
        r_raw = table(DK, NE)
        logitT = at(1536, S)
        r_split = sb("r_split", [P, DK, 2 * NE], F32R)
        w_uq0, w_uq1 = small[:, 0:384], small[0:64, 384:768]
        w_ukv = small[:, 768:1280]
        g_q, g_kv = small[:, 1280:1472], small[:, 1472:1600]
        g_gqa, g_sub = small[:, 1600:1984], small[:, 1984:2048]

        chunk_loaded = [sem(f"chunk_loaded{i}") for i in range(RAW)]
        hi_done, lo_done = sem("hi_done"), sem("lo_done")
        chunk_used = sem("chunk_used")
        phase_done = sem("phase_done")
        start_loaded, gains_loaded = sem("start_loaded"), sem("gains_loaded")
        x_loaded = [sem(f"x_loaded{t}") for t in range(NT)]
        ident_loaded, const_loaded = sem("ident_loaded"), sem("const_loaded")
        params_loaded, bias_loaded = sem("params_loaded"), sem("bias_loaded")
        router_loaded, stored = sem("router_loaded"), sem("stored")
        dve_step = sem("dve_step")
        turned4, turn_hi = sem("turned4"), sem("turn_hi")
        proj_used = [sem("proj_used_act"), sem("proj_used_dve")]
        var_ready, std_ready = sem("var_ready"), sem("std_ready")
        lam_sum, lam_exp = sem("lam_sum"), sem("lam_exp")
        scores, negmax, exps = sem("scores"), sem("negmax"), sem("exps")
        prob_turned, pv_done, out_taken = sem("prob_turned"), sem("pv_done"), sem("out_taken")
        branch_turned, branch_hi, branch_lo = sem("branch_turned"), sem("branch_hi"), sem("branch_lo")
        diff_normed = sem("diff_normed")
        turned_taken = [sem("turned_taken_act"), sem("turned_taken_dve")]
        prep_dve, prep_act, prep_pe = sem("prep_dve"), sem("prep_act"), sem("prep_pe")
        gate_biased, gate_open, branch_used = sem("gate_biased"), sem("gate_open"), sem("branch_used")
        branch_made = sem("branch_made")
        turn_lo, tile_made = sem("turn_lo"), sem("tile_made")
        silu_done, hid_made, hid_turned = sem("silu_done"), sem("hid_made"), sem("hid_turned")
        hidT_hi_done, hidT_lo_done = sem("hidT_hi_done"), sem("hidT_lo_done")
        x_hi_done, x_lo_done = sem("x_hi_done"), sem("x_lo_done")
        y_free, acc_added = sem("y_free"), sem("acc_added")
        picked, gathered, pick_turned, pickT_ready = sem("picked"), sem("gathered"), sem("pick_turned"), sem("pickT_ready")
        scattered = sem("scattered")
        pick_doubled, a_summed = sem("pick_doubled"), sem("a_summed")
        halves_step = sem("halves_step")
        gathered2, x2_hi_done, x2_lo_done = sem("gathered2"), sem("x2_hi_done"), sem("x2_lo_done")
        ln_tile = sem("ln_tile")
        router_hi, router_lo, logits_done = sem("router_hi"), sem("router_lo"), sem("logits_done")
        logits_copied, logits_turned = sem("logits_copied"), sem("logits_turned")
        expo_in, expo_out, sel_done, counted, items_known = sem("expo_in"), sem("expo_out"), sem("sel_done"), sem("counted"), sem("items_known")

        block = ctx.enter_context(nc.Block())

        def bank(i):
            return ps[:, i, :]

        def token_dst(c0, n, t):
            if c0 == 0:
                return cqkv[:, t, :]
            if c0 < C_DV + 768:
                return dilv[:, t, c0 - C_DV:c0 - C_DV + n]
            return gqa[:, t, :] if c0 == C_DV + 768 else diffv[:, t, :]

        def turns_before(l, part, i):
            return 4 * l + (0, 0, 3 if i >= 11 else 2)[part]

        class Steps:

            def __init__(self, eng, s, base=0):
                self.eng, self.s, self.base, self.n = eng, s, base, 0

            def __call__(self, ins):
                self.n += 1
                ins.then_inc(self.s, 1)
                self.eng.wait_ge(self.s, self.base + self.n)

        class Phases:

            def __init__(self, eng):
                self.eng, self.n = eng, 0

            def __call__(self):
                self.n += 1
                self.eng.drain().then_inc(phase_done, 1)
                self.eng.wait_ge(phase_done, 3 * self.n)

        @block.sync
        def _(sp):
            x = a["x"][0].rearrange("(t p) d -> t p d", p=P)
            for t in range(NT):
                sp.dma_start(h[:, t, :], x[t]).then_inc(x_loaded[t], 16)
            sp.dma_start(ident, a["consts"][:, K_ID:K_ID + P]).then_inc(ident_loaded, 16)
            sp.dma_start(small[:, 0:D], a["ln_emb_g"].partition_broadcast(P)).then_inc(start_loaded, 16)
            sp.dma_start(small[:, D:2 * D], a["ln_emb_b"].partition_broadcast(P)).then_inc(start_loaded, 16)

            def load(pos, i, src, width, k):
                static = isinstance(pos, int)
                s = slot_at(pos + i) if static else i % RAW
                if not static:
                    sp.wait_ge(lo_done, pos + (i - RAW + 1))
                elif pos + i >= RAW_MIX:
                    last = [q for q in range(pos + i) if slot_at(q) == s]
                    if last:
                        sp.wait_ge(lo_done, last[-1] + 1)
                    if DENSE_BASE <= pos + i < DENSE_BASE + RAW and s >= RAW_MIX:
                        sp.wait_ge(turned4, 4 * 2)
                dst = raw[:, s, 0:width].rearrange("p (k n) -> p k n", k=k)
                sp.dma_start(dst, src).then_inc(chunk_loaded[s], 16)

            def mixer(l):
                base = mix_base(l)
                w_in = a["w_in"][l].rearrange("(k p) n -> p k n", p=P)
                w_br = a["w_branch"][l].rearrange("n (k p) d -> n p k d", p=P)
                w_out = a["w_out"][l].rearrange("(k p) n -> p k n", p=P)
                i = 0
                for c0, n, _feat in SLOTS:
                    for half in range(2):
                        load(base, i, w_in[:, 4 * half:4 * half + 4, c0:c0 + n], 4 * n, 4)
                        i += 1
                        if i == 3:
                            load_params(l)
                for n in BRANCHES:
                    for c in range(2):
                        for half in range(2):
                            c0 = C_GATE + n * D + c * 512
                            load(base, i, w_in[:, 4 * half:4 * half + 4, c0:c0 + 512], CH, 4)
                            i += 1
                    load(base, i, w_br[n], CH, 2)
                    i += 1
                for q in range(N_OUT):
                    load(base, i, w_out[:, 2 * q:2 * q + 2, :], CH, 2)
                    i += 1

            def load_params(l):
                if l == 0:
                    rest = slice(K_ID + P, K_ALL)
                    sp.dma_start(const[:, rest], a["consts"][:, rest]).then_inc(const_loaded, 16)
                sp.wait_ge(ln_tile, NT * (2 * l + 1))
                q = a["mla_w_uq"][l]
                for dst, src in ((lamp[:, :, :], a["diff_lambda"][l].partition_broadcast(P)),
                                 (g_sub, a["diff_subln"][l].partition_broadcast(P)),
                                 (w_uq0, q[0:P, :]), (w_uq1, q[P:QL, :]), (w_ukv, a["mla_w_ukv"][l]),
                                 (g_q, a["mla_q_norm"][l].partition_broadcast(P)),
                                 (g_kv, a["mla_kv_norm"][l].partition_broadcast(P))):
                    sp.dma_start(dst, src).then_inc(params_loaded, 16)
                for hd in range(6):
                    g = a["gqa_q_norm" if hd < 4 else "gqa_k_norm"][l].partition_broadcast(P)
                    sp.dma_start(g_gqa[:, hd * HD:(hd + 1) * HD], g).then_inc(params_loaded, 16)
                if l:
                    sp.wait_ge(lo_done, mix_base(l))
                sp.dma_start(gate_bias, a["b_gate"][l][BRANCHES[0]].partition_broadcast(P)).then_inc(bias_loaded, 16)

            def expert(pos, w13, w2, chunks=range(NX)):
                for i in chunks:
                    m, j, half = ORDER[i % NX]
                    if m == "w":
                        load(pos, i, w2[:, 4 * j + 2 * half:4 * j + 2 * half + 2, :], CH, 2)
                    else:
                        c0 = j * FB + (FF if m == "b" else 0)
                        load(pos, i, w13[:, 4 * half:4 * half + 4, c0:c0 + FB], CH, 4)

            mixer(0)
            expert(DENSE_BASE, a["ffn_w13"][0].rearrange("(k p) n -> p k n", p=P),
                   a["ffn_w2"][0].rearrange("(k p) n -> p k n", p=P))
            mixer(1)
            sp.wait_ge(turned4, 4 * 5)
            sp.dma_start(r_raw, a["moe_router"][0].rearrange("(k p) e -> p k e", p=P)).then_inc(router_loaded, 16)
            sp.dma_start(route_k, a["router_consts"]).then_inc(router_loaded, 16)
            w13 = a["moe_w13"][0].rearrange("e (k p) n -> e p k n", p=P)
            w2 = a["moe_w2"][0].rearrange("e (k p) n -> e p k n", p=P)
            expert(MOE_BASE, w13[0], w2[0], range(EARLY))
            sp.wait_ge(items_known, 1)
            items = sp.value_load(n_items[0:1, 0:1], min_val=1, max_val=NE)
            with sp.Fori(0, items) as g:
                for q, chunks in ((g, range(EARLY, NX)), (g + 1, range(NX, NX + EARLY))):
                    e = sp.value_load(item_expert[0:1, bass.ds(q, 1)], min_val=0, max_val=NE - 1)
                    expert(g * NX + MOE_BASE, w13[bass.ds(e, 1)].squeeze(0), w2[bass.ds(e, 1)].squeeze(0), chunks)
            out = a["out"][0].rearrange("(t p) d -> t p d", p=P)
            for t in range(NT):
                sp.wait_ge(ln_tile, NT * 2 * DEPTH + t + 1)
                sp.dma_start(out[t], h[:, t, :]).then_inc(stored, 16)
            sp.wait_ge(stored, 16 * NT)

        @block.tensor
        def _(pe):
            phase = Phases(pe)

            def three(out, l_hi, l_lo, r_hi_, r_lo_, start, stop):
                pe.matmul(out, l_hi, r_hi_, start=start, stop=False, skip_group_check=True)
                pe.matmul(out, l_hi, r_lo_, start=False, stop=False, skip_group_check=True)
                return pe.matmul(out, l_lo, r_hi_, start=False, stop=stop, skip_group_check=True)

            def two(out, packed, r_hi_, r_lo_, start, stop):
                pe.matmul(out, packed, r_hi_, start=start, stop=False, skip_group_check=True)
                return pe.matmul(out, packed, r_lo_, start=False, stop=stop, skip_group_check=True)

            def chunk(pos, i):
                pe.wait_ge(lo_done, pos + (i + 1))
                return w_hi[:, i % SPL, :], w_lo[:, i % SPL, :]

            def turn(src, after):
                for b in range(4):
                    t, half = b // 2, b % 2
                    pe.wait_ge(ln_tile, NT * after + t + 1)
                    for i in range(4):
                        c = (4 * half + i) * P
                        mm = pe.transpose(bank(b)[:, i * P:(i + 1) * P], src[:, t, c:c + P], ident)
                    mm.then_inc(turned4, 1)

            def turn_mixed(l):
                pe.wait_ge(exps, (l + 1) * N_UNIT)
                for b in range(4):
                    c, t = b // 2, b % 2
                    pe.wait_ge(branch_used, 16 * l + 12 + b + 1)
                    for i in range(4):
                        x = c * 512 + i * P
                        mm = pe.transpose(bank(4 + b)[:, i * P:(i + 1) * P], mixed[:, t, x:x + P], ident)
                    mm.then_inc(turned4, 1)

            def side(l, i, half):
                for piece in SIDE.get((i, half), []):
                    if piece[0] == "unit":
                        unit(l, piece[1], piece[2])
                    elif piece[0] == "prep":
                        prepare(l, piece[1])
                    elif piece[0] == "turn":
                        turn_branch(l, piece[1])

            def project(l):
                base = mix_base(l)
                for s, (c0, n, feat) in enumerate(SLOTS):
                    b0 = 2 * (s % 2)
                    if s >= 2:
                        for q in range(2):
                            pe.wait_ge(proj_used[q], l * len(SLOTS) + s - 1)
                    for half in range(2):
                        if s == 0:
                            pe.wait_ge(turn_lo, 4 * 3 * l + 3 + half)
                        hi, lo = chunk(base, 2 * s + half)
                        for o in range(4 if feat else NT):
                            for kk in range(4):
                                k, first, last = 4 * half + kk, half == 0 and kk == 0, half == 1 and kk == 3
                                if feat:
                                    w = slice(kk * n + o * P, kk * n + (o + 1) * P)
                                    out = bank(b0 + o // 2)[:, (o % 2) * S:(o % 2 + 1) * S]
                                    mm = three(out, hi[:, w], lo[:, w], actT_hi[:, k, :], actT_lo[:, k, :],
                                               first and o % 2 == 0, last)
                                else:
                                    w = slice(kk * n, (kk + 1) * n)
                                    x = slice(o * P, (o + 1) * P)
                                    mm = three(bank(b0 + o)[:, 0:n], actT_hi[:, k, x], actT_lo[:, k, x],
                                               hi[:, w], lo[:, w], first, last)
                            if o == (1 if feat else 0):
                                side(l, 2 * s + half, 0)
                        mm.then_inc(chunk_used, 1)
                        side(l, 2 * s + half, 1)

            def turn_branch(l, q):
                n = BRANCHES[q]
                units_done = unit_base(l, (DIL, DIL, LATE, LATE)[q]) + (8, 8, 8, 16)[q]
                pe.wait_ge(out_taken, units_done)
                if q == 0:
                    pe.wait_ge(diff_normed, l + 1)
                if q == 1:
                    pe.wait_ge(branch_lo, 4 * l + 1)
                for e in range(2):
                    if EVACS[units_done][e]:
                        pe.wait_ge(turned_taken[e], EVACS[units_done][e])
                for k in range(2):
                    for t in range(NT):
                        mm = pe.transpose(bank(6)[:, (2 * k + t) * P:(2 * k + t + 1) * P],
                                          y[:, t, n * BW + k * P:n * BW + (k + 1) * P], ident)
                mm.then_inc(branch_turned, 1)

            def operands(kind, hd, t, m):
                q = slice(t * P, (t + 1) * P)
                if kind == "dil":
                    out = []
                    for g in range(3):
                        n = g * 4 + hd
                        r = slice(64 * (n % 2), 64 * (n % 2) + 64)
                        out.append((featT[r, n // 2, q], featT[r, 6 + n // 2, :],
                                    [dilv[:, kt, n * HD:(n + 1) * HD] for kt in range(NT)]))
                    return out
                if kind == "diff":
                    r0 = (hd % 2) * 64 + m * 32
                    return [(featT[r0:r0 + 32, 12 + hd // 2, q], featT[r0:r0 + 32, 14 + hd // 2, :],
                             [diffv[:, kt, hd * HD:(hd + 1) * HD] for kt in range(NT)])]
                if kind == "mla":
                    return [(mqT[0:96, hd, q], mkT[0:96, hd, :], [mv[:, kt, hd, :] for kt in range(NT)])]
                kv = hd // 2
                return [(gT[0:64, hd, q], gT[0:64, 4 + kv, :],
                         [gqa[:, kt, 384 + kv * HD:384 + (kv + 1) * HD] for kt in range(NT)])]

            def unit(l, part, i):
                us, base = PARTS[part], unit_base(l, part)
                turned = i - 2 if 2 <= i < len(us) + 2 else None

                if turned is not None:
                    u, kind = base + turned, us[turned][0]
                    pe.wait_ge(exps, u + 1)
                    for e in range(2):
                        if EVACS[u][e]:
                            pe.wait_ge(turned_taken[e], EVACS[u][e])
                    if turns_before(l, part, i):
                        pe.wait_ge(branch_lo, turns_before(l, part, i))
                    if kind == "dil" and i >= 4:
                        pe.wait_ge(out_taken, base + i - 3)
                    for b in range(6 if kind == "dil" else 2):
                        dst = bank(6)[:, b * P:(b + 1) * P] if b < 4 else bank(7)[:, (b - 2) * P:(b - 1) * P]
                        mm = pe.transpose(dst, prob[:, turned % 3, b * P:(b + 1) * P], ident)
                    mm.then_inc(prob_turned, 1)
                if i < len(us):
                    u, kind = base + i, us[i][0]
                    if i == 0:
                        if part == LATE:
                            pe.wait_ge(prep_act, 8 * (l + 1))
                            pe.wait_ge(prep_dve, 5 * (l + 1))
                        else:
                            for e in range(2):
                                pe.wait_ge(proj_used[e], l * len(SLOTS) + (SLOTS_DIFF if part == DIFF else SLOTS_DIL))
                    if part == LATE and i >= 2:
                        pe.wait_ge(exps, u - 1)
                    elif part == DIFF and i >= 2:
                        pe.wait_ge(negmax, u - 1)
                    elif part != LATE and u:
                        pe.wait_ge(negmax, u)
                    for g, (q, k, _v) in enumerate(operands(*us[i])):
                        b = 4 + g // 2 if kind == "dil" else 4 + i % 2
                        mm = pe.matmul(bank(b)[:, (g % 2) * S:(g % 2 + 1) * S], q, k, start=True, stop=True)
                    mm.then_inc(scores, 1)
                if i >= 3:
                    j = i - 3
                    u, kind = base + j, us[j][0]
                    for e in range(2):
                        if EVAC[kind][e]:
                            pe.wait_ge(turned_taken[e], EVACS[u + 1][e])
                    if u:
                        pe.wait_ge(out_taken, u)
                    vs = [v for (_q, _k, vv) in operands(*us[j]) for v in vv]
                    for b, v in enumerate(vs):
                        mm = pe.matmul(bank(7)[:, 0:HD], probT[:, j % 2, b * P:(b + 1) * P], v,
                                       start=(b == 0), stop=(b == len(vs) - 1))
                    mm.then_inc(pv_done, 1)

            def prepare(l, stage):
                if stage == 1:
                    pe.wait_ge(prep_dve, 5 * l + 1)
                    pe.wait_ge(exps, unit_base(l, LATE))
                    for t in range(NT):
                        pe.transpose(bank(4 + t)[:, 0:P], cn[:, t, 0:P], ident)
                        pe.transpose(bank(4 + t)[0:64, P:2 * P], cn[:, t, P:QL], ident)
                        pe.transpose(bank(4 + t)[:, 2 * P:3 * P], cn[:, t, QL:QL + KVL], ident).then_inc(prep_pe, 1)
                if stage == 2:
                    pe.wait_ge(params_loaded, 16 * N_PARAM * (l + 1))
                    pe.wait_ge(branch_lo, 4 * l + 2)
                    for t in range(NT):
                        x = slice(t * P, (t + 1) * P)
                        pe.wait_ge(prep_act, 8 * l + t + 1)
                        pe.matmul(bank(4 + t)[:, 0:384], cT[:, 0, x], w_uq0, start=True, stop=False)
                        pe.matmul(bank(4 + t)[:, 0:384], cT[0:64, 1, x], w_uq1, start=False, stop=True)
                        pe.matmul(bank(6 + t)[:, :], cT[:, 2, x], w_ukv, start=True, stop=True).then_inc(prep_pe, 1)
                if stage == 4:
                    pe.wait_ge(prep_dve, 5 * l + 3)
                    pe.wait_ge(prep_act, 8 * l + 4)
                    for b in range(2):
                        for i in range(4):
                            hd, t = 2 * b + i // 2, i % 2
                            mm = pe.transpose(bank(6 + b)[0:64, i * P:(i + 1) * P], gr[:, t, hd * HD:(hd + 1) * HD], ident)
                        mm.then_inc(prep_pe, 1)
                    for i in range(4):
                        hd, t = 4 + i // 2, i % 2
                        mm = pe.transpose(bank(4)[0:64, i * P:(i + 1) * P], gr[:, t, hd * HD:(hd + 1) * HD], ident)
                    mm.then_inc(prep_pe, 1)
                if stage == 5:
                    for n, (src, hds, b) in enumerate(((mq, 0, 5), (mq, 2, 6), (mk, 0, 7), (mk, 2, 4))):
                        if n in (1, 2):
                            pe.wait_ge(prep_act, 8 * l + 4 + n)
                        if n == 3:
                            pe.wait_ge(prep_dve, 5 * l + 4)
                        for i in range(4):
                            hd, t = hds + i // 2, i % 2
                            mm = pe.transpose(bank(b)[0:96, i * P:(i + 1) * P], src[:, t, hd, :], ident)
                        mm.then_inc(prep_pe, 1)

            def gates(l):
                base = mix_base(l)
                for q, n in enumerate(BRANCHES):
                    i0 = N_PROJ + 5 * q
                    for c in range(2):
                        for half in range(2):
                            hi, lo = chunk(base, i0 + 2 * c + half)
                            if half == 0 and q:
                                pe.wait_ge(branch_used, 16 * l + 4 * (q - 1) + 2 * c + 2)
                            if half == 0 and q == 0:
                                for e in range(2):
                                    pe.wait_ge(proj_used[e], (l + 1) * len(SLOTS))
                            for t in range(NT):
                                x = slice(t * P, (t + 1) * P)
                                for kk in range(4):
                                    k, w = 4 * half + kk, slice(kk * 512, (kk + 1) * 512)
                                    mm = three(bank(2 * c + t), actT_hi[:, k, x], actT_lo[:, k, x],
                                               hi[:, w], lo[:, w], k == 0, k == DK - 1)
                                if t == 0:
                                    side(l, i0 + 2 * c + half, 0)
                            mm.then_inc(chunk_used, 1)
                            side(l, i0 + 2 * c + half, 1)
                    hi, lo = chunk(base, i0 + 4)
                    pe.wait_ge(branch_lo, 4 * l + q + 1)
                    for c in range(2):
                        for t in range(NT):
                            pe.wait_ge(gate_biased, 16 * l + 4 * q + 2 * c + t + 1)
                            x = slice(t * P, (t + 1) * P)
                            for kk in range(2):
                                w = slice(kk * D + c * 512, kk * D + (c + 1) * 512)
                                mm = three(bank(2 * c + t), brT_hi[:, 2 * n + kk, x], brT_lo[:, 2 * n + kk, x],
                                           hi[:, w], lo[:, w], kk == 0, kk == 1)
                            if (c, t) != (1, 1):
                                mm.then_inc(branch_made, 1)
                        if c == 0:
                            side(l, i0 + 4, 0)
                    mm.then_inc(chunk_used, 1)
                    side(l, i0 + 4, 1)

            def output(l):
                base = mix_base(l)
                for q in range(N_OUT):
                    if q % 2 == 0:
                        pe.wait_ge(turn_lo, 4 * (3 * l + 1) + q + 2)
                    hi, lo = chunk(base, N_PROJ + N_GATE + q)
                    for t in range(NT):
                        x = slice(t * P, (t + 1) * P)
                        for kk in range(2):
                            k = 2 * q + kk
                            for c in range(2):
                                w = slice(kk * D + c * 512, kk * D + (c + 1) * 512)
                                mm = three(bank(2 * t + c), actT_hi[:, k, x], actT_lo[:, k, x], hi[:, w], lo[:, w],
                                           k == 0, k == DK - 1)
                        if q == N_OUT - 1 and t == 0:
                            mm.then_inc(tile_made, 1)
                    mm.then_inc(chunk_used, 1)

            def gather(item, tile, banks, done):
                for r in range(2):
                    for i in range(4):
                        d = (4 * r + i) * P
                        for t in range(NT):
                            mm = pe.matmul(bank(banks + r)[:, i * P:(i + 1) * P], h[:, t, d:d + P],
                                           pick[:, t, tile * P:(tile + 1) * P], start=(t == 0), stop=(t == 1))
                    mm.then_inc(done, 1)

            def turn_picks(tiles, b):
                for i in range(tiles):
                    for t in range(NT):
                        mm = pe.transpose(bank(b)[:, (2 * i + t) * P:(2 * i + t + 1) * P],
                                          pick_g[:, t, i * P:(i + 1) * P], ident)
                mm.then_inc(pick_turned, 1)

            def expert(pos, g, tiles, item=None, packed=False):
                one, moe = tiles == 1, item is not None
                if moe and one:
                    pe.nop().then_inc(gathered2, 2)
                if moe and not one:
                    gather(item, 1, 6, gathered2)
                    pe.wait_ge(acc_added, 4 * item + 1)
                    pe.wait_ge(pick_doubled, item + 1)
                    turn_picks(2, 3)
                for i, (m, j, half) in enumerate(ORDER):
                    jt = turned_before(i, one)
                    if jt is not None:
                        pe.wait_ge(hid_made, g * NB + (jt + 1))
                        for t in range(tiles):
                            rows = HALF if packed and t else P
                            for q in range(4):
                                mm = pe.transpose(bank(7 if one else 2 + t)[:, q * P:q * P + rows],
                                                  hid[0:rows, t, q * P:(q + 1) * P], ident[0:rows, 0:rows])
                        mm.then_inc(hid_turned, 1)
                        if moe and one and jt == 1:
                            turn_picks(1, 6)
                    hi, lo = chunk(pos, i)
                    if moe and i == 0:
                        pe.wait_ge(x_lo_done, 2 * item + 2)
                        if not one:
                            pe.wait_ge(x2_lo_done, 2 * item + 2)
                    if moe and (m, j, half) == ("b", 0, 0):
                        pe.wait_ge(acc_added, 4 * item + 1)
                    if m in "ab":
                        if one and j >= 2 and half == 0:
                            pe.wait_ge(hid_made, g * NB + (j - 1))
                        if not one and j and half == 0:
                            if m == "a":
                                pe.wait_ge(silu_done, g * NB + j)
                            else:
                                pe.wait_ge(hidT_lo_done, g * NB + j)
                        for t in range(tiles):
                            b = (j % 2 if one else t) + (2 if m == "b" else 0)
                            x = slice(t * P, (t + 1) * P)
                            for kk in range(4):
                                k, w = 4 * half + kk, slice(kk * FB, (kk + 1) * FB)
                                if packed and t:
                                    mm = two(bank(b), xT_hi[:, k, x], hi[:, w], lo[:, w], k == 0, k == DK - 1)
                                else:
                                    mm = three(bank(b), xT_hi[:, k, x], xT_lo[:, k, x], hi[:, w], lo[:, w],
                                               k == 0, k == DK - 1)
                    else:
                        if half == 0:
                            pe.wait_ge(hidT_lo_done, g * NB + (j + 1))
                        for t in range(tiles):
                            for kk in range(2):
                                for c in range(2):
                                    w = slice(kk * D + c * 512, kk * D + (c + 1) * 512)
                                    o = j % 2 if one else t
                                    out, k = bank(4 + 2 * t + c), 2 * half + kk
                                    first, last = (j, half, kk) == (0, 0, 0), (j, half, kk) == (NB - 1, 1, 1)
                                    if packed and t:
                                        mm = two(out, hidT_hi[o][:, k, :], hi[:, w], lo[:, w], first, last)
                                    else:
                                        mm = three(out, hidT_hi[o][:, k, :], hidT_lo[o][:, k, :], hi[:, w], lo[:, w],
                                                   first, last)
                            if not moe and i == NX - 1 and t == 0:
                                mm.then_inc(tile_made, 1)
                    mm.then_inc(chunk_used, 1)
                if moe:
                    pe.wait_ge(picked, item + 2)
                    gather(item, 0, 0, gathered)
                    pe.wait_ge(y_free, 2 * item + 2)
                    pe.wait_ge(pickT_ready, item + 1)
                    for t in range(NT):
                        for c in range(2):
                            for i in range(tiles):
                                mm = pe.matmul(bank(2 + 2 * t + c), pick_gT[:, i, t * P:(t + 1) * P],
                                               y_exp[:, i, c * 512:(c + 1) * 512], start=(i == 0), stop=(i == tiles - 1))
                            mm.then_inc(scattered, 1)

            def route():
                pe.wait_ge(router_lo, 1)
                for k in range(DK):
                    pe.matmul(bank(0)[0:2 * NE, 0:S], r_split[:, k, :], actT_hi[:, k, :], start=(k == 0), stop=False,
                              skip_group_check=True)
                for k in range(DK):
                    mm = pe.matmul(bank(0)[0:NE, 0:S], r_split[:, k, 0:NE], actT_lo[:, k, :], start=False,
                                   stop=(k == DK - 1), skip_group_check=True)
                mm.then_inc(logits_done, 1)
                pe.wait_ge(logits_copied, 1)
                for t in range(NT):
                    mm = pe.transpose(bank(1)[:, 2 * NE * t:2 * NE * (t + 1)], logitT[0:2 * NE, t * P:(t + 1) * P],
                                      ident[0:2 * NE, 0:2 * NE])
                mm.then_inc(logits_turned, 1)
                pe.wait_ge(sel_done, 1)
                pe.matmul(bank(2)[:, 0:NE], tri, sel[:, 0, :], start=True, stop=True)
                pe.matmul(bank(3)[:, 0:NE], ones, sel[:, 0, :], start=True, stop=False)
                pe.matmul(bank(3)[:, 0:NE], tri, sel[:, 1, :], start=False, stop=True)
                pe.matmul(bank(4)[:, 0:NE], ones, sel[:, 0, :], start=True, stop=False)
                pe.matmul(bank(4)[:, 0:NE], ones, sel[:, 1, :], start=False, stop=True).then_inc(counted, 1)

            def mixer(l):
                turn(h, 2 * l)
                project(l)
                gates(l)
                turn_mixed(l)
                output(l)
                turn(h, 2 * l + 1)
                pe.wait_ge(turn_lo, 4 * (3 * l + 3))

            pe.wait_ge(ident_loaded, 16)
            mixer(0)
            expert(DENSE_BASE, 0, 2)
            mixer(1)
            route()
            phase()
            pe.wait_ge(items_known, 1)
            items = pe.value_load(n_items[0:1, 0:1], min_val=1, max_val=NE)
            pe.wait_ge(picked, 1)
            gather(0, 0, 0, gathered)
            with pe.Fori(0, items) as item:
                kind = pe.value_load(item_kind[0:1, bass.ds(item, 1)], min_val=0, max_val=2)
                pos, g = pe.snap(item * NX + MOE_BASE), pe.snap(item + 1)
                with pe.If(kind == 0):
                    expert(pos, g, 1, item)
                with pe.Else():
                    with pe.If(kind == 1):
                        expert(pos, g, 2, item, packed=True)
                    with pe.Else():
                        expert(pos, g, 2, item)

        @block.scalar
        def _(act):
            phase = Phases(act)

            def split(pos, i, width=CH):
                q = i % SPL
                if isinstance(pos, int):
                    s = slot_at(pos + i)
                    act.wait_ge(chunk_loaded[s], 16 * loads_at(pos + i))
                else:
                    s = i % RAW
                    act.wait_ge(chunk_loaded[s], item_loads[0] + 16 * (LOADS[s] + i // RAW + 1))
                if not (isinstance(pos, int) and pos + i < SPL):
                    act.wait_ge(chunk_used, pos + (i - SPL + 1))
                act.activation(w_hi[:, q, 0:width], raw[:, s, 0:width], ACT.Copy).then_inc(hi_done, 1)

            item_loads = [0]

            def take_turned(n, dst_hi, first=0):
                for b in range(4):
                    t, half = (b % 2, b // 2) if first else (b // 2, b % 2)
                    act.wait_ge(turned4, 4 * n + b + 1)
                    act.activation(dst_hi[:, 4 * half:4 * half + 4, t * P:(t + 1) * P],
                                   bank(first + b).rearrange("p (k t) -> p k t", k=4), ACT.Copy).then_inc(turn_hi, 1)

            def load_gains(g, b):
                act.dma_start(small[:, 0:D], g.partition_broadcast(P)).then_inc(gains_loaded, 16)
                act.dma_start(small[:, D:2 * D], b.partition_broadcast(P)).then_inc(gains_loaded, 16)

            def norm_std(n):
                act.activation(stat[:, 94:95], ident[:, 0:1], ACT.Sqrt)
                act.wait_ge(var_ready, n + 1)
                act.activation(stat[:, 16:32], stat[:, 0:16], ACT.Sqrt).then_inc(std_ready, 1)

            def ahead(i):
                split(0, i + AHEAD, width_at(i + AHEAD))

            def side(l, i, half):
                for piece in SIDE.get((i, half), []):
                    if piece[0] == "unit":
                        unit(l, piece[1], piece[2])
                    elif piece[0] == "prep":
                        prepare(l, piece[1])
                    elif piece[0] == "turn":
                        n = BRANCHES[piece[1]]
                        act.wait_ge(branch_turned, 4 * l + piece[1] + 1)
                        act.activation(brT_hi[:, 2 * n:2 * n + 2, :], bank(6).rearrange("p (k t) -> p k t", k=2),
                                       ACT.Copy).then_inc(branch_hi, 1)
                    elif piece[0] == "diff_var":
                        norm_std(VAR_PREP[l])
                    elif piece[0] == "prep_var":
                        norm_std(VAR_PREP[l] + 1)
                    elif piece[0] == "lambda":
                        act.wait_ge(lam_sum, l + 1)
                        act.activation(stat[:, 50:52], stat[:, 48:50], ACT.Exp).then_inc(lam_exp, 1)

            def project(l):
                base = mix_base(l)
                for s, (c0, n, feat) in enumerate(SLOTS):
                    for half in range(2):
                        ahead(base + 2 * s + half)
                        side(l, 2 * s + half, 0)
                        if half:
                            b0 = 2 * (s % 2)
                            act.wait_ge(chunk_used, base + 2 * s + 2)
                            if feat:
                                f = (c0 - C_FEAT) // P if c0 < C_DV else 12
                                scale = HD ** -0.5 if f < 6 else 32 ** -0.5 if f == 12 else 1.0
                                act.activation(featT[:, f:f + 2, :], bank(b0).rearrange("p (b t) -> p b t", b=2),
                                               ACT.Copy, scale=scale).then_inc(proj_used[0], 1)
                            else:
                                act.activation(token_dst(c0, n, 0), bank(b0)[:, 0:n], ACT.Copy).then_inc(proj_used[0], 1)
                        side(l, 2 * s + half, 1)

            def unit(l, part, i):
                us, base = PARTS[part], unit_base(l, part)
                if 2 <= i < len(us) + 2 and EVAC[us[i - 2][0]][0]:
                    j = i - 2
                    u, kind = base + j, us[j][0]
                    act.wait_ge(prob_turned, u + 1)
                    if j >= 2:
                        act.wait_ge(pv_done, u - 1)
                    n = 512 if kind == "dil" else S
                    act.activation(probT[:, j % 2, 0:n], bank(6)[:, 0:n], ACT.Copy).then_inc(turned_taken[0], 1)
                if i < len(us):
                    u, kind = base + i, us[i][0]
                    n = 3 * S if kind == "dil" else S
                    act.wait_ge(negmax, u + 1)
                    if part == LATE and i >= 3:
                        act.wait_ge(prob_turned, u - 2)
                    src = bank(4 + i % 2)[:, 0:n] if part == LATE else prob[:, i % 3, 0:n]
                    act.activation(prob[:, i % 3, 0:n], src, ACT.Exp, bias=stat[:, 32 + i % 2:33 + i % 2],
                                   scale=scale_of(kind), accum_out=stat[:, 36 + i % 4:37 + i % 4]).then_inc(exps, 1)

            def prepare(l, stage):
                if stage == 1:
                    for t in range(NT):
                        act.wait_ge(prep_pe, 11 * l + t + 1)
                        x = slice(t * P, (t + 1) * P)
                        act.activation(cT[:, 0, x], bank(4 + t)[:, 0:P], ACT.Copy)
                        act.activation(cT[0:64, 1, x], bank(4 + t)[0:64, P:2 * P], ACT.Copy)
                        act.activation(cT[:, 2, x], bank(4 + t)[:, 2 * P:3 * P], ACT.Copy).then_inc(prep_act, 1)
                if stage == 2:
                    for t in range(NT):
                        act.wait_ge(prep_pe, 11 * l + 2 + t + 1)
                        q = bank(4 + t)[:, 0:384].rearrange("p (h d) -> p h d", h=4)
                        kv = bank(6 + t).rearrange("p (h d) -> p h d", h=4)
                        act.activation(mq[:, t, :, 0:64], q[:, :, 0:64], ACT.Copy)
                        act.activation(mk[:, t, :, 0:64], kv[:, :, 0:64], ACT.Copy)
                        act.activation(mv[:, t, :, :], kv[:, :, 64:128], ACT.Copy).then_inc(prep_act, 1)
                if stage == 4:
                    for b in range(2):
                        act.wait_ge(prep_pe, 11 * l + 4 + b + 1)
                        act.activation(gT[0:64, 2 * b:2 * b + 2, :], bank(6 + b)[0:64].rearrange("p (h t) -> p h t", h=2),
                                       ACT.Copy).then_inc(prep_act, 1)
                if stage == 5:
                    for b in range(2):
                        act.wait_ge(prep_pe, 11 * l + 7 + b + 1)
                        act.activation(mqT[0:96, 2 * b:2 * b + 2, :], bank(5 + b)[0:96].rearrange("p (h t) -> p h t", h=2),
                                       ACT.Copy).then_inc(prep_act, 1)

            def gates(l):
                base = mix_base(l)
                for i in range(N_GATE):
                    ahead(base + N_PROJ + i)
                    side(l, N_PROJ + i, 0)
                    q, c = i // 5, (i % 5) // 2
                    if i % 5 in (1, 3):
                        for t in range(NT):
                            act.wait_ge(gate_biased, 16 * l + 4 * q + 2 * c + t + 1)
                            s = gate_sb[:, 2 * c + t, :]
                            act.activation(s, s, ACT.Sigmoid).then_inc(gate_open, 1)
                        if c == 1 and q + 1 < NBR:
                            load_bias(l, q + 1)
                    side(l, N_PROJ + i, 1)

            def load_bias(l, q):
                act.dma_start(gate_bias, a["b_gate"][l][BRANCHES[q]].partition_broadcast(P)).then_inc(bias_loaded, 16)

            def output(l):
                for q in range(N_OUT):
                    ahead(mix_base(l) + N_PROJ + N_GATE + q)

            def take_x(item, tile, banks, at_, ready, slots=P):
                for r in range(2):
                    act.wait_ge(at_, 2 * item + (r + 1))
                    act.activation(xT_hi[:, 4 * r:4 * r + 4, tile * P:tile * P + slots],
                                   bank(banks + r).rearrange("p (k s) -> p k s", k=4)[:, :, 0:slots], ACT.Copy).then_inc(ready, 1)

            def expert(pos, g, tiles, item=None, packed=False):
                one, moe = tiles == 1, item is not None
                if moe and one:
                    act.nop().then_inc(x2_hi_done, 2)
                if moe and not one:
                    take_x(item, 1, 6, gathered2, x2_hi_done, HALF if packed else P)
                    act.wait_ge(pick_turned, item + 1)
                    act.activation(pick_gT, bank(3).rearrange("p (i t) -> p i t", i=2), ACT.Copy).then_inc(pickT_ready, 1)
                for i, (m, j, half) in enumerate(ORDER):
                    if moe:
                        split(pos, i + AHEAD)
                    else:
                        ahead(pos + i)
                    if (m, half) == ("a", 1):
                        act.wait_ge(chunk_used, pos + (i + 1))
                        if j:
                            act.wait_ge(hid_made, g * NB + j)
                        for t in range(tiles):
                            if packed and t:
                                act.wait_ge(a_summed, item * NB + (j + 1))
                                last = act.activation(silu[0:HALF, t, :], silu[0:HALF, t, :], ACT.Silu)
                            else:
                                last = act.activation(silu[:, t, :], bank(j % 2 if one else t), ACT.Silu)
                        last.then_inc(silu_done, 1)
                    jt = take_after(i, one)
                    if jt is not None:
                        act.wait_ge(hid_turned, g * NB + (jt + 1))
                        for t in range(tiles):
                            n = HALF if packed and t else P
                            src = bank(7 if one else 2 + t).rearrange("p (k s) -> p k s", k=4)
                            last = act.activation(hidT_hi[jt % 2 if one else t][:, :, 0:n], src[:, :, 0:n], ACT.Copy)
                        last.then_inc(hidT_hi_done, 1)
                        if moe and one and jt == 1:
                            act.wait_ge(pick_turned, item + 1)
                            act.activation(pick_gT[:, 0, :], bank(6)[:, 0:S], ACT.Copy).then_inc(pickT_ready, 1)
                if moe:
                    act.wait_ge(chunk_used, pos + NX)
                    for t in range(tiles):
                        last = act.activation(y_exp[:, t, 0:512], bank(4 + 2 * t), ACT.Copy)
                    last.then_inc(y_free, 1)
                    take_x(item + 1, 0, 0, gathered, x_hi_done)

            def route():
                act.wait_ge(logits_done, 1)
                act.activation(logitT[0:2 * NE, :], bank(0)[0:2 * NE, 0:S], ACT.Copy).then_inc(logits_copied, 1)
                act.wait_ge(expo_in, 1)
                for t in range(NT):
                    act.activation(expo[:, t, :], logit[:, t, :], ACT.Exp, bias=stat[:, 40 + t:41 + t]).then_inc(expo_out, 1)

            def mixer(l):
                take_turned(3 * l, actT_hi)
                project(l)
                gates(l)
                take_turned(3 * l + 1, actT_hi, 4)
                load_gains(a["ln1_g"][l], a["ln1_b"][l])
                if l == DEPTH - 1:
                    act.wait_ge(router_loaded, 32)
                    act.activation(r_split[:, :, 0:NE], r_raw, ACT.Copy).then_inc(router_hi, 1)
                output(l)
                norm_std(VAR_PREP[l] + 2)
                take_turned(3 * l + 2, actT_hi)

            act.wait_ge(ident_loaded, 16)
            norm_std(0)
            for q in range(AHEAD):
                split(0, q)
            mixer(0)
            load_gains(a["ln2_g"][0], a["ln2_b"][0])
            expert(DENSE_BASE, 0, 2)
            norm_std(VAR_PREP[0] + 3)
            mixer(1)
            load_gains(a["ln2_g"][1], a["ln2_b"][1])
            route()
            phase()
            act.wait_ge(items_known, 1)
            items = act.value_load(n_items[0:1, 0:1], min_val=1, max_val=NE)
            take_x(0, 0, 0, gathered, x_hi_done)
            with act.Fori(0, items) as item:
                kind = act.value_load(item_kind[0:1, bass.ds(item, 1)], min_val=0, max_val=2)
                item_loads[0] = act.snap(item * (16 * NX // RAW))
                pos, g = act.snap(item * NX + MOE_BASE), act.snap(item + 1)
                with act.If(kind == 0):
                    expert(pos, g, 1, item)
                with act.Else():
                    with act.If(kind == 1):
                        expert(pos, g, 2, item, packed=True)
                    with act.Else():
                        expert(pos, g, 2, item)
            norm_std(VAR_PREP[1] + 3)
            past = act.snap(items * (16 * NX // RAW))
            for s in range(RAW):
                act.wait_ge(chunk_loaded[s], past + 16 * (LOADS[s] + 1 + (s < AHEAD)))
                act.activation(landed[:, s:s + 1], raw[:, s, 0:1], ACT.Copy)

        @block.vector
        def _(dve):
            phase = Phases(dve)
            step = Steps(dve, dve_step)

            def split(pos, i, width=CH):
                s, q = slot_at(pos + i) if isinstance(pos, int) else i % RAW, i % SPL
                dve.wait_ge(hi_done, pos + (i + 1))
                dve.tensor_tensor(w_lo[:, q, 0:width], raw[:, s, 0:width], w_hi[:, q, 0:width].bitcast(F32),
                                  ALU.subtract).then_inc(lo_done, 1)

            def ahead(i):
                split(0, i + AHEAD, width_at(i + AHEAD))

            def take_turned(n, dst_hi, dst_lo, first=0):
                for b in range(4):
                    t, half = (b % 2, b // 2) if first else (b // 2, b % 2)
                    x = (slice(None), slice(4 * half, 4 * half + 4), slice(t * P, (t + 1) * P))
                    dve.wait_ge(turn_hi, 4 * n + b + 1)
                    dve.tensor_tensor(dst_lo[x], bank(first + b).rearrange("p (k t) -> p k t", k=4),
                                      dst_hi[x].bitcast(F32), ALU.subtract).then_inc(turn_lo, 1)

            def std(n):
                dve.wait_ge(std_ready, n + 1)
                r, v = stat[:, 16:32], stat[:, 0:16]
                step(dve.reciprocal(r, r))
                step(dve.tensor_tensor(v, v, r, ALU.mult))
                step(dve.tensor_tensor(v, v, r, ALU.mult))
                step(dve.tensor_scalar(v, v, -0.5, 1.5, ALU.mult, ALU.add))
                step(dve.tensor_tensor(r, r, v, ALU.mult))

            def layernorm(n, gains_at, add=None, src=h):
                step(dve.memset(stat[:, 0:16], 1.0))
                for t in range(NT):
                    if add is not None:
                        add(t)
                    for c in range(2):
                        part = stat[:, 56 + 12 * t + 6 * c:62 + 12 * t + 6 * c]
                        last = dve.bn_stats(part, src[:, t, c * 512:(c + 1) * 512])
                    step(last)
                    step(dve.bn_aggr(stat[:, 80 + 2 * t:82 + 2 * t], stat[:, 56 + 12 * t:68 + 12 * t]))
                dve.tensor_scalar(stat[:, 0:2], stat[:, 81:84:2], LN_EPS, None, ALU.add).then_inc(var_ready, 1)
                std(n)
                if gains_at:
                    dve.wait_ge(gains_loaded, 32 * gains_at)
                else:
                    dve.wait_ge(start_loaded, 32)
                for t in range(NT):
                    step(dve.scalar_tensor_tensor(h[:, t, :], src[:, t, :], stat[:, 80 + 2 * t:81 + 2 * t], small[:, 0:D],
                                                  ALU.subtract, ALU.mult))
                    dve.scalar_tensor_tensor(h[:, t, :], h[:, t, :], stat[:, 16 + t:17 + t], small[:, D:2 * D],
                                             ALU.mult, ALU.add).then_inc(ln_tile, 1)

            def side(l, i, half):
                for piece in SIDE.get((i, half), []):
                    if piece[0] == "unit":
                        unit(l, piece[1], piece[2])
                    elif piece[0] == "prep":
                        prepare(l, piece[1])
                    elif piece[0] == "turn":
                        n = BRANCHES[piece[1]]
                        dve.wait_ge(branch_hi, 4 * l + piece[1] + 1)
                        dve.tensor_tensor(brT_lo[:, 2 * n:2 * n + 2, :], bank(6).rearrange("p (k t) -> p k t", k=2),
                                          brT_hi[:, 2 * n:2 * n + 2, :].bitcast(F32), ALU.subtract).then_inc(branch_lo, 1)
                    elif piece[0] == "diff_var":
                        diff_var(l)
                    elif piece[0] == "diff_norm":
                        diff_norm(l)
                    elif piece[0] == "prep_var":
                        prep_var(l)
                    elif piece[0] == "lambda":
                        diff_lambda(l)

            def project(l):
                base = mix_base(l)
                for s, (c0, n, feat) in enumerate(SLOTS):
                    for half in range(2):
                        side(l, 2 * s + half, 0)
                        ahead(base + 2 * s + half)
                        if half:
                            b1 = 2 * (s % 2) + 1
                            dve.wait_ge(chunk_used, base + 2 * s + 2)
                            if feat:
                                f = ((c0 - C_FEAT) // P if c0 < C_DV else 12) + 2
                                dve.tensor_scalar(featT[:, f:f + 2, :], bank(b1).rearrange("p (b t) -> p b t", b=2),
                                                  HD ** -0.5 if f < 6 else 1.0, None, ALU.mult).then_inc(proj_used[1], 1)
                            else:
                                dve.tensor_copy(token_dst(c0, n, 1), bank(b1)[:, 0:n]).then_inc(proj_used[1], 1)
                        side(l, 2 * s + half, 1)

            def diff_lambda(l):
                init = 0.8 - 0.6 * math.exp(-0.3 * l)
                dve.wait_ge(params_loaded, 16 * N_PARAM * (l + 1))
                lp = lamp[:, :, :].rearrange("p (m w) d -> p m w d", w=2)
                prod = gate_pr[:, 0, 0:64].rearrange("p (m d) -> p m d", m=2)
                step(dve.tensor_tensor(prod, lp[:, :, 0, :], lp[:, :, 1, :], ALU.mult))
                dve.tensor_reduce(stat[:, 48:50], prod, AX.X, ALU.add).then_inc(lam_sum, 1)
                dve.wait_ge(lam_exp, l + 1)
                step(dve.tensor_tensor(stat[:, 52:53], stat[:, 51:52], stat[:, 50:51], ALU.subtract))
                step(dve.tensor_scalar(stat[:, 52:53], stat[:, 52:53], -init, None, ALU.add))

            def unit(l, part, i):
                us, base = PARTS[part], unit_base(l, part)
                if i < len(us):
                    u = base + i
                    kind, hd, t, m = us[i]
                    nm = stat[:, 32 + i % 2:33 + i % 2]
                    dve.wait_ge(scores, u + 1)
                    if i >= 2:
                        dve.wait_ge(exps, u - 1)
                    if i >= 3:
                        dve.wait_ge(prob_turned, u - 2)
                    if part != LATE:
                        for g in range(3 if kind == "dil" else 1):
                            slope = 2.0 ** (-8.0 * (4 * g + hd + 1) / 12) if kind == "dil" else 2.0 ** (-8.0 * (hd + 1) / 4)
                            k = K_DIST + 384 * (g if kind == "dil" else 3) + P * (1 - t)
                            b = 4 + g // 2 if kind == "dil" else 4 + i % 2
                            last = dve.scalar_tensor_tensor(
                                prob[:, i % 3, g * S:(g + 1) * S], const[:, k:k + S], -slope,
                                bank(b)[:, (g % 2) * S:(g % 2 + 1) * S], ALU.mult, ALU.add)
                        step(last)
                        n = 3 * S if kind == "dil" else S
                        dve.tensor_reduce(nm, prob[:, i % 3, 0:n], AX.X, ALU.max, negate=True).then_inc(negmax, 1)
                    else:
                        step(dve.tensor_reduce(nm, bank(4 + i % 2)[:, 0:S], AX.X, ALU.max, negate=True))
                        dve.tensor_scalar(nm, nm, scale_of(kind), None, ALU.mult).then_inc(negmax, 1)
                if 2 <= i < len(us) + 2 and EVAC[us[i - 2][0]][1]:
                    j = i - 2
                    u, kind = base + j, us[j][0]
                    if j >= 2:
                        dve.wait_ge(pv_done, u - 1)
                    if kind == "dil":
                        dve.wait_ge(prob_turned, u + 1)
                        if j:
                            dve.wait_ge(pv_done, u)
                        dve.tensor_copy(probT[:, j % 2, 512:768], bank(7)[:, S:2 * S]).then_inc(turned_taken[1], 1)
                    else:
                        dve.wait_ge(prob_turned, u + 1)
                        dve.tensor_copy(probT[:, j % 2, 0:S], bank(6)[:, 0:S]).then_inc(turned_taken[1], 1)
                if i >= 3:
                    j = i - 3
                    u = base + j
                    kind, hd, t, m = us[j]
                    r = stat[:, 44:45]
                    c0 = {"mla": 0, "dil": 1, "gqa": 2, "diff": 3}[kind] * BW + hd * HD
                    dst, o = y[:, t, c0:c0 + HD], bank(7)[:, 0:HD]
                    step(dve.reciprocal(r, stat[:, 36 + j % 4:37 + j % 4]))
                    if m:
                        step(dve.tensor_tensor(r, r, stat[:, 52:53], ALU.mult))
                    dve.wait_ge(pv_done, u + 1)
                    if m:
                        step(dve.scalar_tensor_tensor(dst, o, r, dst, ALU.mult, ALU.add))
                    else:
                        step(dve.tensor_scalar(dst, o, r, None, ALU.mult))
                    dve.engine_nop().then_inc(out_taken, 1)

            def prep_var(l):
                for e in range(2):
                    dve.wait_ge(proj_used[e], (l + 1) * len(SLOTS))
                step(dve.memset(stat[:, 0:16], 1.0))
                step(dve.tensor_tensor(sq_c, cqkv[:, :, 0:QL + KVL], cqkv[:, :, 0:QL + KVL], ALU.mult))
                dve.tensor_reduce(stat[:, 0:2], sq_c[:, :, 0:QL], AX.X, ALU.add)
                dve.tensor_reduce(stat[:, 2:4], sq_c[:, :, QL:QL + KVL], AX.X, ALU.add)
                step(dve.tensor_tensor(gn, gqa[:, :, 0:384], gqa[:, :, 0:384], ALU.mult))
                step(dve.tensor_reduce(stat[:, 4:16], gn.rearrange("p t (h d) -> p (t h) d", d=HD), AX.X, ALU.add))
                dve.tensor_scalar(stat[:, 0:2], stat[:, 0:2], 1.0 / QL, RMS_EPS, ALU.mult, ALU.add)
                dve.tensor_scalar(stat[:, 2:4], stat[:, 2:4], 1.0 / KVL, RMS_EPS, ALU.mult, ALU.add)
                dve.tensor_scalar(stat[:, 4:16], stat[:, 4:16], 1.0 / HD, RMS_EPS, ALU.mult, ALU.add).then_inc(var_ready, 1)

            def prepare(l, stage):
                if stage == 0:
                    std(VAR_PREP[l] + 1)
                    for t in range(NT):
                        dve.scalar_tensor_tensor(cn[:, t, 0:QL], cqkv[:, t, 0:QL], stat[:, 16 + t:17 + t], g_q, ALU.mult, ALU.mult)
                        last = dve.scalar_tensor_tensor(cn[:, t, QL:QL + KVL], cqkv[:, t, QL:QL + KVL], stat[:, 18 + t:19 + t],
                                                        g_kv, ALU.mult, ALU.mult)
                    last.then_inc(prep_dve, 1)
                if stage in (1, 2):
                    for t in (stage - 1,):
                        x3 = gn[:, t, :].rearrange("p (h d) -> p h d", d=HD)
                        rs = stat[:, 20 + 6 * t:26 + 6 * t].unsqueeze(2).to_broadcast([P, 6, HD])
                        step(dve.tensor_tensor(x3, gqa[:, t, 0:384].rearrange("p (h d) -> p h d", d=HD), rs, ALU.mult))
                        step(dve.tensor_tensor(gn[:, t, :], gn[:, t, :], g_gqa, ALU.mult))
                        x5 = gn[:, t, :].rearrange("p (h a w d) -> p h a w d", h=6, a=2, w=2)
                        r5 = rope_a[:, t, :].rearrange("p (h a w d) -> p h a w d", h=6, a=2, w=2)
                        sin = const[:, K_GS + 64 * t:K_GS + 64 * t + 64].rearrange("p (a w d) -> p a w d", a=2, w=2)
                        cos = const[:, K_GC + 64 * t:K_GC + 64 * t + 64]
                        for w in range(2):
                            dve.tensor_tensor(r5[:, :, :, w, :], x5[:, :, :, 1 - w, :],
                                              sin[:, :, w, :].unsqueeze(1).to_broadcast([P, 6, 2, 16]), ALU.mult)
                        step(dve.tensor_tensor(gr[:, t, :].rearrange("p (h d) -> p h d", d=HD), x3,
                                               cos.unsqueeze(1).to_broadcast([P, 6, HD]), ALU.mult))
                        last = dve.tensor_tensor(gr[:, t, :], gr[:, t, :], rope_a[:, t, :], ALU.add)
                    if stage == 2:
                        last.then_inc(prep_dve, 1)
                if stage == 3:
                    for t in range(NT):
                        sin = const[:, K_MS + 32 * t:K_MS + 32 * t + 32].rearrange("p (w d) -> p w d", w=2)
                        cos = const[:, K_MC + 32 * t:K_MC + 32 * t + 32]
                        dve.wait_ge(prep_act, 8 * l + 2 + t + 1)
                        q = bank(4 + t)[:, 0:384].rearrange("p (h d) -> p h d", h=4)[:, :, 64:96]
                        q4 = q.rearrange("p h (w d) -> p h w d", w=2)
                        tq = rope_m[:, t, 0:P].rearrange("p (h w d) -> p h w d", h=4, w=2)
                        tc = rope_m[:, t, P:2 * P].rearrange("p (h d) -> p h d", h=4)
                        for w in range(2):
                            dve.tensor_tensor(tq[:, :, w, :], q4[:, :, 1 - w, :],
                                              sin[:, w, :].unsqueeze(1).to_broadcast([P, 4, 16]), ALU.mult)
                        step(dve.tensor_tensor(tc, q, cos.unsqueeze(1).to_broadcast([P, 4, 32]), ALU.mult))
                        step(dve.tensor_tensor(mq[:, t, :, 64:96], tc, rope_m[:, t, 0:P].rearrange("p (h d) -> p h d", h=4), ALU.add))
                        kr = cqkv[:, t, QL + KVL:QL + KVL + MR].rearrange("p (w d) -> p w d", w=2)
                        tk = rope_m[:, t, 0:32].rearrange("p (w d) -> p w d", w=2)
                        for w in range(2):
                            dve.tensor_tensor(tk[:, w, :], kr[:, 1 - w, :], sin[:, w, :], ALU.mult)
                        step(dve.tensor_tensor(rope_m[:, t, 32:64], cqkv[:, t, QL + KVL:QL + KVL + MR], cos, ALU.mult))
                        last = dve.tensor_tensor(mk[:, t, :, 64:96], rope_m[:, t, 0:32].unsqueeze(1).to_broadcast([P, 4, 32]),
                                                 rope_m[:, t, 32:64].unsqueeze(1).to_broadcast([P, 4, 32]), ALU.add)
                    last.then_inc(prep_dve, 1)
                if stage == 4:
                    dve.wait_ge(prep_pe, 11 * l + 7)
                    dve.tensor_copy(gT[0:64, 4:6, :], bank(4)[0:64].rearrange("p (h t) -> p h t", h=2)).then_inc(prep_dve, 1)
                if stage == 5:
                    for b in range(2):
                        dve.wait_ge(prep_pe, 11 * l + 9 + b + 1)
                        last = dve.tensor_copy(mkT[0:96, 2 * b:2 * b + 2, :], bank((7, 4)[b])[0:96].rearrange("p (h t) -> p h t", h=2))
                    last.then_inc(prep_dve, 1)

            def diff_var(l):
                sq = prob[:, 0, 0:512].rearrange("p (t n) -> p t n", t=NT)
                yd = y[:, :, 3 * BW:4 * BW]
                step(dve.memset(stat[:, 0:16], 1.0))
                step(dve.tensor_tensor(sq, yd, yd, ALU.mult))
                step(dve.tensor_reduce(stat[:, 0:8], sq.rearrange("p t (h d) -> p (t h) d", d=HD), AX.X, ALU.add))
                dve.tensor_scalar(stat[:, 0:8], stat[:, 0:8], 1.0 / HD, DIFF_EPS, ALU.mult, ALU.add).then_inc(var_ready, 1)

            def diff_norm(l):
                init = 0.8 - 0.6 * math.exp(-0.3 * l)
                std(VAR_PREP[l])
                for t in range(NT):
                    yt = y[:, t, 3 * BW:4 * BW].rearrange("p (h d) -> p h d", d=HD)
                    rs = stat[:, 16 + 4 * t:20 + 4 * t].unsqueeze(2).to_broadcast([P, 4, HD])
                    step(dve.tensor_tensor(yt, yt, rs, ALU.mult))
                    step(dve.tensor_tensor(yt, yt, g_sub.unsqueeze(1).to_broadcast([P, 4, HD]), ALU.mult))
                    last = dve.tensor_scalar(yt, yt, 1.0 - init, None, ALU.mult)
                last.then_inc(diff_normed, 1)

            def take_branch(l, q, c):
                for t in range(NT):
                    dst = mixed[:, t, c * 512:(c + 1) * 512]
                    if (c, t) == (1, 1):
                        dve.wait_ge(chunk_used, mix_base(l) + N_PROJ + 5 * q + 5)
                    else:
                        dve.wait_ge(branch_made, 3 * (NBR * l + q) + 2 * c + t + 1)
                    dve.wait_ge(gate_open, 16 * l + 4 * q + 2 * c + t + 1)
                    if q == 0:
                        dve.tensor_tensor(dst, gate_sb[:, 2 * c + t, :], bank(2 * c + t), ALU.mult).then_inc(branch_used, 1)
                    else:
                        pr = gate_pr[:, t, :]
                        step(dve.tensor_tensor(pr, gate_sb[:, 2 * c + t, :], bank(2 * c + t), ALU.mult))
                        dve.tensor_tensor(dst, dst, pr, ALU.add).then_inc(branch_used, 1)

            def gates(l):
                base = mix_base(l)
                for i in range(N_GATE):
                    if i % 5 == 4:
                        take_branch(l, i // 5, 0)
                    side(l, N_PROJ + i, 0)
                    if i < N_GATE - 1:
                        ahead(base + N_PROJ + i)
                    q, c = i // 5, (i % 5) // 2
                    if i % 5 in (1, 3):
                        dve.wait_ge(chunk_used, base + N_PROJ + i + 1)
                        dve.wait_ge(bias_loaded, 16 * (NBR * l + q + 1))
                        for t in range(NT):
                            dve.tensor_tensor(gate_sb[:, 2 * c + t, :], bank(2 * c + t),
                                              gate_bias[:, c * 512:(c + 1) * 512], ALU.add).then_inc(gate_biased, 1)
                    if i % 5 == 4:
                        take_branch(l, q, 1)
                    side(l, N_PROJ + i, 1)

            def output(l):
                for q in range(N_OUT - 1):
                    ahead(mix_base(l) + N_PROJ + N_GATE + q)
            def make_picks(item):
                for t in range(NT):
                    s_i = item_slot[:, t, bass.ds(item, 1)]
                    dve.tensor_scalar(pick[:, t, :], iota, s_i, None, ALU.is_equal)
                    last = dve.tensor_scalar(pick_g[:, t, :], iota, s_i, item_gate[:, t, bass.ds(item, 1)],
                                             ALU.is_equal, ALU.mult)
                last.then_inc(picked, 1)

            def take_x(item, tile, banks, at_, ready, packed=False):
                n, t0 = HALF if packed else P, tile * P
                for r in range(2):
                    k = slice(4 * r, 4 * r + 4)
                    lo = xT_hi[:, k, t0 + HALF:t0 + P] if packed else xT_lo[:, k, t0:t0 + P]
                    dve.wait_ge(at_, 2 * item + (r + 1))
                    dve.tensor_tensor(lo, bank(banks + r).rearrange("p (k s) -> p k s", k=4)[:, :, 0:n],
                                      xT_hi[:, k, t0:t0 + n].bitcast(F32), ALU.subtract).then_inc(ready, 1)

            def expert(pos, g, tiles, item=None, packed=False):
                one, moe = tiles == 1, item is not None
                if moe and one:
                    dve.engine_nop().then_inc(x2_lo_done, 2)
                if moe and packed:
                    for t in range(NT):
                        last = dve.tensor_copy(pick_g[:, t, P + HALF:2 * P], pick_g[:, t, P:P + HALF])
                    last.then_inc(pick_doubled, 1)
                elif moe:
                    dve.engine_nop().then_inc(pick_doubled, 1)
                    dve.engine_nop().then_inc(a_summed, NB)
                    dve.engine_nop().then_inc(halves_step, 3 * NB)
                if moe and not one:
                    take_x(item, 1, 6, x2_hi_done, x2_lo_done, packed)
                for i, (m, j, half) in enumerate(ORDER):
                    if moe:
                        split(pos, i + AHEAD)
                    elif i < NX - 1:
                        ahead(pos + i)
                    if packed and (m, half) == ("a", 1):
                        dve.wait_ge(chunk_used, pos + (i + 1))
                        part = silu[0:HALF, 1, :]
                        dve.tensor_copy(part, bank(1)[HALF:P, :]).then_inc(halves_step, 1)
                        dve.wait_ge(halves_step, item * (3 * NB) + (3 * j + 1))
                        dve.tensor_tensor(part, part, bank(1)[0:HALF, :], ALU.add).then_inc(a_summed, 1)
                    if (m, half) == ("b", 1):
                        dve.wait_ge(chunk_used, pos + (i + 1))
                        dve.wait_ge(silu_done, g * NB + (j + 1))
                        for t in range(tiles):
                            if packed and t:
                                part = hid[0:HALF, t, :]
                                dve.tensor_copy(part, bank(3)[HALF:P, :]).then_inc(halves_step, 1)
                                dve.wait_ge(halves_step, item * (3 * NB) + (3 * j + 2))
                                dve.tensor_tensor(part, part, bank(3)[0:HALF, :], ALU.add).then_inc(halves_step, 1)
                                dve.wait_ge(halves_step, item * (3 * NB) + (3 * j + 3))
                                last = dve.tensor_tensor(part, part, silu[0:HALF, t, :], ALU.mult)
                            else:
                                last = dve.tensor_tensor(hid[:, t, :], silu[:, t, :], bank(2 + (j % 2 if one else t)), ALU.mult)
                        last.then_inc(hid_made, 1)
                    jt = take_after(i, one)
                    if jt is not None:
                        dve.wait_ge(hidT_hi_done, g * NB + (jt + 1))
                        for t in range(tiles):
                            o = jt % 2 if one else t
                            n = HALF if packed and t else P
                            lo = hidT_hi[o][:, :, HALF:P] if packed and t else hidT_lo[o]
                            src = bank(7 if one else 2 + t).rearrange("p (k s) -> p k s", k=4)
                            last = dve.tensor_tensor(lo, src[:, :, 0:n], hidT_hi[o][:, :, 0:n].bitcast(F32), ALU.subtract)
                        last.then_inc(hidT_lo_done, 1)
                    if moe and (m, j, half) == ("w", 2, 1):
                        dve.wait_ge(pick_turned, item + 1)
                        make_picks(item + 1)
                if moe:
                    dve.wait_ge(chunk_used, pos + NX)
                    for t in range(tiles):
                        last = dve.tensor_copy(y_exp[:, t, 512:1024], bank(5 + 2 * t))
                    last.then_inc(y_free, 1)
                    take_x(item + 1, 0, 0, x_hi_done, x_lo_done)
                    for t in range(NT):
                        for c in range(2):
                            x = acc[:, t, c * 512:(c + 1) * 512]
                            dve.wait_ge(scattered, 4 * item + (2 * t + c + 1))
                            dve.tensor_tensor(x, x, bank(2 + 2 * t + c), ALU.add).then_inc(acc_added, 1)

            def route():
                for t in range(NT):
                    step(dve.tensor_scalar(acc[:, t, :], h[:, t, :], ALPHA, None, ALU.mult))
                dve.wait_ge(logits_turned, 1)
                parts = bank(1)[:, 0:4 * NE].rearrange("p (t w e) -> p t w e", t=NT, w=2)
                step(dve.tensor_copy(logit, parts[:, :, 0, :]))
                step(dve.tensor_tensor(logit, logit, parts[:, :, 1, :], ALU.add))
                step(dve.tensor_reduce(stat[:, 40:42], logit, AX.X, ALU.max, negate=True))
                dve.engine_nop().then_inc(expo_in, 1)
                all3 = [P, NT, NE, NE]
                this, other = logit.unsqueeze(3).to_broadcast(all3), logit.unsqueeze(2).to_broadcast(all3)
                tie = route_k[:, R_TIE:R_TIE + 64].unsqueeze(1).to_broadcast([P, NT, NE * NE])
                step(dve.tensor_tensor(cmp_a.rearrange("p t (e f) -> p t e f", e=NE), other, this, ALU.is_gt))
                step(dve.tensor_tensor(cmp_b.rearrange("p t (e f) -> p t e f", e=NE), other, this, ALU.is_equal))
                step(dve.tensor_tensor(cmp_b, cmp_b, tie, ALU.mult))
                step(dve.tensor_tensor(cmp_a, cmp_a, cmp_b, ALU.add))
                step(dve.tensor_reduce(rank, cmp_a.rearrange("p t (e f) -> p t e f", e=NE), AX.X, ALU.add))
                dve.tensor_scalar(sel, rank, float(TOP_K), None, ALU.is_lt).then_inc(sel_done, 1)
                dve.wait_ge(sel_done, 1)
                dve.wait_ge(expo_out, 2)
                step(dve.tensor_tensor(expo, expo, sel, ALU.mult))
                step(dve.tensor_reduce(stat[:, 42:44], expo, AX.X, ALU.add))
                step(dve.reciprocal(stat[:, 42:44], stat[:, 42:44]))
                step(dve.tensor_tensor(gate, expo, stat[:, 42:44].unsqueeze(2).to_broadcast([P, NT, NE]), ALU.mult))
                step(dve.tensor_scalar(slot, sel, -NOWHERE, NOWHERE, ALU.mult, ALU.add))
                dve.wait_ge(counted, 1)
                for t in range(NT):
                    step(dve.tensor_tensor(slot[:, t, :], slot[:, t, :], bank(2 + t)[:, 0:NE], ALU.add))
                step(dve.tensor_scalar(tiles_of[:, 0, :], bank(4)[:, 0:NE], 0.0, None, ALU.is_gt))
                step(dve.memset(tiles_of[:, 0, 0:1], 1.0))
                step(dve.tensor_scalar(tiles_of[:, 1, :], bank(4)[:, 0:NE], float(P), None, ALU.is_gt))
                step(dve.tensor_scalar(tiles_of[:, 2, :], bank(4)[:, 0:NE], float(P + HALF), None, ALU.is_gt))
                step(dve.tensor_tensor(tiles_of[:, 1, :], tiles_of[:, 1, :], tiles_of[:, 2, :], ALU.add))
                ef = cmp_b[:, 0, :].rearrange("p (e f) -> p e f", e=NE)
                before = route_k[:, R_TIE:R_TIE + 64].rearrange("p (e f) -> p e f", e=NE)
                step(dve.tensor_tensor(ef, tiles_of[:, 0, :].unsqueeze(1).to_broadcast([P, NE, NE]), before, ALU.mult))
                step(dve.tensor_reduce(ends, ef, AX.X, ALU.add))
                step(dve.tensor_tensor(ends, ends, tiles_of[:, 0, :], ALU.add))
                number = route_k[:, R_ITEM:R_ALL].rearrange("p (i e) -> p i e", e=NE)
                step(dve.tensor_tensor(item_tmp, ends.unsqueeze(1).to_broadcast([P, MAX_ITEMS, NE]), number, ALU.is_le))
                step(dve.tensor_reduce(item_e, item_tmp, AX.X, ALU.add))
                step(dve.tensor_tensor(item_hot, item_e.unsqueeze(2).to_broadcast([P, MAX_ITEMS, NE]),
                                       route_k[:, R_ITEM:R_ITEM + NE * NE:NE].unsqueeze(1).to_broadcast([P, MAX_ITEMS, NE]),
                                       ALU.is_equal))
                four = [P, 2 * NT, MAX_ITEMS, NE]
                step(dve.tensor_tensor(item_four, item_hot.unsqueeze(1).to_broadcast(four),
                                       slot_gate.unsqueeze(2).to_broadcast(four), ALU.mult))
                step(dve.tensor_reduce(item_sg, item_four, AX.X, ALU.add))
                step(dve.tensor_tensor(item_tmp, item_hot, tiles_of[:, 1, :].unsqueeze(1).to_broadcast([P, MAX_ITEMS, NE]),
                                       ALU.mult))
                step(dve.tensor_reduce(item_k, item_tmp, AX.X, ALU.add))
                step(dve.tensor_copy(item_kind[0:1, :], item_k[0:1, :]))
                step(dve.tensor_scalar(item_expert[0:1, :], item_e[0:1, :], float(NE - 1), None, ALU.min))
                dve.tensor_copy(n_items[0:1, 0:1], ends[0:1, NE - 1:NE]).then_inc(items_known, 1)

            def residual(t, made, used, banks):
                if t == 0:
                    dve.wait_ge(tile_made, made)
                else:
                    dve.wait_ge(chunk_used, used)
                for c in range(2):
                    w = slice(c * 512, (c + 1) * 512)
                    last = dve.scalar_tensor_tensor(h[:, t, w], h[:, t, w], ALPHA, bank(banks + 2 * t + c), ALU.mult, ALU.add)
                step(last)

            def mixer(l):
                take_turned(3 * l, actT_hi, actT_lo)
                if l:
                    ahead(mix_base(l) - 1)
                if l == 0:
                    split(0, 1)
                    dve.wait_ge(const_loaded, 16)
                project(l)
                gates(l)
                take_turned(3 * l + 1, actT_hi, actT_lo, 4)
                if l == DEPTH - 1:
                    dve.wait_ge(router_hi, 1)
                    dve.tensor_tensor(r_split[:, :, NE:2 * NE], r_raw, r_split[:, :, 0:NE].bitcast(F32),
                                      ALU.subtract).then_inc(router_lo, 1)
                ahead(mix_base(l) + N_PROJ + N_GATE - 1)
                output(l)
                layernorm(VAR_PREP[l] + 2, 2 * l + 1,
                          lambda t: residual(t, 2 * l + 1, mix_base(l) + N_MIX, 0))
                take_turned(3 * l + 2, actT_hi, actT_lo)
                ahead(mix_base(l) + N_MIX - 1)

            dve.engine_nop().then_inc(acc_added, 1)
            layernorm(0, 0, lambda t: dve.wait_ge(x_loaded[t], 16))
            split(0, 0)
            mixer(0)
            expert(DENSE_BASE, 0, 2)
            layernorm(VAR_PREP[0] + 3, 2, lambda t: residual(t, 2, DENSE_BASE + NX, 4))
            mixer(1)
            route()
            phase()
            items = dve.value_load(n_items[0:1, 0:1], min_val=1, max_val=NE)
            make_picks(0)
            take_x(0, 0, 0, x_hi_done, x_lo_done)
            with dve.Fori(0, items) as item:
                kind = dve.value_load(item_kind[0:1, bass.ds(item, 1)], min_val=0, max_val=2)
                pos, g = dve.snap(item * NX + MOE_BASE), dve.snap(item + 1)
                with dve.If(kind == 0):
                    expert(pos, g, 1, item)
                with dve.Else():
                    with dve.If(kind == 1):
                        expert(pos, g, 2, item, packed=True)
                    with dve.Else():
                        expert(pos, g, 2, item)
            step(dve.drain())
            layernorm(VAR_PREP[1] + 3, 4, src=acc)


N_PARAM = 13
VAR_PREP = [1, 5]

INS = ["x", "ln_emb_g", "ln_emb_b", "w_in", "b_gate", "mla_q_norm", "mla_kv_norm", "mla_w_uq", "mla_w_ukv",
       "gqa_q_norm", "gqa_k_norm", "diff_lambda", "diff_subln", "w_branch", "w_out", "ln1_g", "ln1_b",
       "ffn_w13", "ffn_w2", "moe_router", "moe_w13", "moe_w2", "ln2_g", "ln2_b"]


def kernel(**inputs):
    import numpy as _np
    import concourse.bacc as _bacc
    from concourse import mybir as _mybir
    from concourse.bass_utils import run_bass_kernel_spmd as _run

    nc = _bacc.Bacc("TRN2", target_bir_lowering=False, num_devices=1)
    arrays, args = {}, {}
    tables = {"consts": constants(), "router_consts": router_constants()}
    for name in INS + list(tables):
        v = tables[name] if name in tables else _np.ascontiguousarray(inputs[name])
        arrays[f"in_{name}"] = v
        args[name] = nc.dram_tensor(f"in_{name}", v.shape, _mybir.dt.from_np(v.dtype), kind="ExternalInput").ap()
    args["out"] = nc.dram_tensor("out_h", (1, S, D), _mybir.dt.from_np(_np.dtype("float32")), kind="ExternalOutput").ap()
    encoder(nc, args)
    r = _run(nc, [arrays], core_ids=[0])
    return r.results[0]["out_h"]
```
